# Optimizing a Trainium2 kernel written in Bass

```python
import jax, jax.numpy as jnp
from jax import lax
import numpy as np

D_MODEL = 1024
BATCH = 1
SEQ = 256
DEPTH = 1

CHUNK = 64
Q_BLOCK = 128
RMS_EPS = 1e-6
FOX_HEADS = 8
FOX_HEAD_DIM = 64
FOX_WIDTH = FOX_HEADS * FOX_HEAD_DIM
MLA_HEADS = 8
MLA_Q_LORA = 384
MLA_KV_LORA = 256
MLA_NOPE_DIM = 64
MLA_ROPE_DIM = 32
MLA_V_DIM = 64
MLA_WIDTH = MLA_HEADS * MLA_V_DIM
ROPE_BASE = 10000.0
MIX_WIDTH = FOX_WIDTH + MLA_WIDTH
IN_SIZES = (FOX_WIDTH, FOX_WIDTH, FOX_WIDTH, FOX_HEADS, MLA_Q_LORA, MLA_KV_LORA, MLA_ROPE_DIM)
IN_COLS = sum(IN_SIZES)
MEM_TOKENS = 256
MEM_HEADS = 4
MEM_HEAD_DIM = 128
MEM_WIDTH = MEM_HEADS * MEM_HEAD_DIM
N_EXPERTS = 32
TOP_K = 4
D_EXPERT = D_MODEL
SWIGLU_LIMIT = 7.0
SWIGLU_ALPHA = 1.702

kernel_name = 'hybrid_fox_mla_moe_stream_encoder'

def rmsnorm(x, g):
    xf = x.astype(jnp.float32)
    y = xf * lax.rsqrt(jnp.mean(xf * xf, axis=-1, keepdims=True) + RMS_EPS)
    return (y * g.astype(jnp.float32)).astype(x.dtype)

def rope_tables(seq_len):
    inv = 1.0 / (ROPE_BASE ** (jnp.arange(0, MLA_ROPE_DIM, 2, dtype=jnp.float32) / MLA_ROPE_DIM))
    ang = jnp.arange(seq_len, dtype=jnp.float32)[:, None] * inv[None, :]
    return jnp.cos(ang), jnp.sin(ang)

def apply_rope(x, cos, sin):
    half = x.shape[-1] // 2
    x1, x2 = x[..., :half], x[..., half:]
    cos = cos.astype(x.dtype)
    sin = sin.astype(x.dtype)
    return jnp.concatenate([x1 * cos - x2 * sin, x2 * cos + x1 * sin], axis=-1)

def to_heads(y, n_heads):
    b, s, _ = y.shape
    return y.reshape(b, s, n_heads, -1).transpose(0, 2, 1, 3)

def from_heads(y):
    b, h, s, d = y.shape
    return y.transpose(0, 2, 1, 3).reshape(b, s, h * d)

def frame_causal(t, s):
    return s <= t

def chunk_causal(t, s):
    return (s // CHUNK) <= (t // CHUNK)

def blocked_attention(q, k, v, mask_fn, decay=None):
    b, h, s_len, dk = q.shape
    dv = v.shape[-1]
    nb = s_len // Q_BLOCK
    scale = dk ** -0.5
    kpos = jnp.arange(s_len, dtype=jnp.int32)
    qb = q.reshape(b, h, nb, Q_BLOCK, dk).transpose(2, 0, 1, 3, 4)
    starts = jnp.arange(nb, dtype=jnp.int32) * Q_BLOCK
    if decay is None:
        xs = (qb, starts)
    else:
        xs = (qb, starts, decay.reshape(b, h, nb, Q_BLOCK).transpose(2, 0, 1, 3))

    def block(args):
        qi, start = args[0], args[1]
        tpos = start + jnp.arange(Q_BLOCK, dtype=jnp.int32)
        logits = jnp.einsum('bhqd,bhkd->bhqk', qi, k).astype(jnp.float32) * scale
        if decay is not None:
            logits = logits + (args[2][..., :, None] - decay[..., None, :])
        allowed = mask_fn(tpos[:, None], kpos[None, :])
        logits = jnp.where(allowed, logits, -jnp.inf)
        p = jax.nn.softmax(logits, axis=-1).astype(v.dtype)
        return jnp.einsum('bhqk,bhkd->bhqd', p, v)

    out = lax.map(block, xs)
    return out.transpose(1, 2, 0, 3, 4).reshape(b, h, s_len, dv)

def parallel_mixer(a, w_in, b_f, g_q_lat, w_uq, g_kv_lat, w_ukv, g_fox_out, g_mla_out, w_o, cos, sin):
    b, s_len, _ = a.shape
    points = np.cumsum(IN_SIZES)[:-1].tolist()
    proj = a @ w_in
    fq, fk, fv, f_logit, q_lat, kv_lat, k_rope = jnp.split(proj, points, axis=-1)

    log_f = jax.nn.log_sigmoid(f_logit.astype(jnp.float32) + b_f.astype(jnp.float32))
    decay = jnp.cumsum(log_f, axis=1).transpose(0, 2, 1)
    o_fox = blocked_attention(to_heads(fq, FOX_HEADS), to_heads(fk, FOX_HEADS),
                              to_heads(fv, FOX_HEADS), frame_causal, decay)
    o_fox = from_heads(o_fox)

    q = (rmsnorm(q_lat, g_q_lat) @ w_uq).reshape(b, s_len, MLA_HEADS, MLA_NOPE_DIM + MLA_ROPE_DIM)
    q_nope, q_pe = q[..., :MLA_NOPE_DIM], q[..., MLA_NOPE_DIM:]
    q_pe = apply_rope(q_pe, cos[:, None, :], sin[:, None, :])
    kv = (rmsnorm(kv_lat, g_kv_lat) @ w_ukv).reshape(b, s_len, MLA_HEADS, MLA_NOPE_DIM + MLA_V_DIM)
    k_nope, v = kv[..., :MLA_NOPE_DIM], kv[..., MLA_NOPE_DIM:]
    k_pe = apply_rope(k_rope, cos, sin)[:, :, None, :]
    k_pe = jnp.broadcast_to(k_pe, (b, s_len, MLA_HEADS, MLA_ROPE_DIM))
    q_full = jnp.concatenate([q_nope, q_pe], axis=-1).transpose(0, 2, 1, 3)
    k_full = jnp.concatenate([k_nope, k_pe], axis=-1).transpose(0, 2, 1, 3)
    o_mla = from_heads(blocked_attention(q_full, k_full, v.transpose(0, 2, 1, 3), chunk_causal))

    mixed = jnp.concatenate([rmsnorm(o_fox, g_fox_out), rmsnorm(o_mla, g_mla_out)], axis=-1)
    return mixed @ w_o

def memory_cross_attention(a, mem_n, w_q, w_kv, w_o):
    q = to_heads(a @ w_q, MEM_HEADS)
    kv = mem_n @ w_kv
    k = to_heads(kv[..., :MEM_WIDTH], MEM_HEADS)
    v = to_heads(kv[..., MEM_WIDTH:], MEM_HEADS)
    logits = jnp.einsum('bhqd,bhmd->bhqm', q, k).astype(jnp.float32) * (MEM_HEAD_DIM ** -0.5)
    p = jax.nn.softmax(logits, axis=-1).astype(v.dtype)
    o = jnp.einsum('bhqm,bhmd->bhqd', p, v)
    return from_heads(o) @ w_o

def moe_ffn(a, w_router, b_router, w_gate_up, b_gate_up, w_down, b_down):
    b, s_len, d = a.shape
    t = a.reshape(-1, d)
    logits = (t @ w_router + b_router).astype(jnp.float32)
    top_v, top_i = lax.top_k(logits, TOP_K)
    top_w = jax.nn.softmax(top_v, axis=-1)
    gates = jnp.sum(jax.nn.one_hot(top_i, N_EXPERTS, dtype=jnp.float32) * top_w[..., None], axis=1)
    gates = gates.astype(t.dtype)
    y = jnp.zeros_like(t)
    for e in range(N_EXPERTS):
        gu = t @ w_gate_up[e] + b_gate_up[e]
        gate = jnp.minimum(gu[:, :D_EXPERT], SWIGLU_LIMIT)
        up = jnp.clip(gu[:, D_EXPERT:], -SWIGLU_LIMIT, SWIGLU_LIMIT)
        act = gate * jax.nn.sigmoid(SWIGLU_ALPHA * gate) * (up + 1.0)
        y = y + gates[:, e:e + 1] * (act @ w_down[e] + b_down[e])
    return y.reshape(b, s_len, d)

def setup_inputs(seed: int = 0) -> dict:
    key = jax.random.key(seed)
    ks = jax.random.split(key, 26)
    L = DEPTH

    def normal(k, shape, scale):
        return jax.random.normal(k, shape, jnp.float32) * scale

    def gain(k, shape):
        return 1.0 + 0.02 * jax.random.normal(k, shape, jnp.float32)

    return {
        'x': normal(ks[0], (BATCH, SEQ, D_MODEL), 1.0),
        'mem': normal(ks[1], (BATCH, MEM_TOKENS, D_MODEL), 1.0),
        'g_mix': gain(ks[2], (L, D_MODEL)),
        'w_in': normal(ks[3], (L, D_MODEL, IN_COLS), D_MODEL ** -0.5),
        'b_f': jax.random.uniform(ks[4], (L, FOX_HEADS), jnp.float32, 1.0, 4.0),
        'g_q_lat': gain(ks[5], (L, MLA_Q_LORA)),
        'w_uq': normal(ks[6], (L, MLA_Q_LORA, MLA_HEADS * (MLA_NOPE_DIM + MLA_ROPE_DIM)), MLA_Q_LORA ** -0.5),
        'g_kv_lat': gain(ks[7], (L, MLA_KV_LORA)),
        'w_ukv': normal(ks[8], (L, MLA_KV_LORA, MLA_HEADS * (MLA_NOPE_DIM + MLA_V_DIM)), MLA_KV_LORA ** -0.5),
        'g_fox_out': gain(ks[9], (L, FOX_WIDTH)),
        'g_mla_out': gain(ks[10], (L, MLA_WIDTH)),
        'w_o': normal(ks[11], (L, MIX_WIDTH, D_MODEL), MIX_WIDTH ** -0.5),
        'g_mem_q': gain(ks[12], (L, D_MODEL)),
        'w_mem_q': normal(ks[13], (L, D_MODEL, MEM_WIDTH), D_MODEL ** -0.5),
        'g_mem_kv': gain(ks[14], (L, D_MODEL)),
        'w_mem_kv': normal(ks[15], (L, D_MODEL, 2 * MEM_WIDTH), D_MODEL ** -0.5),
        'w_mem_o': normal(ks[16], (L, MEM_WIDTH, D_MODEL), MEM_WIDTH ** -0.5),
        'g_ffn': gain(ks[17], (L, D_MODEL)),
        'w_router': normal(ks[18], (L, D_MODEL, N_EXPERTS), D_MODEL ** -0.5),
        'b_router': normal(ks[19], (L, N_EXPERTS), 0.01),
        'w_gate_up': normal(ks[20], (L, N_EXPERTS, D_MODEL, 2 * D_EXPERT), D_MODEL ** -0.5),
        'b_gate_up': normal(ks[21], (L, N_EXPERTS, 2 * D_EXPERT), 0.02),
        'w_down': normal(ks[22], (L, N_EXPERTS, D_EXPERT, D_MODEL), D_EXPERT ** -0.5),
        'b_down': normal(ks[23], (L, N_EXPERTS, D_MODEL), 0.02),
        'g_final': gain(ks[24], (D_MODEL,)),
    }

def reference(x, mem, g_mix, w_in, b_f, g_q_lat, w_uq, g_kv_lat, w_ukv, g_fox_out, g_mla_out, w_o,
              g_mem_q, w_mem_q, g_mem_kv, w_mem_kv, w_mem_o, g_ffn, w_router, b_router,
              w_gate_up, b_gate_up, w_down, b_down, g_final):
    cos, sin = rope_tables(x.shape[1])
    h = x
    for l in range(DEPTH):
        h = h + parallel_mixer(rmsnorm(h, g_mix[l]), w_in[l], b_f[l], g_q_lat[l], w_uq[l],
                               g_kv_lat[l], w_ukv[l], g_fox_out[l], g_mla_out[l], w_o[l], cos, sin)
        h = h + memory_cross_attention(rmsnorm(h, g_mem_q[l]), rmsnorm(mem, g_mem_kv[l]),
                                       w_mem_q[l], w_mem_kv[l], w_mem_o[l])
        h = h + moe_ffn(rmsnorm(h, g_ffn[l]), w_router[l], b_router[l], w_gate_up[l],
                        b_gate_up[l], w_down[l], b_down[l])
    return rmsnorm(h, g_final)


_drawn_inputs = setup_inputs


def setup_inputs(seed=0):
    import zlib

    import numpy as np

    out = dict(_drawn_inputs(seed))
    spreads = {}
    factors = {'g_mem_q': 6.537,
     'g_mem_kv': 4.009,
     'b_gate_up': 18.581,
     'b_down': 21.229,
     'g_final': 8.163,
     'g_ffn': 4.355,
     'b_router': 6.22}
    for name, (base, spread) in spreads.items():
        noise = np.random.default_rng([zlib.crc32(name.encode()), seed]).standard_normal(out[name].shape)
        drawn = base * np.exp(spread * noise) if base else spread * noise
        out[name] = __import__('jax').numpy.asarray(drawn.astype(out[name].dtype))
    for name, factor in factors.items():
        out[name] = (out[name] * factor).astype(out[name].dtype)
    return out
```

```python
from contextlib import ExitStack

import numpy as np

import concourse.bass as bass
from concourse import mybir

F32 = mybir.dt.float32
I32 = mybir.dt.int32
ALU = mybir.AluOpType
ACT = mybir.ActivationFunctionType
AX = mybir.AxisListType.X

P = 128
D = 1024
S = 256
TT = S // P
DC = D // P
EPS = 1e-6
HEADS = 8
DH = 64
ROPE = 32
HALF = ROPE // 2
DQ = DH + ROPE
QL, KL = 384, 256
REST = HEADS + QL + KL + ROPE
MEM_HEADS = 4
MD = 128
E = 32
TOPK = 4
SEATS = 64
LIMIT, ALPHA = 7.0, 1.702
MASKED = -1e30

C_ID, C_TRI, C_FOX, C_MLA, C_SEAT, C_COS, C_SIN = 0, 128, 640, 1024, 1408, 1536, 1568
C_AUG, C_DEL, C_ONE, C_LIM, C_END = 1600, 1604, 1608, 1609, 1612

GAINS = (("g_mix", 8), ("g_q_lat", 3), ("g_kv_lat", 2), ("g_fox_out", 4), ("g_mla_out", 4),
         ("g_mem_q", 8), ("g_mem_kv", 8), ("g_ffn", 8))
G_AT = {}
for _n, _c in GAINS:
    G_AT[_n] = sum(c for _, c in GAINS[:len(G_AT)])
G_ALL = sum(c for _, c in GAINS)


def constants():
    c = np.zeros((P, C_END), np.float32)
    tok = np.arange(S)
    c[:, C_ID:C_ID + P] = np.eye(P)
    tri = (tok[:, None] <= tok[None, :]).astype(np.float32)
    c[:, C_TRI:C_TRI + 2 * S] = tri.reshape(TT, P, S).transpose(1, 0, 2).reshape(P, TT * S)
    for at, ok in ((C_FOX, tok[None, :] <= tok[:, None]), (C_MLA, tok[None, :] // 64 <= tok[:, None] // 64)):
        m = np.where(ok, 0.0, MASKED).astype(np.float32)
        c[:, at:at + P] = m[:P, :P]
        c[:, at + P:at + P + S] = m[P:, :]
    c[:, C_SEAT:C_SEAT + P] = np.tile(np.arange(SEATS), P // SEATS)
    inv = (1.0 / (np.float32(10000.0) ** (np.arange(0, ROPE, 2, dtype=np.float32) / ROPE))).astype(np.float32)
    ang = tok.astype(np.float32)[:, None] * inv[None, :]
    for at, f in ((C_COS, np.cos), (C_SIN, np.sin)):
        c[:, at:at + TT * HALF] = f(ang).astype(np.float32).reshape(TT, P, HALF).transpose(1, 0, 2).reshape(P, -1)
    for base in (0, 64):
        lo, hi = slice(base, base + 8), slice(base + 32, base + 40)
        c[hi, C_AUG] = 8.0
        c[lo, C_AUG + 1] = -8.0
        c[lo, C_AUG + 2] = 1.0
        c[hi, C_AUG + 3] = 1.0
        for pair in range(HEADS // 2):
            h = 2 * pair + base // 64
            c[base + h, C_DEL + pair] = c[base + 32 + h, C_DEL + pair] = 1.0
    c[:, C_ONE] = 1.0
    c[:, C_LIM:C_LIM + 3] = (SEATS, 2 * SEATS, 3 * SEATS)
    return c


def fills():
    order = [("gT", 0)]

    def stage(name, n):
        order.extend((name, i) for i in range(n))

    stage("xT", 4)
    stage("rest", 4)
    stage("v", 2)
    stage("qk", 4)
    stage("latT", 3)
    stage("decay", 1)
    stage("uq", 4)
    stage("ukv", 4)
    stage("mqT", 4)
    stage("mkT", 4)
    stage("memT", 4)
    for i in range(2 * HEADS + 2):
        if i < 2 * HEADS:
            order.append(("S", i))
        if 1 <= i <= 2 * HEADS:
            order.append(("T", i - 1))
        if i >= 2:
            order.append(("PV", i - 2))
        if i in (2, 5, 8, 11):
            order.append(("memkv", (i - 2) // 3))
    stage("oss", 1)
    stage("wo", 8)
    stage("h1T", 4)
    stage("mq", 2)
    for i in range(MEM_HEADS + 2):
        if i < MEM_HEADS:
            order.append(("cS", i))
        if 1 <= i <= MEM_HEADS:
            order.append(("cT", i - 1))
        if i >= 2:
            order.append(("cPV", i - 2))
    stage("mo", 4)
    stage("h2T", 4)
    stage("router", 1)
    stage("rank", 1)
    stage("gatesT", 1)
    return order


ORDER = fills()
FILL = {key: n for n, key in enumerate(ORDER)}
BANKS = 8
Y0 = len(ORDER)
Y_BANK = [(Y0 + i) % BANKS for i in range(4)]
X_BANK, A_BANK, B_BANK, D_BANK = [(Y0 + 4 + i) % BANKS for i in range(4)]


def layer_kernel(nc, A, out):
    with ExitStack() as ctx:
        def sb(name, width, dt=F32):
            return ctx.enter_context(nc.sbuf_tensor(name, [P, width], dt))

        def sem(name):
            return ctx.enter_context(nc.semaphore(name))

        bank = [ctx.enter_context(nc.psum_tensor(f"bank{i}", [P, 512], F32)) for i in range(BANKS)]

        SLOT = 4096
        slots = sb("slots", 6 * SLOT)
        cst = sb("cst", C_END)
        gT = sb("gT", G_ALL)
        hres = sb("hres", TT * D)
        xn = sb("xn", TT * D)
        aT = sb("aT", DC * S)
        memo = sb("memo", TT * D)
        qkf = sb("qkf", 2 * 4 * S)
        vf = sb("vf", TT * 512)
        latr = sb("latr", TT * REST + 5 * S)
        qkt = sb("qkt", 2 * TT * HEADS * DQ)
        vm = sb("vm", TT * 512)
        work = sb("work", 2 * HEADS * S + 3 * 512 + 2 * 512)
        aug = sb("aug", 2 * S)
        wr = sb("wr", DC * E)
        brt = sb("brt", E)
        bf = sb("bf", HEADS)
        small = sb("small", 96)
        route = sb("route", 12 * TT * E)
        nit = sb("nit", 1, I32)

        def v3(t, a, at=0, n=None, rows=slice(None)):
            n = n or t.shape[1] - at
            return t[rows, at:at + n].rearrange("p (a b) -> p a b", a=a)

        h_v, xn_v = v3(hres, TT), v3(xn, TT)
        aT_v = v3(aT, DC)
        mem_v, oT_v = v3(memo, TT), v3(memo, 8)
        sq_v = v3(xn, 8)
        qfT, kfT = v3(qkf, 4, 0, 1024), v3(qkf, 4, 1024, 1024)
        bdown, gfin = qkf[:, 0:D], qkf[:, D:2 * D]
        vf_v, vm_v = v3(vf, TT), v3(vm, TT)
        lat = v3(latr, TT, 0, TT * REST)
        latT = v3(latr, 5, TT * REST, 5 * S)
        mq, moT = v3(latr, 4, 0, 1024), v3(latr, 4, 1024, 1024)
        qt, kt = v3(qkt, TT, 0, TT * 768), v3(qkt, TT, TT * 768, TT * 768)
        mk, mv = v3(qkt, 4, 0, 1024), v3(qkt, TT, 1024, 1024)
        qmT = work[0:DQ, 0:2048].rearrange("p (h s) -> p h s", h=HEADS)
        kmT = work[0:DQ, 2048:4096].rearrange("p (h s) -> p h s", h=HEADS)
        logit = v3(work, 3, 4096, 3 * 512)
        probT = v3(work, 2, 4096 + 3 * 512, 2 * 512)
        scratch = work
        rope_tmp = v3(work, 4, 0, 1024)
        ident = cst[:, C_ID:C_ID + P]
        tri = v3(cst, TT, C_TRI, TT * S)
        one = cst[:, C_ONE:C_ONE + 1]
        graw = logit[:, 0, 0:P]
        augL = slots[:, 5 * SLOT + 2048:5 * SLOT + 3072].rearrange("p (a s) -> p a s", a=4)
        aug_base, aug_right = aug[:, 0:S], aug[:, S:2 * S]
        logfpad = v3(slots, TT, 5 * SLOT + 3072, TT * P)
        fz = slots[:, 5 * SLOT + 3328:5 * SLOT + 3328 + 64].rearrange("p (k t h) -> p k t h", k=4, t=TT)

        def slot(c, a, n, at=0):
            return slots[:, c * SLOT + at:c * SLOT + at + n].rearrange("p (a b) -> p a b", a=a)

        w_qk = slot(0, DC, DC * 1024)
        w_v = slot(2, DC, DC * 512)
        w_rest = slot(3, DC, DC * REST)
        w_uq = slot(3, 3, 3 * 768, DC * REST)
        w_ukv = slot(5, 2, 2 * 1024)
        w_mkv = slot(0, DC, DC * 1024)
        w_mq = slot(2, DC, DC * 512)
        w_o = slot(3, 8, 8 * D)
        w_mo = slot(5, 4, 4 * D)
        w_gate = [slot(0, 4, 4 * D), slot(1, 4, 4 * D)]
        w_up = [slot(2, 4, 4 * D), slot(3, 4, 4 * D)]
        w_down = [slot(4, 4, 4 * D), slot(5, 4, 4 * D)]

        def st(i, n=2):
            return small[:, i:i + n]

        ssq, rms, rstd, x_rstd = st(0), st(2), st(4), st(6)
        o_ssq, o_rstd = st(8, 4), st(12, 4)
        mx, nmx, den, rden = [v3(small, 3, 16 + 6 * k, 6) for k in range(4)]
        topv = v3(small, TT, 40, 16)
        r_tmp = st(56, 4)
        cntmax, over, novr = small[0:1, 60:61], small[0:1, 62:65], small[0:1, 66:67]
        lat_ssq, lat_rstd = v3(small, 2, 68, 4), v3(small, 2, 72, 4)
        lat_rms = v3(small, 2, 76, 4)

        def rt(i):
            return v3(route, TT, i * TT * E, TT * E)

        lg, gt, eq, cs, sel, ex, gates, pos, keep = [rt(i) for i in range(9)]
        gatesT = aug[0:E, 0:S]

        oh = work[:, 0:256].rearrange("p (b t c) -> p b t c", b=2, t=TT)
        ohg = work[:, 256:768].rearrange("p (b t c) -> p b t c", b=2, t=TT)
        back = v3(work, 2, 768, 512)
        xg = work[:, 1280:2304].rearrange("p (b c s) -> p b c s", b=2, c=DC)
        zg, zu, sig, prod, act_rows = [work[:, 2304 + 512 * k:2816 + 512 * k] for k in range(5)]
        actT = work[:, 4864:5376].rearrange("p (j h s) -> p j h s", j=4, h=2)
        res = v3(work, 2, 5376, 1024)
        chosen = v3(aug, 2, S, 2 * SEATS)
        bgu = memo[0:E, :]

        filled = [sem(f"filled{i}") for i in range(BANKS)]
        drained = [sem(f"drained{i}") for i in range(BANKS)]
        names = ("x cst gains bias b_f b_r w_r w_rest w_uq w_ukv w_v w_qk mem w_mkv w_o w_mq w_mo "
                 "b_down b_gu g_final").split()
        loaded = {n: sem("loaded_" + n) for n in names}
        vec_chain = sem("vec_chain")
        act_chain = sem("act_chain")
        sumsq = {n: sem("sumsq_" + n) for n in "x mem lat h1 h2 h3".split()}
        meansq = {n: sem("meansq_" + n) for n in "x mem lat o h1 h2 h3".split()}
        rooted = {n: sem("rooted_" + n) for n in "x mem lat o h1 h2 h3".split()}
        inv_root = {n: sem("inv_root_" + n) for n in "x mem lat h1 h2".split()}
        normed = {n: sem("normed_" + n) for n in "x mem lat h1 h2".split()}
        residual3 = sem("residual3")
        residual1, residual2 = sem("residual1"), sem("residual2")
        f_in, f_exp = sem("f_in"), sem("f_exp")
        logf_ready, aug_ready = sem("logf_ready"), sem("aug_ready")
        rope_ready = sem("rope_ready")
        max_ready, exp_ready, prob_ready = sem("max_ready"), sem("exp_ready"), sem("prob_ready")
        cmax_ready, cexp_ready, cprob_ready = sem("cmax_ready"), sem("cexp_ready"), sem("cprob_ready")
        r_shift, r_exp, sel_ready, gates_ready = sem("r_shift"), sem("r_exp"), sem("sel_ready"), sem("gates_ready")
        rounds_ready = sem("rounds_ready")
        y_started = sem("y_started")
        slot_loaded = [sem(f"slot_loaded{c}") for c in range(6)]
        onehot_ready = sem("onehot_ready")
        gathered, xg_ready = sem("gathered"), sem("xg_ready")
        gate_used, gate_full = sem("gate_used"), sem("gate_full")
        up_used, up_full = sem("up_used"), sem("up_full")
        down_used = sem("down_used")
        gate_ready, sig_ready, act_ready = sem("gate_ready"), sem("sig_ready"), sem("act_ready")
        actT_full, actT_ready = sem("actT_full"), sem("actT_ready")
        back_full, back_ready = sem("back_full"), sem("back_ready")
        down_full, res_ready = sem("down_full"), sem("res_ready")
        moe_chain = sem("moe_chain")
        y_done = sem("y_done")
        out_ready, stored = sem("out_ready"), sem("stored")

        def wait_bank(pe, name, i=0):
            n = FILL[(name, i)]
            if n >= BANKS:
                pe.wait_ge(drained[n % BANKS], n // BANKS)
            return bank[n % BANKS]

        def wait_filled(eng, name, i=0):
            n = FILL[(name, i)]
            eng.wait_ge(filled[n % BANKS], n // BANKS + 1)
            return bank[n % BANKS]

        def wait_drained(eng, name, i=0):
            n = FILL[(name, i)]
            eng.wait_ge(drained[n % BANKS], n // BANKS + 1)

        def fill_sem(name, i=0):
            return filled[FILL[(name, i)] % BANKS]

        def drain_sem(name, i=0):
            return drained[FILL[(name, i)] % BANKS]

        def dram(name, pat, **kw):
            return A[name].rearrange(pat, **kw)

        block = ctx.enter_context(nc.Block())

        @block.sync
        def _(sp):
            def load(name, dst, src):
                sp.dma_start(dst, src).then_inc(loaded[name], 16)

            w_in = dram("w_in", "o (c p) n -> p (o c) n", p=P)
            load("x", h_v, dram("x", "b (t p) d -> p (b t) d", p=P))
            at = 0
            for name, n in GAINS:
                load("gains", graw[at:at + n, :], dram(name, "o (c q) -> (o c) q", q=P))
                at += n
            load("cst", cst[:, :], A["constants"])
            load("w_rest", w_rest, w_in[:, :, 1536:1536 + REST])
            load("b_f", bf[:, :], A["b_f"].partition_broadcast(P).rearrange("p o n -> p (o n)"))
            load("b_r", brt[:, :], A["b_router"].partition_broadcast(P).rearrange("p o n -> p (o n)"))
            load("w_v", w_v, w_in[:, :, 1024:1536])
            load("w_qk", w_qk, w_in[:, :, 0:1024])
            load("w_uq", w_uq, dram("w_uq", "o (c p) n -> p (o c) n", p=P))
            load("w_ukv", w_ukv, dram("w_ukv", "o (c p) n -> p (o c) n", p=P))
            load("mem", mem_v, dram("mem", "b (t p) d -> p (b t) d", p=P))
            load("w_r", v3(wr, DC), dram("w_router", "o (c p) n -> p (o c) n", p=P))
            wait_filled(sp, "qk", 3)
            load("w_mkv", w_mkv, dram("w_mem_kv", "o (c p) n -> p (o c) n", p=P))
            load("w_mq", w_mq, dram("w_mem_q", "o (c p) n -> p (o c) n", p=P))
            wait_filled(sp, "uq", 3)
            load("w_o", w_o, dram("w_o", "o (c p) n -> p (o c) n", p=P))
            wait_filled(sp, "S", HEADS - 1)
            load("w_mo", w_mo, dram("w_mem_o", "o (c p) n -> p (o c) n", p=P))
            load("g_final", gfin, A["g_final"].partition_broadcast(P))
            load("b_down", bdown[0:E, :], dram("b_down", "o e n -> (o e) n"))

            w_gu = dram("w_gate_up", "o e (c p) n -> p (o e) c n", p=P)
            w_dn = dram("w_down", "o e (c p) n -> p (o e) c n", p=P)

            def expert_piece(c, e):
                k = slice(4 * (c % 2), 4 * (c % 2) + 4)
                src = w_dn[:, bass.ds(e, 1), k, :] if c >= 4 else w_gu[:, bass.ds(e, 1), k, (c // 2) * D:(c // 2 + 1) * D]
                sp.dma_start((w_gate + w_up + w_down)[c], src.rearrange("p o c n -> p (o c) n")).then_inc(slot_loaded[c], 16)

            wait_filled(sp, "memkv", 3)
            expert_piece(0, 0)
            expert_piece(1, 0)
            wait_filled(sp, "wo", 7)
            load("b_gu", bgu, dram("b_gate_up", "o e n -> (o e) n"))
            expert_piece(3, 0)
            expert_piece(4, 0)
            wait_filled(sp, "mq", 1)
            expert_piece(2, 0)
            wait_filled(sp, "mo", 3)
            expert_piece(5, 0)
            sp.wait_ge(rounds_ready, 1)
            n_pairs = sp.value_load(nit[0:1, 0:1], min_val=E // 2, max_val=S // SEATS * E // 2)
            piece_used = [gate_used, gate_full, up_used, up_full, down_used, down_full]
            with sp.Fori(1, n_pairs * 2) as g:
                for c in range(6):
                    sp.wait_ge(piece_used[c], g)
                    sp.nop(nofuse=True)
                    expert_piece(c, g & (E - 1))
            for t in range(TT):
                sp.wait_ge(out_ready, t + 1)
                sp.dma_start(out.rearrange("b (t p) d -> p (b t) d", p=P)[:, t, :], xn_v[:, t, :]).then_inc(stored, 16)
            sp.wait_ge(stored, 16 * TT)

        @block.tensor
        def _(pe):
            def transposes(name, i, blocks):
                b = wait_bank(pe, name, i)
                for col, rows, src in blocks:
                    last = nc.tensor.transpose(b[0:rows, col:col + src.shape[0]], src, ident[0:src.shape[0], 0:src.shape[0]])
                last.then_inc(fill_sem(name, i), 1)

            def rows_to_T(name, src):
                for i in range(4):
                    transposes(name, i, [(256 * c + 128 * t, P, src[:, t, (2 * i + c) * P:(2 * i + c + 1) * P])
                                         for c in range(2) for t in range(TT)])

            def product(name, i, parts, b=None):
                for o, l, r, first, stop in parts:
                    mm = nc.tensor.matmul(o, l, r, start=first, stop=stop)
                mm.then_inc(fill_sem(name, i), 1)

            def contract(o, ls, rs):
                n = len(ls)
                return [(o, ls[k], rs[k], k == 0, k == n - 1) for k in range(n)]

            pe.wait_ge(loaded["cst"], 16)
            pe.wait_ge(loaded["gains"], 16 * len(GAINS))
            transposes("gT", 0, [(0, P, graw[0:G_ALL, :])])
            pe.wait_ge(normed["x"], TT)
            rows_to_T("xT", xn_v)
            for i in range(4):
                wait_drained(pe, "xT", i)
            pe.wait_ge(loaded["w_rest"], 16)
            for t in range(TT):
                for n in range(2):
                    b = wait_bank(pe, "rest", 2 * t + n)
                    product("rest", 2 * t + n, contract(b[:, 0:340], [aT_v[:, c, t * P:(t + 1) * P] for c in range(DC)],
                                                        [w_rest[:, c, n * 340:(n + 1) * 340] for c in range(DC)]))
            pe.wait_ge(loaded["w_v"], 16)
            for t in range(TT):
                b = wait_bank(pe, "v", t)
                product("v", t, contract(b[:, :], [aT_v[:, c, t * P:(t + 1) * P] for c in range(DC)],
                                         [w_v[:, c, :] for c in range(DC)]))
            pe.wait_ge(loaded["w_qk"], 16)
            for i in range(4):
                b = wait_bank(pe, "qk", i)
                parts = []
                for j in range(2):
                    f = 2 * i + j
                    parts += contract(b[:, j * S:(j + 1) * S], [w_qk[:, c, f * P:(f + 1) * P] for c in range(DC)],
                                      [aT_v[:, c, :] for c in range(DC)])
                product("qk", i, parts)
            pe.wait_ge(normed["lat"], 2 * TT)
            for i in range(3):
                transposes("latT", i, [(256 * j + 128 * t, P, lat[:, t, 8 + (2 * i + j) * P:8 + (2 * i + j + 1) * P])
                                       for j in range(2 if i < 2 else 1) for t in range(TT)])
            pe.wait_ge(logf_ready, 1)
            b = wait_bank(pe, "decay")
            product("decay", 0, contract(b[:, 0:S], [logfpad[:, t, :] for t in range(TT)], [tri[:, t, :] for t in range(TT)]))
            for i in range(3):
                wait_drained(pe, "latT", i)
            pe.wait_ge(loaded["w_uq"], 16)
            for t in range(TT):
                for n in range(2):
                    b = wait_bank(pe, "uq", 2 * t + n)
                    product("uq", 2 * t + n, contract(b[:, 0:384], [latT[:, c, t * P:(t + 1) * P] for c in range(3)],
                                                      [w_uq[:, c, n * 384:(n + 1) * 384] for c in range(3)]))
            pe.wait_ge(loaded["w_ukv"], 16)
            for t in range(TT):
                for n in range(2):
                    b = wait_bank(pe, "ukv", 2 * t + n)
                    product("ukv", 2 * t + n, contract(b[:, :], [latT[:, 3 + c, t * P:(t + 1) * P] for c in range(2)],
                                                       [w_ukv[:, c, n * 512:(n + 1) * 512] for c in range(2)]))
            pe.wait_ge(rope_ready, 1)
            for i in range(4):
                transposes("mqT", i, [(256 * j + 128 * t, DQ, qt[:, t, (2 * i + j) * DQ:(2 * i + j + 1) * DQ])
                                      for j in range(2) for t in range(TT)])
            pe.wait_ge(rope_ready, 2)
            for i in range(4):
                transposes("mkT", i, [(256 * j + 128 * t, DQ, kt[:, t, (2 * i + j) * DQ:(2 * i + j + 1) * DQ])
                                      for j in range(2) for t in range(TT)])
            pe.wait_ge(normed["mem"], TT)
            rows_to_T("memT", mem_v)

            def scores(i):
                b = wait_bank(pe, "S", i)
                parts = []
                for o, q0, n in ((0, 0, P), (P, P, S)):
                    if i < HEADS:
                        r = slice(64 * (i % 2), 64 * (i % 2) + 64)
                        a = slice(64 * (i % 2), 64 * (i % 2) + 40)
                        ls = [qfT[r, i // 2, q0:q0 + P], augL[a, i // 2, q0:q0 + P]]
                        rs = [kfT[r, i // 2, 0:n], aug_right[a, 0:n]]
                    else:
                        ls, rs = [qmT[:, i - HEADS, q0:q0 + P]], [kmT[:, i - HEADS, 0:n]]
                    parts += contract(b[:, o:o + n], ls, rs)
                product("S", i, parts)

            def head_out(i):
                wait_drained(pe, "T", i)
                b = wait_bank(pe, "PV", i)
                v = vf_v if i < HEADS else vm_v
                h, r = i % HEADS, slice(64 * (i % 2), 64 * (i % 2) + 64)
                product("PV", i, [(b[r, 0:S], v[:, 0, h * DH:(h + 1) * DH], probT[:, i % 2, 0:S], True, False),
                                  (b[r, P:S], v[:, 1, h * DH:(h + 1) * DH], probT[:, i % 2, S:S + P], False, True)])

            for i in range(4):
                wait_drained(pe, "qk", i)
            for t in range(TT):
                wait_drained(pe, "v", t)
            pe.wait_ge(aug_ready, 2)
            for i in range(2 * HEADS + 2):
                if i < 2 * HEADS:
                    if i == HEADS:
                        for j in range(4):
                            wait_drained(pe, "mqT", j)
                            wait_drained(pe, "mkT", j)
                            wait_drained(pe, "ukv", j)
                    scores(i)
                if 1 <= i <= 2 * HEADS:
                    j = i - 1
                    pe.wait_ge(prob_ready, j + 1)
                    transposes("T", j, [(P * k, P, logit[:, j % 3, P * k:P * (k + 1)]) for k in range(3)])
                if i >= 2:
                    head_out(i - 2)
                if i in (2, 5, 8, 11):
                    n = (i - 2) // 3
                    if n == 0:
                        pe.wait_ge(loaded["w_mkv"], 16)
                        for j in range(4):
                            wait_drained(pe, "memT", j)
                    b = wait_bank(pe, "memkv", n)
                    parts = []
                    if n < 2:
                        for j in range(2):
                            f = 2 * n + j
                            parts += contract(b[:, j * S:(j + 1) * S], [w_mkv[:, c, f * P:(f + 1) * P] for c in range(DC)],
                                              [aT_v[:, c, :] for c in range(DC)])
                    else:
                        t = n - 2
                        parts = contract(b[:, :], [aT_v[:, c, t * P:(t + 1) * P] for c in range(DC)],
                                         [w_mkv[:, c, 512:1024] for c in range(DC)])
                    product("memkv", n, parts)
            for i in range(2 * HEADS):
                wait_drained(pe, "PV", i)
            b = wait_bank(pe, "oss")
            parts = []
            for grp in range(2):
                for t in range(TT):
                    parts += contract(b[:, 2 * grp + t:2 * grp + t + 1],
                                      [sq_v[:, 4 * grp + c, t * P:(t + 1) * P] for c in range(4)], [one] * 4)
            product("oss", 0, parts)
            pe.wait_ge(loaded["w_o"], 16)
            for t in range(TT):
                for grp in range(2):
                    for n in range(2):
                        i = 4 * t + 2 * grp + n
                        b = wait_bank(pe, "wo", i)
                        product("wo", i, contract(b[:, :], [oT_v[:, 4 * grp + c, t * P:(t + 1) * P] for c in range(4)],
                                                  [w_o[:, 4 * grp + c, n * 512:(n + 1) * 512] for c in range(4)]))
            pe.wait_ge(normed["h1"], TT)
            rows_to_T("h1T", xn_v)
            for i in range(4):
                wait_drained(pe, "h1T", i)
            pe.wait_ge(loaded["w_mq"], 16)
            for i in range(2):
                b = wait_bank(pe, "mq", i)
                parts = []
                for j in range(2):
                    f = 2 * i + j
                    parts += contract(b[:, j * S:(j + 1) * S], [w_mq[:, c, f * P:(f + 1) * P] for c in range(DC)],
                                      [aT_v[:, c, :] for c in range(DC)])
                product("mq", i, parts)
            for i in range(2):
                wait_drained(pe, "mq", i)
            for i in range(4):
                wait_drained(pe, "memkv", i)
            for i in range(MEM_HEADS + 2):
                if i < MEM_HEADS:
                    b = wait_bank(pe, "cS", i)
                    product("cS", i, [(b[:, t * S:(t + 1) * S], mq[:, i, t * P:(t + 1) * P], mk[:, i, :], True, True)
                                      for t in range(TT)])
                if 1 <= i <= MEM_HEADS:
                    j = i - 1
                    pe.wait_ge(cprob_ready, j + 1)
                    transposes("cT", j, [(k * S + t * P, P, logit[:, j % 3, t * S + k * P:t * S + (k + 1) * P])
                                         for k in range(TT) for t in range(TT)])
                if i >= 2:
                    j = i - 2
                    wait_drained(pe, "cT", j)
                    b = wait_bank(pe, "cPV", j)
                    product("cPV", j, contract(b[:, 0:S], [mv[:, k, j * MD:(j + 1) * MD] for k in range(TT)],
                                               [probT[:, j % 2, k * S:(k + 1) * S] for k in range(TT)]))
            for i in range(MEM_HEADS):
                wait_drained(pe, "cPV", i)
            pe.wait_ge(loaded["w_mo"], 16)
            for t in range(TT):
                for n in range(2):
                    b = wait_bank(pe, "mo", 2 * t + n)
                    product("mo", 2 * t + n, contract(b[:, :], [moT[:, c, t * P:(t + 1) * P] for c in range(MEM_HEADS)],
                                                      [w_mo[:, c, n * 512:(n + 1) * 512] for c in range(MEM_HEADS)]))
            pe.wait_ge(normed["h2"], TT)
            rows_to_T("h2T", xn_v)
            for i in range(4):
                wait_drained(pe, "h2T", i)
            pe.wait_ge(loaded["w_r"], 16)
            b = wait_bank(pe, "router")
            parts = []
            for t in range(TT):
                parts += contract(b[:, t * E:(t + 1) * E], [aT_v[:, c, t * P:(t + 1) * P] for c in range(DC)],
                                  [wr[:, c * E:(c + 1) * E] for c in range(DC)])
            product("router", 0, parts)
            pe.wait_ge(sel_ready, 1)
            b = wait_bank(pe, "rank")
            product("rank", 0, contract(b[:, 0:E], [tri[:, 0, 0:P]], [sel[:, 0, :]])
                    + contract(b[:, E:2 * E], [tri[:, t, P:S] for t in range(TT)], [sel[:, t, :] for t in range(TT)])
                    + contract(b[0:1, 2 * E:3 * E], [one] * TT, [sel[:, t, :] for t in range(TT)]))
            pe.wait_ge(gates_ready, 1)
            transposes("gatesT", 0, [(t * P, E, gates[:, t, :]) for t in range(TT)])
            wait_drained(pe, "gatesT")
            pe.wait_ge(loaded["b_down"], 16)
            for i in range(4):
                pe.wait_ge(drained[Y_BANK[i]], (Y0 + i) // BANKS)
                t, n = i // 2, i % 2
                nc.tensor.matmul(bank[Y_BANK[i]][:, :], gatesT[:, t * P:(t + 1) * P], bdown[0:E, n * 512:(n + 1) * 512],
                                 start=True, stop=False, skip_group_check=True)
            for i in range(4, 8):
                pe.wait_ge(drained[(Y0 + i) % BANKS], (Y0 + i) // BANKS)

            def gather(p):
                for c in range(DC):
                    for t in range(TT):
                        mm = nc.tensor.matmul(bank[X_BANK][:, c * SEATS:(c + 1) * SEATS], xn_v[:, t, c * P:(c + 1) * P],
                                              oh[:, p, t, :], start=(t == 0), stop=(t == TT - 1))
                mm.then_inc(gathered, 1)

            def half_rows(b, lhsT, w, used, full, first=True):
                for c in range(DC):
                    for n in range(2):
                        mm = nc.tensor.matmul(b[64 * n:64 * n + 64, :], lhsT(c), w[c // 4][:, c % 4, n * 512:(n + 1) * 512],
                                              start=(first and c == 0), stop=(c == DC - 1), skip_group_check=True)
                    if c == DC // 2 - 1:
                        mm.then_inc(used, 1)
                mm.then_inc(full, 1)

            def gate_or_up(u, p, b, w, used, full):
                for n in range(2):
                    nc.tensor.matmul(b[64 * n:64 * n + 64, :], chosen[0:E, p, :], bgu[:, u * D + n * 512:u * D + (n + 1) * 512],
                                     start=True, stop=False, skip_group_check=True)
                half_rows(b, lambda c: xg[:, p, c, :], w, used, full, first=False)

            def scatter(p):
                for t in range(TT):
                    for n in range(2):
                        r = slice(64 * n, 64 * n + 64)
                        mm = nc.tensor.matmul(bank[Y_BANK[2 * t + n]][:, :], back[r, p, t * P:(t + 1) * P], res[r, p, :],
                                              start=False, stop=False, skip_group_check=True)
                return mm

            pe.wait_ge(onehot_ready, 1)
            gather(0)
            pe.wait_ge(rounds_ready, 1)
            n_pairs = pe.value_load(nit[0:1, 0:1], min_val=E // 2, max_val=S // SEATS * E // 2)
            pe.wait_ge(loaded["b_gu"], 16)
            bank_a, bank_b, bank_d = bank[A_BANK], bank[B_BANK], bank[D_BANK]
            with pe.Fori(0, n_pairs) as pair:
                for p in range(2):
                    g = 2 * pair + p
                    pe.wait_ge(xg_ready, g + 1)
                    pe.wait_ge(slot_loaded[0], 16 * g + 16)
                    pe.wait_ge(slot_loaded[1], 16 * g + 16)
                    gate_or_up(0, p, bank_a, w_gate, gate_used, gate_full)
                    pe.wait_ge(slot_loaded[2], 16 * g + 16)
                    pe.wait_ge(slot_loaded[3], 16 * g + 16)
                    gate_or_up(1, p, bank_b, w_up, up_used, up_full)
                    pe.wait_ge(onehot_ready, g + 2)
                    gather(1 - p)
                    pe.wait_ge(act_ready, g + 1)
                    for j in range(4):
                        mm = nc.tensor.transpose(bank_a[:, j * P:(j + 1) * P], act_rows[:, j * P:(j + 1) * P], ident)
                    mm.then_inc(actT_full, 1)
                    for t in range(TT):
                        mm = nc.tensor.transpose(bank_b[:, t * P:(t + 1) * P], ohg[:, p, t, :], ident)
                    mm.then_inc(back_full, 1)
                    pe.wait_ge(res_ready, g + 1)
                    scatter(1 - p)
                    pe.wait_ge(actT_ready, g + 1)
                    pe.wait_ge(back_ready, g + 1)
                    pe.wait_ge(slot_loaded[4], 16 * g + 16)
                    pe.wait_ge(slot_loaded[5], 16 * g + 16)
                    half_rows(bank_d, lambda c: actT[:, c % 4, c // 4, :], w_down, down_used, down_full)
            pe.wait_ge(res_ready, n_pairs * 2 + 1)
            scatter(1).then_inc(y_done, 1)

        @block.vector
        def _(dve):
            V = nc.vector
            steps = [0]

            def link(ins):
                steps[0] += 1
                ins.then_inc(vec_chain, 1)
                dve.wait_ge(vec_chain, steps[0])

            def inverse_rms(name, src, width, mean, inv, signal=None):
                V.tensor_scalar(mean, src, 1.0 / width, EPS, ALU.mult, ALU.add).then_inc(meansq[name], 1)
                dve.wait_ge(rooted[name], 1)
                link(V.reciprocal(inv, mean))

            def normalise(name, src, dst):
                dve.wait_ge(sumsq[name], TT)
                inverse_rms(name, ssq, D, rms, rstd)
                dve.sem_inc(inv_root[name], 1)
                V.tensor_scalar(dst[:, 0, :], src[:, 0, :], rstd[:, 0:1], None, ALU.mult).then_inc(normed[name], 1)

            def scaled_T(name, gain, i):
                b = wait_filled(dve, name, i)
                for j in range(2):
                    c = 2 * i + j
                    last = V.tensor_scalar(aT_v[:, c, :], b[:, j * S:(j + 1) * S], gT[:, gain + c:gain + c + 1], None, ALU.mult)
                last.then_inc(drain_sem(name, i), 1)

            normalise("x", h_v, xn_v)
            b = wait_filled(dve, "gT")
            V.tensor_copy(gT[:, :], b[:, 0:G_ALL]).then_inc(drain_sem("gT"), 1)
            wait_drained(dve, "gT")
            scaled_T("xT", G_AT["g_mix"], 0)
            scaled_T("xT", G_AT["g_mix"], 2)
            for t in range(TT):
                b = wait_filled(dve, "rest", 2 * t)
                V.tensor_copy(lat[:, t, 0:340], b[:, 0:340]).then_inc(drain_sem("rest", 2 * t), 1)
            dve.wait_ge(loaded["b_f"], 16)
            for t in range(TT):
                wait_drained(dve, "rest", 2 * t)
            link(V.memset(logfpad, 0.0))
            link(V.tensor_tensor(fz[:, 0], lat[:, :, 0:HEADS], bf[:, :].unsqueeze(1).to_broadcast([P, TT, HEADS]), ALU.add))
            link(V.tensor_scalar(fz[:, 1], fz[:, 0], -1.0, None, ALU.mult))
            V.tensor_tensor(fz[:, 1], fz[:, 1], fz[:, 0], ALU.min).then_inc(f_in, 1)
            link(V.tensor_scalar(fz[:, 3], fz[:, 0], 0.0, None, ALU.min))
            dve.wait_ge(f_exp, 1)
            link(V.tensor_tensor(fz[:, 0], fz[:, 3], fz[:, 2], ALU.subtract))
            for t in range(TT):
                last = V.tensor_copy(logfpad[:, t, :].rearrange("p (a b) -> p a b", a=4)[:, :, 0:HEADS],
                                     fz[:, 0, t, :].unsqueeze(1).to_broadcast([P, 4, HEADS]))
            last.then_inc(logf_ready, 1)
            for t in range(TT):
                wait_drained(dve, "rest", 2 * t + 1)
            dve.wait_ge(sumsq["lat"], 2 * TT)
            link(V.tensor_scalar(lat_rms[:, 0, :], lat_ssq[:, 0, :], 1.0 / QL, EPS, ALU.mult, ALU.add))
            V.tensor_scalar(lat_rms[:, 1, :], lat_ssq[:, 1, :], 1.0 / KL, EPS, ALU.mult, ALU.add).then_inc(meansq["lat"], 1)
            dve.wait_ge(rooted["lat"], 1)
            link(V.reciprocal(lat_rstd, lat_rms))
            for t in range(TT):
                for k, (at, n) in enumerate(((8, QL), (8 + QL, KL))):
                    V.tensor_scalar(lat[:, t, at:at + n], lat[:, t, at:at + n], lat_rstd[:, k, t:t + 1], None,
                                    ALU.mult).then_inc(normed["lat"], 1)
            for t in range(TT):
                b = wait_filled(dve, "v", t)
                V.tensor_copy(vf_v[:, t, :], b[:, :]).then_inc(drain_sem("v", t), 1)
            for i in range(2):
                b = wait_filled(dve, "qk", i)
                V.tensor_copy(qkf[:, i * 512:(i + 1) * 512], b[:, :]).then_inc(drain_sem("qk", i), 1)
            normalise("mem", mem_v, mem_v)
            for i in range(3):
                b = wait_filled(dve, "latT", i)
                for j in range(2 if i < 2 else 1):
                    c = 2 * i + j
                    g = G_AT["g_q_lat"] + c
                    last = V.tensor_scalar(latT[:, c, :], b[:, j * S:(j + 1) * S], gT[:, g:g + 1], None, ALU.mult)
                last.then_inc(drain_sem("latT", i), 1)
            b = wait_filled(dve, "decay")
            link(V.tensor_scalar(aug_base, b[:, 0:S], cst[:, C_AUG:C_AUG + 1], cst[:, C_AUG + 1:C_AUG + 2], ALU.mult, ALU.add))
            V.tensor_scalar(aug_right, b[:, 0:S], cst[:, C_AUG + 2:C_AUG + 3], cst[:, C_AUG + 3:C_AUG + 4], ALU.mult,
                            ALU.add).then_inc(drain_sem("decay"), 1)
            wait_drained(dve, "decay")
            dve.sem_inc(aug_ready, 1)
            for pair in range(4):
                last = V.tensor_scalar(augL[:, pair, :], aug_base, cst[:, C_DEL + pair:C_DEL + pair + 1], None, ALU.mult)
            last.then_inc(aug_ready, 1)

            def rotate(x1, x2, cos, sin, tmp):
                V.tensor_tensor(tmp(0), x1, cos, ALU.mult)
                V.tensor_tensor(tmp(1), x2, sin, ALU.mult)
                V.tensor_tensor(tmp(2), x2, cos, ALU.mult)
                link(V.tensor_tensor(tmp(3), x1, sin, ALU.mult))
                V.tensor_tensor(x1, tmp(0), tmp(1), ALU.subtract)
                return V.tensor_tensor(x2, tmp(2), tmp(3), ALU.add)

            cos = cst[:, C_COS:C_COS + TT * HALF].rearrange("p (t r) -> p t r", t=TT)
            sin = cst[:, C_SIN:C_SIN + TT * HALF].rearrange("p (t r) -> p t r", t=TT)
            kr = lat[:, :, 8 + QL + KL:]
            link(rotate(kr[:, :, 0:HALF], kr[:, :, HALF:], cos, sin,
                        lambda k: rope_tmp[:, k, 0:TT * HALF].rearrange("p (t r) -> p t r", t=TT)))
            qh = qt.rearrange("p t (h d) -> p t h d", h=HEADS)
            kh = kt.rearrange("p t (h d) -> p t h d", h=HEADS)
            for t in range(TT):
                for n in range(2):
                    b = wait_filled(dve, "ukv", 2 * t + n)
                    bv = b[:, :].rearrange("p (h d) -> p h d", h=4)
                    V.tensor_copy(kh[:, t, 4 * n:4 * n + 4, 0:DH], bv[:, :, 0:DH])
                    V.tensor_copy(vm_v[:, t, 256 * n:256 * (n + 1)].rearrange("p (h d) -> p h d", h=4),
                                  bv[:, :, DH:]).then_inc(drain_sem("ukv", 2 * t + n), 1)
            for i in range(4):
                wait_drained(dve, "uq", i)
            for t in range(TT):
                last = rotate(qh[:, t, :, DH:DH + HALF], qh[:, t, :, DH + HALF:],
                              cos[:, t, :].unsqueeze(1).to_broadcast([P, HEADS, HALF]),
                              sin[:, t, :].unsqueeze(1).to_broadcast([P, HEADS, HALF]),
                              lambda k: rope_tmp[:, k, 128 * t:128 * (t + 1)].rearrange("p (h r) -> p h r", h=HEADS))
            last.then_inc(rope_ready, 1)
            for t in range(TT):
                last = V.tensor_copy(kh[:, t, :, DH:], kr[:, t, :].unsqueeze(1).to_broadcast([P, HEADS, ROPE]))
            for i in range(4):
                wait_drained(dve, "ukv", i)
            last.then_inc(rope_ready, 1)
            for i in range(4):
                b = wait_filled(dve, "mkT", i)
                V.tensor_copy(kmT[:, 2 * i:2 * i + 2, :], b[0:DQ, :].rearrange("p (h s) -> p h s", h=2)).then_inc(drain_sem("mkT", i), 1)
            wait_filled(dve, "qk", 3)
            for i in (0, 2):
                scaled_T("memT", G_AT["g_mem_kv"], i)

            def head_max(i):
                b = wait_filled(dve, "S", i)
                if i >= 3:
                    wait_filled(dve, "T", i - 3)
                l = logit[:, i % 3, :]
                mask = C_FOX if i < HEADS else C_MLA
                V.scalar_tensor_tensor(out=l[:, 0:384], in0=b[:, 0:384], scalar=(DH if i < HEADS else DQ) ** -0.5,
                                       in1=cst[:, mask:mask + 384], op0=ALU.mult, op1=ALU.add).then_inc(drain_sem("S", i), 1)
                wait_drained(dve, "S", i)
                V.reduce_max(mx[:, i % 3, 0:1], l[:, 0:P], AX)
                link(V.reduce_max(mx[:, i % 3, 1:2], l[:, P:384], AX))
                V.tensor_scalar(nmx[:, i % 3, :], mx[:, i % 3, :], -1.0, None, ALU.mult).then_inc(max_ready, 1)

            def head_probs(i):
                dve.wait_ge(exp_ready, i + 1)
                l = logit[:, i % 3, :]
                link(V.reciprocal(rden[:, i % 3, :], den[:, i % 3, :]))
                V.tensor_scalar(l[:, 0:P], l[:, 0:P], rden[:, i % 3, 0:1], None, ALU.mult)
                V.tensor_scalar(l[:, P:384], l[:, P:384], rden[:, i % 3, 1:2], None, ALU.mult).then_inc(prob_ready, 1)

            for i in range(4):
                wait_filled(dve, "mqT", i)
            for i in range(2 * HEADS + 1):
                if i < 2 * HEADS:
                    head_max(i)
                if i >= 1:
                    head_probs(i - 1)
                if i in (3, 6, 9, 12):
                    n = (i - 3) // 3
                    b = wait_filled(dve, "memkv", n)
                    V.tensor_copy(qkt[:, n * 512:(n + 1) * 512], b[:, :]).then_inc(drain_sem("memkv", n), 1)
            b = wait_filled(dve, "oss")
            V.tensor_scalar(o_ssq, b[:, 0:4], 1.0 / 512, EPS, ALU.mult, ALU.add).then_inc(drain_sem("oss"), 1)
            wait_drained(dve, "oss")
            dve.sem_inc(meansq["o"], 1)
            dve.wait_ge(rooted["o"], 1)
            link(V.reciprocal(o_rstd, o_ssq))
            for t in range(TT):
                for grp in range(2):
                    for n in range(2):
                        i = 4 * t + 2 * grp + n
                        b = wait_filled(dve, "wo", i)
                        if grp == 1:
                            wait_drained(dve, "wo", i - 2)
                        hs = h_v[:, t, n * 512:(n + 1) * 512]
                        V.scalar_tensor_tensor(out=hs, in0=b[:, :], scalar=o_rstd[:, 2 * grp + t:2 * grp + t + 1], in1=hs,
                                               op0=ALU.mult, op1=ALU.add).then_inc(drain_sem("wo", i), 1)
            for i in (2, 3, 6, 7):
                wait_drained(dve, "wo", i)
            dve.sem_inc(residual1, 1)
            normalise("h1", h_v, xn_v)
            for i in (0, 2):
                scaled_T("h1T", G_AT["g_mem_q"], i)
            b = wait_filled(dve, "mq", 0)
            V.tensor_copy(latr[:, 0:512], b[:, :]).then_inc(drain_sem("mq", 0), 1)
            for i in range(MEM_HEADS + 1):
                if i < MEM_HEADS:
                    b = wait_filled(dve, "cS", i)
                    link(V.tensor_reduce(mx[:, i % 3, :], b[:, :].rearrange("p (t s) -> p t s", t=TT), AX, ALU.max))
                    V.tensor_scalar(nmx[:, i % 3, :], mx[:, i % 3, :], -(MD ** -0.5), None, ALU.mult).then_inc(cmax_ready, 1)
                if i >= 1:
                    j = i - 1
                    dve.wait_ge(cexp_ready, j + 1)
                    wait_drained(dve, "cS", j)
                    l = logit[:, j % 3, :]
                    link(V.reciprocal(rden[:, j % 3, :], den[:, j % 3, :]))
                    V.tensor_scalar(l[:, 0:S], l[:, 0:S], rden[:, j % 3, 0:1], None, ALU.mult)
                    V.tensor_scalar(l[:, S:2 * S], l[:, S:2 * S], rden[:, j % 3, 1:2], None, ALU.mult).then_inc(cprob_ready, 1)
            for i in range(4):
                t, n = i // 2, i % 2
                b = wait_filled(dve, "mo", i)
                hs = h_v[:, t, n * 512:(n + 1) * 512]
                V.tensor_tensor(hs, b[:, :], hs, ALU.add).then_inc(drain_sem("mo", i), 1)
            for i in range(4):
                wait_drained(dve, "mo", i)
            dve.sem_inc(residual2, 1)
            normalise("h2", h_v, xn_v)
            for i in (0, 2):
                scaled_T("h2T", G_AT["g_ffn"], i)
            b = wait_filled(dve, "router")
            dve.wait_ge(loaded["b_r"], 16)
            V.tensor_tensor(lg, b[:, 0:TT * E].rearrange("p (t e) -> p t e", t=TT),
                            brt[:, :].unsqueeze(1).to_broadcast([P, TT, E]), ALU.add).then_inc(drain_sem("router"), 1)
            wait_drained(dve, "router")
            for t in range(TT):
                last = V.max(topv[:, t, :], lg[:, t, :])
            link(last)
            for t in range(TT):
                V.tensor_scalar(ex[:, t, :], lg[:, t, :], topv[:, t, 0:1], None, ALU.subtract).then_inc(r_shift, 1)
                V.tensor_scalar(gt[:, t, :], lg[:, t, :], topv[:, t, TOPK - 1:TOPK], None, ALU.is_gt)
                last = V.tensor_scalar(eq[:, t, :], lg[:, t, :], topv[:, t, TOPK - 1:TOPK], None, ALU.is_equal)
            link(last)
            for t in range(TT):
                V.tensor_tensor_scan(cs[:, t, :], cst[:, C_ONE:C_ONE + 1].to_broadcast([P, E]), eq[:, t, :], 0.0, ALU.mult, ALU.add)
            link(V.reduce_sum(r_tmp[:, 0:2], gt, AX))
            link(V.tensor_scalar(r_tmp[:, 2:4], r_tmp[:, 0:2], -1.0, float(TOPK), ALU.mult, ALU.add))
            for t in range(TT):
                last = V.tensor_scalar(keep[:, t, :], cs[:, t, :], r_tmp[:, 2 + t:3 + t], None, ALU.is_le)
            link(last)
            link(V.tensor_tensor(keep, keep, eq, ALU.mult))
            V.tensor_tensor(sel, keep, gt, ALU.add).then_inc(sel_ready, 1)
            dve.wait_ge(sel_ready, 1)
            dve.wait_ge(r_exp, 1)
            link(V.tensor_tensor(ex, ex, sel, ALU.mult))
            link(V.reduce_sum(r_tmp[:, 0:2], ex, AX))
            link(V.reciprocal(r_tmp[:, 0:2], r_tmp[:, 0:2]))
            for t in range(TT):
                last = V.tensor_scalar(gates[:, t, :], ex[:, t, :], r_tmp[:, t:t + 1], None, ALU.mult)
            last.then_inc(gates_ready, 1)
            b = wait_filled(dve, "rank")
            link(V.tensor_tensor(pos, b[:, 0:TT * E].rearrange("p (t e) -> p t e", t=TT), sel, ALU.mult))
            link(V.tensor_scalar(pos, pos, -1.0, None, ALU.add))
            V.reduce_max(cntmax, b[0:1, 2 * E:3 * E], AX).then_inc(drain_sem("rank"), 1)
            wait_drained(dve, "rank")
            link(V.tensor_scalar(over, cst[0:1, C_LIM:C_LIM + 3], cntmax, None, ALU.is_lt))
            link(V.reduce_sum(novr, over, AX))
            V.tensor_scalar(nit[0:1, 0:1], novr, float(E // 2), float(E // 2), ALU.mult, ALU.add).then_inc(rounds_ready, 1)
            b = wait_filled(dve, "gatesT")
            V.tensor_copy(gatesT, b[0:E, 0:S]).then_inc(drain_sem("gatesT"), 1)
            dve.wait_ge(gates_ready, 1)

            V.memset(back[:, 1, :], 0.0)
            V.memset(res[:, 1, :], 0.0).then_inc(res_ready, 1)

            def select(e, p):
                for t in range(TT):
                    at = pos[:, t, bass.ds(e, 1)]
                    V.tensor_scalar(oh[:, p, t, :], cst[:, C_SEAT:C_SEAT + SEATS], at, None, ALU.is_equal)
                    last = V.tensor_scalar(ohg[:, p, t, :], cst[:, C_SEAT:C_SEAT + P], at, gates[:, t, bass.ds(e, 1)],
                                           ALU.is_equal, ALU.mult)
                last = V.tensor_copy(chosen[0:E, p, :], cst[0:E, bass.ds(e, 1)].to_broadcast([E, SEATS]))
                last.then_inc(onehot_ready, 1)

            def advance(e):
                return V.tensor_scalar(pos[:, :, bass.ds(e, 1)], pos[:, :, bass.ds(e, 1)], -float(SEATS), None, ALU.add)

            def take_rows(p):
                g0 = G_AT["g_ffn"]
                V.tensor_tensor(xg[:, p, :, :], bank[X_BANK][:, :].rearrange("p (c s) -> p c s", c=DC),
                                gT[:, g0:g0 + DC].unsqueeze(2).to_broadcast([P, DC, SEATS]), ALU.mult).then_inc(xg_ready, 1)

            select(0, 0)
            dve.wait_ge(onehot_ready, 1)
            link(advance(0))
            dve.wait_ge(gathered, 1)
            take_rows(0)
            dve.wait_ge(rounds_ready, 1)
            n_pairs = dve.value_load(nit[0:1, 0:1], min_val=E // 2, max_val=S // SEATS * E // 2)
            LINKS = 3
            with dve.Fori(0, n_pairs) as pair:
                for p in range(2):
                    g = 2 * pair + p
                    e_next = (g + 1) & (E - 1)
                    at = [LINKS * p]

                    def chain(ins):
                        at[0] += 1
                        ins.then_inc(moe_chain, 1)
                        dve.wait_ge(moe_chain, pair * (2 * LINKS) + at[0])

                    dve.wait_ge(gate_full, g + 1)
                    V.tensor_scalar(zg, bank[A_BANK][:, :], LIMIT, None, ALU.min).then_inc(gate_ready, 1)
                    select(e_next, 1 - p)
                    dve.wait_ge(onehot_ready, g + 2)
                    chain(advance(e_next))
                    dve.wait_ge(up_full, g + 1)
                    chain(V.tensor_scalar(zu, bank[B_BANK][:, :], LIMIT, -LIMIT, ALU.min, ALU.max))
                    chain(V.scalar_tensor_tensor(out=prod, in0=zu, scalar=1.0, in1=zg, op0=ALU.add, op1=ALU.mult))
                    dve.wait_ge(sig_ready, g + 1)
                    V.tensor_tensor(act_rows, prod, sig, ALU.mult).then_inc(act_ready, 1)
                    dve.wait_ge(gathered, g + 2)
                    take_rows(1 - p)
            dve.wait_ge(y_done, 1)
            for i in range(4):
                t, n = i // 2, i % 2
                hs = h_v[:, t, n * 512:(n + 1) * 512]
                last = V.tensor_tensor(hs, bank[Y_BANK[i]][:, :], hs, ALU.add)
            last.then_inc(residual3, 1)
            dve.wait_ge(sumsq["h3"], TT)
            dve.wait_ge(loaded["g_final"], 16)
            inverse_rms("h3", ssq, D, rms, rstd)
            for t in range(TT):
                V.scalar_tensor_tensor(out=xn_v[:, t, :], in0=h_v[:, t, :], scalar=rstd[:, t:t + 1], in1=gfin,
                                       op0=ALU.mult, op1=ALU.mult).then_inc(out_ready, 1)

        @block.scalar
        def _(act):
            A_ = nc.scalar.activation
            steps = [0]

            def link(ins):
                steps[0] += 1
                ins.then_inc(act_chain, 1)
                act.wait_ge(act_chain, steps[0])

            def squares(name, src, dst):
                for t in range(TT):
                    A_(dst[:, t, :], src[:, t, :], ACT.Square, accum_out=ssq[:, t:t + 1]).then_inc(sumsq[name], 1)

            def root(name, ap):
                act.wait_ge(meansq[name], 1)
                A_(ap, ap, ACT.Sqrt).then_inc(rooted[name], 1)

            def second_tile(name, src, dst):
                act.wait_ge(inv_root[name], 1)
                A_(dst[:, 1, :], src[:, 1, :], ACT.Copy, scale=rstd[:, 1:2]).then_inc(normed[name], 1)

            def scaled_T(name, gain, i):
                b = wait_filled(act, name, i)
                for j in range(2):
                    c = 2 * i + j
                    last = A_(aT_v[:, c, :], b[:, j * S:(j + 1) * S], ACT.Copy, scale=gT[:, gain + c:gain + c + 1])
                last.then_inc(drain_sem(name, i), 1)

            act.wait_ge(loaded["x"], 16)
            squares("x", h_v, xn_v)
            act.wait_ge(sumsq["x"], TT)
            root("x", rms)
            second_tile("x", h_v, xn_v)
            wait_drained(act, "gT")
            for i in (1, 3):
                scaled_T("xT", G_AT["g_mix"], i)
            for t in range(TT):
                b = wait_filled(act, "rest", 2 * t + 1)
                A_(lat[:, t, 340:680], b[:, 0:340], ACT.Copy).then_inc(drain_sem("rest", 2 * t + 1), 1)
            for i in range(4):
                wait_drained(act, "rest", i)
            for t in range(TT):
                for k, (at, n) in enumerate(((8, QL), (8 + QL, KL))):
                    A_(scratch[:, 1024 * k + 512 * t:1024 * k + 512 * t + n], lat[:, t, at:at + n], ACT.Square,
                       accum_out=lat_ssq[:, k, t:t + 1]).then_inc(sumsq["lat"], 1)
            act.wait_ge(f_in, 1)
            link(A_(fz[:, 2], fz[:, 1], ACT.Exp))
            A_(fz[:, 2], fz[:, 2], ACT.Ln, bias=1.0).then_inc(f_exp, 1)
            root("lat", lat_rms)
            act.wait_ge(loaded["mem"], 16)
            act.wait_ge(normed["x"], TT)
            act.wait_ge(sumsq["lat"], 2 * TT)
            squares("mem", mem_v, v3(work, TT, 0, TT * D))
            for i in (2, 3):
                b = wait_filled(act, "qk", i)
                A_(qkf[:, i * 512:(i + 1) * 512], b[:, :], ACT.Copy).then_inc(drain_sem("qk", i), 1)
            act.wait_ge(sumsq["mem"], TT)
            root("mem", rms)
            second_tile("mem", mem_v, mem_v)
            for i in range(4):
                t, n = i // 2, i % 2
                b = wait_filled(act, "uq", i)
                A_(qt[:, t, n * 384:(n + 1) * 384], b[:, 0:384], ACT.Copy).then_inc(drain_sem("uq", i), 1)
            for i in range(4):
                b = wait_filled(act, "mqT", i)
                A_(qmT[:, 2 * i:2 * i + 2, :], b[0:DQ, :].rearrange("p (h s) -> p h s", h=2), ACT.Copy).then_inc(drain_sem("mqT", i), 1)
            for i in (1, 3):
                scaled_T("memT", G_AT["g_mem_kv"], i)

            for i in range(2 * HEADS + 2):
                if i < 2 * HEADS:
                    act.wait_ge(max_ready, i + 1)
                    l = logit[:, i % 3, :]
                    for k, (a, n) in enumerate(((0, P), (P, S))):
                        last = A_(l[:, a:a + n], l[:, a:a + n], ACT.Exp, bias=nmx[:, i % 3, k:k + 1],
                                  accum_out=den[:, i % 3, k:k + 1])
                    last.then_inc(exp_ready, 1)
                if 1 <= i <= 2 * HEADS:
                    j = i - 1
                    b = wait_filled(act, "T", j)
                    if j >= 2:
                        wait_filled(act, "PV", j - 2)
                    A_(probT[:, j % 2, 0:384], b[:, 0:384], ACT.Copy).then_inc(drain_sem("T", j), 1)
                if i >= 2:
                    j = i - 2
                    b = wait_filled(act, "PV", j)
                    if j == 0:
                        wait_filled(act, "memT", 3)
                        act.wait_ge(normed["x"], TT)
                    r = slice(64 * (j % 2), 64 * (j % 2) + 64)
                    g = G_AT["g_fox_out"] + j // 2
                    A_(oT_v[r, j // 2, :], b[r, 0:S], ACT.Copy, scale=gT[r, g:g + 1])
                    A_(sq_v[r, j // 2, :], b[r, 0:S], ACT.Square).then_inc(drain_sem("PV", j), 1)
            root("o", o_ssq)
            act.wait_ge(residual1, 1)
            wait_filled(act, "oss")
            squares("h1", h_v, xn_v)
            act.wait_ge(sumsq["h1"], TT)
            root("h1", rms)
            second_tile("h1", h_v, xn_v)
            for i in (1, 3):
                scaled_T("h1T", G_AT["g_mem_q"], i)
            b = wait_filled(act, "mq", 1)
            A_(latr[:, 512:1024], b[:, :], ACT.Copy).then_inc(drain_sem("mq", 1), 1)
            for i in range(MEM_HEADS + 2):
                if i < MEM_HEADS:
                    act.wait_ge(cmax_ready, i + 1)
                    if i >= 3:
                        wait_filled(act, "cT", i - 3)
                    b = wait_filled(act, "cS", i)
                    for t in range(TT):
                        last = A_(logit[:, i % 3, t * S:(t + 1) * S], b[:, t * S:(t + 1) * S], ACT.Exp,
                                  bias=nmx[:, i % 3, t:t + 1], scale=MD ** -0.5, accum_out=den[:, i % 3, t:t + 1])
                    last.then_inc(drain_sem("cS", i), 1)
                    wait_drained(act, "cS", i)
                    act.sem_inc(cexp_ready, 1)
                if 1 <= i <= MEM_HEADS:
                    j = i - 1
                    b = wait_filled(act, "cT", j)
                    if j >= 2:
                        wait_filled(act, "cPV", j - 2)
                    A_(probT[:, j % 2, :], b[:, :], ACT.Copy).then_inc(drain_sem("cT", j), 1)
                if i >= 2:
                    j = i - 2
                    b = wait_filled(act, "cPV", j)
                    A_(moT[:, j, :], b[:, 0:S], ACT.Copy).then_inc(drain_sem("cPV", j), 1)
            act.wait_ge(residual2, 1)
            squares("h2", h_v, xn_v)
            act.wait_ge(sumsq["h2"], TT)
            root("h2", rms)
            second_tile("h2", h_v, xn_v)
            for i in (1, 3):
                scaled_T("h2T", G_AT["g_ffn"], i)
            act.wait_ge(r_shift, TT)
            A_(ex, ex, ACT.Exp).then_inc(r_exp, 1)
            act.wait_ge(rounds_ready, 1)
            n_pairs = act.value_load(nit[0:1, 0:1], min_val=E // 2, max_val=S // SEATS * E // 2)
            with act.Fori(0, n_pairs) as pair:
                for p in range(2):
                    g = 2 * pair + p
                    act.wait_ge(gate_ready, g + 1)
                    A_(sig, zg, ACT.Sigmoid, scale=ALPHA).then_inc(sig_ready, 1)
                    act.wait_ge(actT_full, g + 1)
                    A_(actT.rearrange("p j h s -> p (j h s)"), bank[A_BANK][:, :], ACT.Copy).then_inc(actT_ready, 1)
                    act.wait_ge(back_full, g + 1)
                    A_(back[:, p, :], bank[B_BANK][:, 0:S], ACT.Copy).then_inc(back_ready, 1)
                    act.wait_ge(down_full, g + 1)
                    A_(res[:, p, :], bank[D_BANK][:, :], ACT.Copy).then_inc(res_ready, 1)
            act.wait_ge(residual3, 1)
            squares("h3", h_v, xn_v)
            act.wait_ge(sumsq["h3"], TT)
            root("h3", rms)


def kernel(**inputs):
    import concourse.bacc as bacc
    from concourse.bass_utils import run_bass_kernel_spmd

    nc = bacc.Bacc("TRN2", target_bir_lowering=False, num_devices=1)
    arrays, access = {}, {}
    for name, a in dict(inputs, constants=constants()).items():
        a = np.ascontiguousarray(a)
        arrays[f"in_{name}"] = a
        access[name] = nc.dram_tensor(f"in_{name}", a.shape, mybir.dt.from_np(a.dtype), kind="ExternalInput").ap()
    out = nc.dram_tensor("out", (1, S, D), F32, kind="ExternalOutput").ap()
    layer_kernel(nc, access, out)
    r = run_bass_kernel_spmd(nc, [arrays], core_ids=[0])
    return r.results[0]["out"]
```

```python
from contextlib import ExitStack

import numpy as np

import concourse.bass as bass
from concourse import mybir

F32 = mybir.dt.float32
I32 = mybir.dt.int32
ALU = mybir.AluOpType
ACT = mybir.ActivationFunctionType
AX = mybir.AxisListType.X

P = 128
D = 1024
S = 256
TT = S // P
DC = D // P
EPS = 1e-6
HEADS = 8
DH = 64
ROPE = 32
HALF = ROPE // 2
DQ = DH + ROPE
QL, KL = 384, 256
REST = HEADS + QL + KL + ROPE
MEM_HEADS = 4
MD = 128
E = 32
TOPK = 4
SEATS = 64
LIMIT, ALPHA = 7.0, 1.702
MASKED = -1e30

C_ID, C_TRI, C_FOX, C_MLA, C_SEAT, C_COS, C_SIN = 0, 128, 640, 1024, 1408, 1536, 1568
C_AUG, C_DEL, C_ONE, C_LIM, C_END = 1600, 1604, 1608, 1609, 1612

GAINS = (("g_mix", 8), ("g_q_lat", 3), ("g_kv_lat", 2), ("g_fox_out", 4), ("g_mla_out", 4),
         ("g_mem_q", 8), ("g_mem_kv", 8), ("g_ffn", 8))
G_AT = {}
for _n, _c in GAINS:
    G_AT[_n] = sum(c for _, c in GAINS[:len(G_AT)])
G_ALL = sum(c for _, c in GAINS)


def constants():
    c = np.zeros((P, C_END), np.float32)
    tok = np.arange(S)
    c[:, C_ID:C_ID + P] = np.eye(P)
    tri = (tok[:, None] <= tok[None, :]).astype(np.float32)
    c[:, C_TRI:C_TRI + 2 * S] = tri.reshape(TT, P, S).transpose(1, 0, 2).reshape(P, TT * S)
    for at, ok in ((C_FOX, tok[None, :] <= tok[:, None]), (C_MLA, tok[None, :] // 64 <= tok[:, None] // 64)):
        m = np.where(ok, 0.0, MASKED).astype(np.float32)
        c[:, at:at + P] = m[:P, :P]
        c[:, at + P:at + P + S] = m[P:, :]
    c[:, C_SEAT:C_SEAT + P] = np.tile(np.arange(SEATS), P // SEATS)
    inv = (1.0 / (np.float32(10000.0) ** (np.arange(0, ROPE, 2, dtype=np.float32) / ROPE))).astype(np.float32)
    ang = tok.astype(np.float32)[:, None] * inv[None, :]
    for at, f in ((C_COS, np.cos), (C_SIN, np.sin)):
        c[:, at:at + TT * HALF] = f(ang).astype(np.float32).reshape(TT, P, HALF).transpose(1, 0, 2).reshape(P, -1)
    for base in (0, 64):
        lo, hi = slice(base, base + 8), slice(base + 32, base + 40)
        c[hi, C_AUG] = 8.0
        c[lo, C_AUG + 1] = -8.0
        c[lo, C_AUG + 2] = 1.0
        c[hi, C_AUG + 3] = 1.0
        for pair in range(HEADS // 2):
            h = 2 * pair + base // 64
            c[base + h, C_DEL + pair] = c[base + 32 + h, C_DEL + pair] = 1.0
    c[:, C_ONE] = 1.0
    c[:, C_LIM:C_LIM + 3] = (SEATS, 2 * SEATS, 3 * SEATS)
    return c


def fills():
    order = [("gT", 0)]

    def stage(name, n):
        order.extend((name, i) for i in range(n))

    stage("xT", 4)
    stage("rest", 4)
    stage("v", 2)
    stage("qk", 4)
    stage("latT", 3)
    stage("decay", 1)
    stage("uq", 4)
    stage("ukv", 4)
    stage("mqT", 4)
    stage("mkT", 4)
    stage("memT", 4)
    for i in range(2 * HEADS + 3):
        if i < 2 * HEADS:
            order.append(("S", i))
        if 2 <= i < 2 * HEADS + 2:
            order.append(("T", i - 2))
        if i >= 3:
            order.append(("PV", i - 3))
        if i in (2, 5, 8, 11):
            order.append(("memkv", (i - 2) // 3))
    stage("oss", 1)
    stage("wo", 8)
    stage("h1T", 4)
    stage("mq", 2)
    for i in range(MEM_HEADS + 3):
        if i < MEM_HEADS:
            order.append(("cS", i))
        if 2 <= i < MEM_HEADS + 2:
            order.append(("cT", i - 2))
        if i >= 3:
            order.append(("cPV", i - 3))
    stage("mo", 4)
    stage("h2T", 4)
    stage("router", 1)
    stage("rank", 1)
    return order


ORDER = fills()
FILL = {key: n for n, key in enumerate(ORDER)}
BANKS = 8
Y0 = len(ORDER)
Y_BANK = [(Y0 + i) % BANKS for i in range(4)]
X_BANK, A_BANK, B_BANK, D_BANK = [(Y0 + 4 + i) % BANKS for i in range(4)]


def layer_kernel(nc, A, out):
    with ExitStack() as ctx:
        def sb(name, width, dt=F32):
            return ctx.enter_context(nc.sbuf_tensor(name, [P, width], dt))

        def sem(name):
            return ctx.enter_context(nc.semaphore(name))

        bank = [ctx.enter_context(nc.psum_tensor(f"bank{i}", [P, 512], F32)) for i in range(BANKS)]

        SLOT = 4096
        slots = sb("slots", 6 * SLOT)
        cst = sb("cst", C_END)
        gT = sb("gT", G_ALL)
        hres = sb("hres", TT * D)
        xn = sb("xn", TT * D)
        late = sb("late", SLOT)
        aT = late[:, 0:DC * S]
        qkf = late[:, DC * S:2 * DC * S]
        memo = sb("memo", TT * D)
        mid = sb("mid", 2 * SLOT)
        vf = mid[:, 0:1024]
        vm = mid[:, 1024:2048]
        latr = mid[:, 2048:2048 + TT * REST + 5 * S]
        qkt = mid[:, 4736:4736 + 2 * TT * HEADS * DQ]
        work = sb("work", 2 * HEADS * S + 3 * 512 + 2 * 512)
        aug = sb("aug", 2 * S)
        wr = sb("wr", DC * E)
        brt = sb("brt", E)
        bf = sb("bf", HEADS)
        small = sb("small", 96)
        route = sb("route", 12 * TT * E)
        nit = sb("nit", 1, I32)

        def v3(t, a, at=0, n=None, rows=slice(None)):
            n = n or t.shape[1] - at
            return t[rows, at:at + n].rearrange("p (a b) -> p a b", a=a)

        h_v, xn_v = v3(hres, TT), v3(xn, TT)
        aT_v = v3(aT, DC)
        mem_v, oT_v = v3(memo, TT), v3(memo, 8)
        sq_v = v3(xn, 8)
        qfT, kfT = v3(qkf, 4, 0, 1024), v3(qkf, 4, 1024, 1024)
        gfin = slots[:, 0:D]
        vf_v, vm_v = v3(vf, TT), v3(vm, TT)
        lat = v3(latr, TT, 0, TT * REST)
        latT = v3(latr, 5, TT * REST, 5 * S)
        mq, moT = v3(latr, 4, 0, 1024), v3(latr, 4, 1024, 1024)
        qt, kt = v3(qkt, TT, 0, TT * 768), v3(qkt, TT, TT * 768, TT * 768)
        mk, mv = v3(qkt, 4, 0, 1024), v3(qkt, TT, 1024, 1024)
        qmT = work[0:DQ, 0:2048].rearrange("p (h s) -> p h s", h=HEADS)
        kmT = work[0:DQ, 2048:4096].rearrange("p (h s) -> p h s", h=HEADS)
        logit = v3(work, 3, 4096, 3 * 512)
        probT = v3(work, 2, 4096 + 3 * 512, 2 * 512)
        scratch = work
        rope_tmp = v3(work, 4, 0, 1024)
        ident = cst[:, C_ID:C_ID + P]
        tri = v3(cst, TT, C_TRI, TT * S)
        one = cst[:, C_ONE:C_ONE + 1]
        graw = logit[:, 0, 0:P]
        augL = slots[:, 5 * SLOT + 2048:5 * SLOT + 3072].rearrange("p (a s) -> p a s", a=4)
        aug_base, aug_right = aug[:, 0:S], aug[:, S:2 * S]
        logfpad = v3(slots, TT, 5 * SLOT + 3072, TT * P)
        fz = slots[:, 5 * SLOT + 3328:5 * SLOT + 3328 + 64].rearrange("p (k t h) -> p k t h", k=4, t=TT)

        def slot(c, a, n, at=0):
            return slots[:, c * SLOT + at:c * SLOT + at + n].rearrange("p (a b) -> p a b", a=a)

        w_qk = slot(0, DC, DC * 1024)
        w_v = slot(2, DC, DC * 512)
        w_rest = slot(3, DC, DC * REST)
        w_uq = slot(3, 3, 3 * 768, DC * REST)
        w_ukv = slot(5, 2, 2 * 1024)
        w_mkv = slot(0, DC, DC * 1024)
        w_mq = slot(2, DC, DC * 512)
        w_o = slot(3, 8, 8 * D)
        w_mo = slot(5, 4, 4 * D)
        w_gate = [[slot(0, 4, 4 * D), slot(1, 4, 4 * D)],
                  [v3(mid, 4, 0, 4 * D), v3(mid, 4, SLOT, 4 * D)]]
        w_up = [[slot(2, 4, 4 * D), slot(3, 4, 4 * D)], [v3(late, 4), slot(3, 4, 4 * D)]]
        w_down = [slot(4, 4, 4 * D), slot(5, 4, 4 * D)]

        def st(i, n=2):
            return small[:, i:i + n]

        ssq, rms, rstd, x_rstd = st(0), st(2), st(4), st(6)
        o_ssq, o_rstd = st(8, 4), st(12, 4)
        mx, nmx, den, rden = [v3(small, 3, 16 + 6 * k, 6) for k in range(4)]
        topv = v3(small, TT, 40, 16)
        r_tmp = st(56, 4)
        cntmax, over, novr = small[0:1, 60:61], small[0:1, 62:65], small[0:1, 66:67]
        lat_ssq, lat_rstd = v3(small, 2, 68, 4), v3(small, 2, 72, 4)
        lat_rms = v3(small, 2, 76, 4)

        q_scale, q_neg = st(80), st(82)

        def rt(i):
            return v3(route, TT, i * TT * E, TT * E)

        lg, gt, eq, cs, sel, ex, gates, pos, keep = [rt(i) for i in range(9)]
        gatesT = memo[0:E, 512:512 + S]

        oh = work[:, 0:256].rearrange("p (b t c) -> p b t c", b=2, t=TT)
        ohg = work[:, 256:768].rearrange("p (b t c) -> p b t c", b=2, t=TT)
        back = v3(work, 2, 768, 512)
        xg = work[:, 1280:2304].rearrange("p (b c s) -> p b c s", b=2, c=DC)
        zg, zu, sig, prod, act_rows = [work[:, 2304 + 512 * k:2816 + 512 * k] for k in range(5)]
        actT = work[:, 4864:5376].rearrange("p (j h s) -> p j h s", j=4, h=2)
        res = v3(work, 2, 5376, 1024)
        chosen = aug[:, :].rearrange("p (b q s) -> p b q s", b=2, q=4)
        bgu = memo[:, 0:512]
        bdown = work[0:E, 2304:2304 + D]

        filled = [sem(f"filled{i}") for i in range(BANKS)]
        drained = [sem(f"drained{i}") for i in range(BANKS)]
        names = ("x cst gains bias b_f b_r w_r w_rest w_uq w_ukv w_v w_qk mem w_mkv w_o w_mq w_mo "
                 "b_down b_gu g_final").split()
        loaded = {n: sem("loaded_" + n) for n in names}
        vec_chain = sem("vec_chain")
        act_chain = sem("act_chain")
        sumsq = {n: sem("sumsq_" + n) for n in "x mem lat h1 h2 h3".split()}
        meansq = {n: sem("meansq_" + n) for n in "x mem lat o h1 h2 h3".split()}
        rooted = {n: sem("rooted_" + n) for n in "x mem lat o h1 h2 h3".split()}
        inv_root = {n: sem("inv_root_" + n) for n in "x mem lat h1 h2".split()}
        normed = {n: sem("normed_" + n) for n in "x mem lat h1 h2".split()}
        residual3 = sem("residual3")
        f_in, f_exp = sem("f_in"), sem("f_exp")
        logf_ready, aug_ready = sem("logf_ready"), sem("aug_ready")
        rope_ready = sem("rope_ready")
        max_ready, exp_ready, prob_ready = sem("max_ready"), sem("exp_ready"), sem("prob_ready")
        cmax_ready, cexp_ready, cprob_ready = sem("cmax_ready"), sem("cexp_ready"), sem("cprob_ready")
        r_shift, r_exp, sel_ready, gates_ready = sem("r_shift"), sem("r_exp"), sem("sel_ready"), sem("gates_ready")
        rounds_ready = sem("rounds_ready")
        gatesT_full, gatesT_ready = sem("gatesT_full"), sem("gatesT_ready")
        gate_loaded = [[sem(f"gate_loaded{p}_{k}") for k in range(2)] for p in range(2)]
        up_loaded = [sem("up_loaded_even0"), sem("up_loaded_odd0")]
        up1_loaded = sem("up_loaded1")
        down_loaded = [sem(f"down_loaded{k}") for k in range(2)]
        onehot_ready = sem("onehot_ready")
        gathered, xg_ready = sem("gathered"), sem("xg_ready")
        gate_used, gate_full = sem("gate_used"), sem("gate_full")
        up_used, up_full = sem("up_used"), sem("up_full")
        down_used = sem("down_used")
        gate_ready, sig_ready, act_ready = sem("gate_ready"), sem("sig_ready"), sem("act_ready")
        actT_full, actT_ready = sem("actT_full"), sem("actT_ready")
        back_full, back_ready = sem("back_full"), sem("back_ready")
        down_full, res_ready = sem("down_full"), sem("res_ready")
        moe_chain = sem("moe_chain")
        y_done = sem("y_done")
        out_ready, stored = sem("out_ready"), sem("stored")

        def wait_bank(pe, name, i=0):
            n = FILL[(name, i)]
            if n >= BANKS:
                pe.wait_ge(drained[n % BANKS], n // BANKS)
            return bank[n % BANKS]

        def wait_filled(eng, name, i=0):
            n = FILL[(name, i)]
            eng.wait_ge(filled[n % BANKS], n // BANKS + 1)
            return bank[n % BANKS]

        def wait_drained(eng, name, i=0):
            n = FILL[(name, i)]
            eng.wait_ge(drained[n % BANKS], n // BANKS + 1)

        def fill_sem(name, i=0):
            return filled[FILL[(name, i)] % BANKS]

        def drain_sem(name, i=0):
            return drained[FILL[(name, i)] % BANKS]

        def dram(name, pat, **kw):
            return A[name].rearrange(pat, **kw)

        block = ctx.enter_context(nc.Block())

        @block.sync
        def _(sp):
            def load(name, dst, src):
                sp.dma_start(dst, src).then_inc(loaded[name], 16)

            w_in = dram("w_in", "o (c p) n -> p (o c) n", p=P)
            load("x", h_v, dram("x", "b (t p) d -> p (b t) d", p=P))
            at = 0
            for name, n in GAINS:
                load("gains", graw[at:at + n, :], dram(name, "o (c q) -> (o c) q", q=P))
                at += n
            load("cst", cst[:, :], A["constants"])
            load("w_rest", w_rest, w_in[:, :, 1536:1536 + REST])
            load("b_f", bf[:, :], A["b_f"].partition_broadcast(P).rearrange("p o n -> p (o n)"))
            load("b_r", brt[:, :], A["b_router"].partition_broadcast(P).rearrange("p o n -> p (o n)"))
            load("w_v", w_v, w_in[:, :, 1024:1536])
            load("w_qk", w_qk, w_in[:, :, 0:1024])
            load("w_uq", w_uq, dram("w_uq", "o (c p) n -> p (o c) n", p=P))
            load("w_ukv", w_ukv, dram("w_ukv", "o (c p) n -> p (o c) n", p=P))
            load("mem", mem_v, dram("mem", "b (t p) d -> p (b t) d", p=P))
            load("w_r", v3(wr, DC), dram("w_router", "o (c p) n -> p (o c) n", p=P))
            wait_filled(sp, "qk", 3)
            load("w_mkv", w_mkv, dram("w_mem_kv", "o (c p) n -> p (o c) n", p=P))
            load("w_mq", w_mq, dram("w_mem_q", "o (c p) n -> p (o c) n", p=P))
            wait_filled(sp, "uq", 3)
            load("w_o", w_o, dram("w_o", "o (c p) n -> p (o c) n", p=P))
            wait_filled(sp, "S", HEADS - 1)
            load("w_mo", w_mo, dram("w_mem_o", "o (c p) n -> p (o c) n", p=P))

            w_gu = dram("w_gate_up", "o e (c p) n -> p (o e) c n", p=P)
            w_dn = dram("w_down", "o e (c p) n -> p (o e) c n", p=P)

            def load_rows(dst, src, arrived):
                sp.dma_start(dst, src.rearrange("p o c n -> p (o c) n")).then_inc(arrived, 16)

            def rows(k):
                return slice(4 * k, 4 * k + 4)

            def load_gate(k, p, e):
                load_rows(w_gate[p][k], w_gu[:, bass.ds(e, 1), rows(k), 0:D], gate_loaded[p][k])

            def load_up(k, p, e):
                load_rows(w_up[p][k], w_gu[:, bass.ds(e, 1), rows(k), D:2 * D], (up_loaded[p], up1_loaded)[k])

            def load_down(k, e):
                load_rows(w_down[k], w_dn[:, bass.ds(e, 1), rows(k), :], down_loaded[k])

            wait_filled(sp, "memkv", 3)
            load_gate(0, 0, 0)
            load_gate(1, 0, 0)
            wait_filled(sp, "wo", 7)
            load("b_gu", bgu, dram("b_gate_up", "o e (q n) -> (o e q) n", q=4))
            load_up(1, 0, 0)
            load_down(0, 0)
            wait_filled(sp, "mq", 1)
            load_up(0, 0, 0)
            wait_filled(sp, "cPV", MEM_HEADS - 1)
            load("b_down", bdown, dram("b_down", "o e n -> (o e) n"))
            wait_filled(sp, "mo", 3)
            load_down(1, 0)
            load_gate(0, 1, 1)
            load_gate(1, 1, 1)
            wait_filled(sp, "router", 0)
            load_up(0, 1, 1)
            sp.wait_ge(rounds_ready, 1)
            more_pairs = sp.value_load(nit[0:1, 0:1], min_val=E // 2 - 1, max_val=S // SEATS * E // 2 - 1)

            def refill(used, count, load_piece, *where):
                sp.wait_ge(used, count)
                sp.nop(nofuse=True)
                load_piece(*where)

            def single_pieces(g, p, e):
                refill(up_full, g, load_up, 1, p, e)
                refill(down_used, g, load_down, 0, e)
                refill(down_full, g, load_down, 1, e)

            with sp.Fori(0, more_pairs) as pair:
                for p in range(2):
                    g = 2 * pair + p
                    single_pieces(g + 1, 1 - p, (g + 1) & (E - 1))
                    refill(gate_used, g + 1, load_gate, 0, p, (g + 2) & (E - 1))
                    refill(gate_full, g + 1, load_gate, 1, p, (g + 2) & (E - 1))
                    refill(up_used, g + 1, load_up, 0, p, (g + 2) & (E - 1))
            single_pieces(2 * more_pairs + 1, 1, E - 1)
            load("g_final", gfin, A["g_final"].partition_broadcast(P))
            for t in range(TT):
                sp.wait_ge(out_ready, t + 1)
                sp.dma_start(out.rearrange("b (t p) d -> p (b t) d", p=P)[:, t, :], xn_v[:, t, :]).then_inc(stored, 16)
            sp.wait_ge(stored, 16 * TT)

        @block.tensor
        def _(pe):
            def transposes(name, i, blocks):
                b = wait_bank(pe, name, i)
                for col, rows, src in blocks:
                    last = nc.tensor.transpose(b[0:rows, col:col + src.shape[0]], src, ident[0:src.shape[0], 0:src.shape[0]])
                last.then_inc(fill_sem(name, i), 1)

            def rows_to_T(name, src):
                for i in range(4):
                    transposes(name, i, [(256 * c + 128 * t, P, src[:, t, (2 * i + c) * P:(2 * i + c + 1) * P])
                                         for c in range(2) for t in range(TT)])

            def product(name, i, parts, b=None):
                for o, l, r, first, stop in parts:
                    mm = nc.tensor.matmul(o, l, r, start=first, stop=stop)
                mm.then_inc(fill_sem(name, i), 1)

            def contract(o, ls, rs):
                n = len(ls)
                return [(o, ls[k], rs[k], k == 0, k == n - 1) for k in range(n)]

            pe.wait_ge(loaded["cst"], 16)
            pe.wait_ge(loaded["gains"], 16 * len(GAINS))
            transposes("gT", 0, [(0, P, graw[0:G_ALL, :])])
            pe.wait_ge(normed["x"], TT)
            rows_to_T("xT", xn_v)
            for i in range(4):
                wait_drained(pe, "xT", i)
            pe.wait_ge(loaded["w_rest"], 16)
            for t in range(TT):
                for n in range(2):
                    b = wait_bank(pe, "rest", 2 * t + n)
                    product("rest", 2 * t + n, contract(b[:, 0:340], [aT_v[:, c, t * P:(t + 1) * P] for c in range(DC)],
                                                        [w_rest[:, c, n * 340:(n + 1) * 340] for c in range(DC)]))
            pe.wait_ge(loaded["w_v"], 16)
            for t in range(TT):
                b = wait_bank(pe, "v", t)
                product("v", t, contract(b[:, :], [aT_v[:, c, t * P:(t + 1) * P] for c in range(DC)],
                                         [w_v[:, c, :] for c in range(DC)]))
            pe.wait_ge(loaded["w_qk"], 16)
            for i in range(4):
                b = wait_bank(pe, "qk", i)
                parts = []
                for j in range(2):
                    f = 2 * i + j
                    parts += contract(b[:, j * S:(j + 1) * S], [w_qk[:, c, f * P:(f + 1) * P] for c in range(DC)],
                                      [aT_v[:, c, :] for c in range(DC)])
                product("qk", i, parts)
            pe.wait_ge(normed["lat"], 2 * TT)
            for i in range(3):
                transposes("latT", i, [(256 * j + 128 * t, P, lat[:, t, 8 + (2 * i + j) * P:8 + (2 * i + j + 1) * P])
                                       for j in range(2 if i < 2 else 1) for t in range(TT)])
            pe.wait_ge(logf_ready, 1)
            b = wait_bank(pe, "decay")
            product("decay", 0, contract(b[:, 0:S], [logfpad[:, t, :] for t in range(TT)], [tri[:, t, :] for t in range(TT)]))
            for i in range(3):
                wait_drained(pe, "latT", i)
            pe.wait_ge(loaded["w_uq"], 16)
            for t in range(TT):
                for n in range(2):
                    b = wait_bank(pe, "uq", 2 * t + n)
                    product("uq", 2 * t + n, contract(b[:, 0:384], [latT[:, c, t * P:(t + 1) * P] for c in range(3)],
                                                      [w_uq[:, c, n * 384:(n + 1) * 384] for c in range(3)]))
            pe.wait_ge(loaded["w_ukv"], 16)
            for t in range(TT):
                for n in range(2):
                    b = wait_bank(pe, "ukv", 2 * t + n)
                    product("ukv", 2 * t + n, contract(b[:, :], [latT[:, 3 + c, t * P:(t + 1) * P] for c in range(2)],
                                                       [w_ukv[:, c, n * 512:(n + 1) * 512] for c in range(2)]))
            pe.wait_ge(rope_ready, 1)
            for i in range(4):
                transposes("mqT", i, [(256 * j + 128 * t, DQ, qt[:, t, (2 * i + j) * DQ:(2 * i + j + 1) * DQ])
                                      for j in range(2) for t in range(TT)])
            pe.wait_ge(rope_ready, 2)
            for i in range(4):
                transposes("mkT", i, [(256 * j + 128 * t, DQ, kt[:, t, (2 * i + j) * DQ:(2 * i + j + 1) * DQ])
                                      for j in range(2) for t in range(TT)])
            pe.wait_ge(normed["mem"], TT)
            rows_to_T("memT", mem_v)

            def scores(i):
                b = wait_bank(pe, "S", i)
                parts = []
                for o, q0, n in ((0, 0, P), (P, P, S)):
                    if i < HEADS:
                        r = slice(64 * (i % 2), 64 * (i % 2) + 64)
                        a = slice(64 * (i % 2), 64 * (i % 2) + 40)
                        ls = [qfT[r, i // 2, q0:q0 + P], augL[a, i // 2, q0:q0 + P]]
                        rs = [kfT[r, i // 2, 0:n], aug_right[a, 0:n]]
                    else:
                        ls, rs = [qmT[:, i - HEADS, q0:q0 + P]], [kmT[:, i - HEADS, 0:n]]
                    parts += contract(b[:, o:o + n], ls, rs)
                product("S", i, parts)

            def head_out(i):
                wait_drained(pe, "T", i)
                b = wait_bank(pe, "PV", i)
                v = vf_v if i < HEADS else vm_v
                h, r = i % HEADS, slice(64 * (i % 2), 64 * (i % 2) + 64)
                product("PV", i, [(b[r, 0:S], v[:, 0, h * DH:(h + 1) * DH], probT[:, i % 2, 0:S], True, False),
                                  (b[r, P:S], v[:, 1, h * DH:(h + 1) * DH], probT[:, i % 2, S:S + P], False, True)])

            for i in range(4):
                wait_drained(pe, "qk", i)
            for t in range(TT):
                wait_drained(pe, "v", t)
            pe.wait_ge(aug_ready, 2)
            for i in range(2 * HEADS + 3):
                if i < 2 * HEADS:
                    if i == HEADS:
                        for j in range(4):
                            wait_drained(pe, "mqT", j)
                            wait_drained(pe, "mkT", j)
                            wait_drained(pe, "ukv", j)
                    scores(i)
                if 2 <= i < 2 * HEADS + 2:
                    j = i - 2
                    pe.wait_ge(prob_ready, j + 1)
                    transposes("T", j, [(P * k, P, logit[:, j % 3, P * k:P * (k + 1)]) for k in range(3)])
                if i >= 3:
                    head_out(i - 3)
                if i in (2, 5, 8, 11):
                    n = (i - 2) // 3
                    if n == 0:
                        pe.wait_ge(loaded["w_mkv"], 16)
                        for j in range(4):
                            wait_drained(pe, "memT", j)
                    b = wait_bank(pe, "memkv", n)
                    parts = []
                    if n < 2:
                        for j in range(2):
                            f = 2 * n + j
                            parts += contract(b[:, j * S:(j + 1) * S], [w_mkv[:, c, f * P:(f + 1) * P] for c in range(DC)],
                                              [aT_v[:, c, :] for c in range(DC)])
                    else:
                        t = n - 2
                        parts = contract(b[:, :], [aT_v[:, c, t * P:(t + 1) * P] for c in range(DC)],
                                         [w_mkv[:, c, 512:1024] for c in range(DC)])
                    product("memkv", n, parts)
            for i in range(2 * HEADS):
                wait_drained(pe, "PV", i)
            b = wait_bank(pe, "oss")
            parts = []
            for grp in range(2):
                for t in range(TT):
                    parts += contract(b[:, 2 * grp + t:2 * grp + t + 1],
                                      [sq_v[:, 4 * grp + c, t * P:(t + 1) * P] for c in range(4)], [one] * 4)
            product("oss", 0, parts)
            pe.wait_ge(loaded["w_o"], 16)
            for t in range(TT):
                for grp in range(2):
                    for n in range(2):
                        i = 4 * t + 2 * grp + n
                        b = wait_bank(pe, "wo", i)
                        product("wo", i, contract(b[:, :], [oT_v[:, 4 * grp + c, t * P:(t + 1) * P] for c in range(4)],
                                                  [w_o[:, 4 * grp + c, n * 512:(n + 1) * 512] for c in range(4)]))
            for i in (2, 3, 6, 7):
                wait_drained(pe, "wo", i)
            rows_to_T("h1T", h_v)
            for i in range(4):
                wait_drained(pe, "h1T", i)
            pe.wait_ge(loaded["w_mq"], 16)
            for i in range(2):
                b = wait_bank(pe, "mq", i)
                parts = []
                for j in range(2):
                    f = 2 * i + j
                    parts += contract(b[:, j * S:(j + 1) * S], [w_mq[:, c, f * P:(f + 1) * P] for c in range(DC)],
                                      [aT_v[:, c, :] for c in range(DC)])
                product("mq", i, parts)
            for i in range(2):
                wait_drained(pe, "mq", i)
            for i in range(4):
                wait_drained(pe, "memkv", i)
            for i in range(MEM_HEADS + 3):
                if i < MEM_HEADS:
                    b = wait_bank(pe, "cS", i)
                    product("cS", i, [(b[:, t * S:(t + 1) * S], mq[:, i, t * P:(t + 1) * P], mk[:, i, :], True, True)
                                      for t in range(TT)])
                if 2 <= i < MEM_HEADS + 2:
                    j = i - 2
                    pe.wait_ge(cprob_ready, j + 1)
                    transposes("cT", j, [(k * S + t * P, P, logit[:, j % 3, t * S + k * P:t * S + (k + 1) * P])
                                         for k in range(TT) for t in range(TT)])
                if i >= 3:
                    j = i - 3
                    wait_drained(pe, "cT", j)
                    b = wait_bank(pe, "cPV", j)
                    product("cPV", j, contract(b[:, 0:S], [mv[:, k, j * MD:(j + 1) * MD] for k in range(TT)],
                                               [probT[:, j % 2, k * S:(k + 1) * S] for k in range(TT)]))
            for i in range(MEM_HEADS):
                wait_drained(pe, "cPV", i)
            pe.wait_ge(loaded["w_mo"], 16)
            for t in range(TT):
                for n in range(2):
                    b = wait_bank(pe, "mo", 2 * t + n)
                    product("mo", 2 * t + n, contract(b[:, :], [moT[:, c, t * P:(t + 1) * P] for c in range(MEM_HEADS)],
                                                      [w_mo[:, c, n * 512:(n + 1) * 512] for c in range(MEM_HEADS)]))
            for i in range(4):
                wait_drained(pe, "mo", i)
            rows_to_T("h2T", h_v)
            for i in range(4):
                wait_drained(pe, "h2T", i)
            pe.wait_ge(loaded["w_r"], 16)
            b = wait_bank(pe, "router")
            parts = []
            for t in range(TT):
                parts += contract(b[:, t * E:(t + 1) * E], [aT_v[:, c, t * P:(t + 1) * P] for c in range(DC)],
                                  [wr[:, c * E:(c + 1) * E] for c in range(DC)])
            product("router", 0, parts)
            pe.wait_ge(sel_ready, 1)
            b = wait_bank(pe, "rank")
            product("rank", 0, contract(b[:, 0:E], [tri[:, 0, 0:P]], [sel[:, 0, :]])
                    + contract(b[:, E:2 * E], [tri[:, t, P:S] for t in range(TT)], [sel[:, t, :] for t in range(TT)])
                    + contract(b[0:1, 2 * E:3 * E], [one] * TT, [sel[:, t, :] for t in range(TT)]))
            wait_drained(pe, "rank")
            for i in range(BANKS - 1):
                n = Y0 + i
                pe.wait_ge(drained[n % BANKS], n // BANKS)

            def gather(p):
                for c in range(DC):
                    for t in range(TT):
                        mm = nc.tensor.matmul(bank[X_BANK][:, c * SEATS:(c + 1) * SEATS], xn_v[:, t, c * P:(c + 1) * P],
                                              oh[:, p, t, :], start=(t == 0), stop=(t == TT - 1))
                mm.then_inc(gathered, 1)

            pe.wait_ge(onehot_ready, 1)
            pe.wait_ge(normed["h2"], TT)
            gather(0)
            pe.wait_ge(gates_ready, 1)
            for t in range(TT):
                mm = nc.tensor.transpose(bank[D_BANK][0:E, t * P:(t + 1) * P], gates[:, t, :], ident)
            mm.then_inc(gatesT_full, 1)
            pe.wait_ge(gatesT_ready, 1)
            pe.wait_ge(loaded["b_down"], 16)
            for i in range(4):
                t, n = i // 2, i % 2
                nc.tensor.matmul(bank[Y_BANK[i]][:, :], gatesT[:, t * P:(t + 1) * P], bdown[0:E, n * 512:(n + 1) * 512],
                                 start=True, stop=False, skip_group_check=True)

            def half_rows(b, lhsT, w, arrived, count, used, full, first=True):
                for c in range(DC):
                    if c % (DC // 2) == 0:
                        pe.wait_ge(arrived[c // (DC // 2)], count[c // (DC // 2)])
                    for n in range(2):
                        mm = nc.tensor.matmul(b[64 * n:64 * n + 64, :], lhsT(c), w[c // 4][:, c % 4, n * 512:(n + 1) * 512],
                                              start=(first and c == 0), stop=(c == DC - 1), skip_group_check=True)
                    if c == DC // 2 - 1:
                        mm.then_inc(used, 1)
                mm.then_inc(full, 1)

            def gate_or_up(u, p, b, w, arrived, count, used, full):
                for n in range(2):
                    nc.tensor.matmul(b[64 * n:64 * n + 64, :], chosen[:, p, 2 * u + n, :], bgu,
                                     start=True, stop=False, skip_group_check=True)
                half_rows(b, lambda c: xg[:, p, c, :], w, arrived, count, used, full, first=False)

            def scatter(p, signal=None):
                for t in range(TT):
                    for n in range(2):
                        r = slice(64 * n, 64 * n + 64)
                        mm = nc.tensor.matmul(bank[Y_BANK[2 * t + n]][:, :], back[r, p, t * P:(t + 1) * P], res[r, p, :],
                                              start=False, stop=False, skip_group_check=True)
                    if signal is not None:
                        mm.then_inc(signal, 1)

            pe.wait_ge(rounds_ready, 1)
            n_pairs = pe.value_load(nit[0:1, 0:1], min_val=E // 2 - 1, max_val=S // SEATS * E // 2 - 1) + 1
            pe.wait_ge(loaded["b_gu"], 16)
            bank_a, bank_b, bank_d = bank[A_BANK], bank[B_BANK], bank[D_BANK]
            with pe.Fori(0, n_pairs) as pair:
                for p in range(2):
                    g = 2 * pair + p
                    pe.wait_ge(xg_ready, g + 1)
                    by_pair, by_expert = 16 * pair + 16, 16 * g + 16
                    gate_or_up(0, p, bank_a, w_gate[p], gate_loaded[p], (by_pair, by_pair), gate_used, gate_full)
                    pe.wait_ge(res_ready, g + 1)
                    scatter(1 - p)
                    for t in range(TT):
                        mm = nc.tensor.transpose(bank_d[:, t * P:(t + 1) * P], ohg[:, p, t, :], ident)
                    mm.then_inc(back_full, 1)
                    gate_or_up(1, p, bank_b, w_up[p], (up_loaded[p], up1_loaded), (by_pair, by_expert), up_used, up_full)
                    pe.wait_ge(onehot_ready, g + 2)
                    gather(1 - p)
                    pe.wait_ge(act_ready, g + 1)
                    for j in range(4):
                        mm = nc.tensor.transpose(bank_a[:, j * P:(j + 1) * P], act_rows[:, j * P:(j + 1) * P], ident)
                    mm.then_inc(actT_full, 1)
                    pe.wait_ge(back_ready, g + 1)
                    pe.wait_ge(actT_ready, g + 1)
                    half_rows(bank_d, lambda c: actT[:, c % 4, c // 4, :], w_down, down_loaded, (by_expert, by_expert),
                              down_used, down_full)
            pe.wait_ge(res_ready, n_pairs * 2 + 1)
            scatter(1, y_done)

        @block.vector
        def _(dve):
            V = nc.vector
            steps = [0]

            def link(ins):
                steps[0] += 1
                ins.then_inc(vec_chain, 1)
                dve.wait_ge(vec_chain, steps[0])

            def inverse_rms(name, src, width, mean, inv, signal=None):
                V.tensor_scalar(mean, src, 1.0 / width, EPS, ALU.mult, ALU.add).then_inc(meansq[name], 1)
                dve.wait_ge(rooted[name], 1)
                link(V.reciprocal(inv, mean))

            def normalise(name, src, dst):
                dve.wait_ge(sumsq[name], TT)
                inverse_rms(name, ssq, D, rms, rstd)
                dve.sem_inc(inv_root[name], 1)
                V.tensor_scalar(dst[:, 0, :], src[:, 0, :], rstd[:, 0:1], None, ALU.mult).then_inc(normed[name], 1)

            def scaled_T(name, gain, i):
                b = wait_filled(dve, name, i)
                for j in range(2):
                    c = 2 * i + j
                    last = V.tensor_scalar(aT_v[:, c, :], b[:, j * S:(j + 1) * S], gT[:, gain + c:gain + c + 1], None, ALU.mult)
                last.then_inc(drain_sem(name, i), 1)

            normalise("x", h_v, xn_v)
            b = wait_filled(dve, "gT")
            V.tensor_copy(gT[:, :], b[:, 0:G_ALL]).then_inc(drain_sem("gT"), 1)
            wait_drained(dve, "gT")
            scaled_T("xT", G_AT["g_mix"], 0)
            scaled_T("xT", G_AT["g_mix"], 2)
            for t in range(TT):
                b = wait_filled(dve, "rest", 2 * t)
                V.tensor_copy(lat[:, t, 0:340], b[:, 0:340]).then_inc(drain_sem("rest", 2 * t), 1)
            dve.wait_ge(loaded["b_f"], 16)
            for t in range(TT):
                wait_drained(dve, "rest", 2 * t)
            link(V.memset(logfpad, 0.0))
            link(V.tensor_tensor(fz[:, 0], lat[:, :, 0:HEADS], bf[:, :].unsqueeze(1).to_broadcast([P, TT, HEADS]), ALU.add))
            link(V.tensor_scalar(fz[:, 1], fz[:, 0], -1.0, None, ALU.mult))
            V.tensor_tensor(fz[:, 1], fz[:, 1], fz[:, 0], ALU.min).then_inc(f_in, 1)
            link(V.tensor_scalar(fz[:, 3], fz[:, 0], 0.0, None, ALU.min))
            dve.wait_ge(f_exp, 1)
            link(V.tensor_tensor(fz[:, 0], fz[:, 3], fz[:, 2], ALU.subtract))
            for t in range(TT):
                last = V.tensor_copy(logfpad[:, t, :].rearrange("p (a b) -> p a b", a=4)[:, :, 0:HEADS],
                                     fz[:, 0, t, :].unsqueeze(1).to_broadcast([P, 4, HEADS]))
            last.then_inc(logf_ready, 1)
            for t in range(TT):
                wait_drained(dve, "rest", 2 * t + 1)
            dve.wait_ge(sumsq["lat"], 2 * TT)
            link(V.tensor_scalar(lat_rms[:, 0, :], lat_ssq[:, 0, :], 1.0 / QL, EPS, ALU.mult, ALU.add))
            V.tensor_scalar(lat_rms[:, 1, :], lat_ssq[:, 1, :], 1.0 / KL, EPS, ALU.mult, ALU.add).then_inc(meansq["lat"], 1)
            dve.wait_ge(rooted["lat"], 1)
            link(V.reciprocal(lat_rstd, lat_rms))
            for t in range(TT):
                for k, (at, n) in enumerate(((8, QL), (8 + QL, KL))):
                    V.tensor_scalar(lat[:, t, at:at + n], lat[:, t, at:at + n], lat_rstd[:, k, t:t + 1], None,
                                    ALU.mult).then_inc(normed["lat"], 1)
            for t in range(TT):
                b = wait_filled(dve, "v", t)
                V.tensor_copy(vf_v[:, t, :], b[:, :]).then_inc(drain_sem("v", t), 1)
            for i in range(2):
                b = wait_filled(dve, "qk", i)
                V.tensor_copy(qkf[:, i * 512:(i + 1) * 512], b[:, :]).then_inc(drain_sem("qk", i), 1)
            normalise("mem", mem_v, mem_v)
            for i in range(3):
                b = wait_filled(dve, "latT", i)
                for j in range(2 if i < 2 else 1):
                    c = 2 * i + j
                    g = G_AT["g_q_lat"] + c
                    last = V.tensor_scalar(latT[:, c, :], b[:, j * S:(j + 1) * S], gT[:, g:g + 1], None, ALU.mult)
                last.then_inc(drain_sem("latT", i), 1)
            b = wait_filled(dve, "decay")
            link(V.tensor_scalar(aug_base, b[:, 0:S], cst[:, C_AUG:C_AUG + 1], cst[:, C_AUG + 1:C_AUG + 2], ALU.mult, ALU.add))
            V.tensor_scalar(aug_right, b[:, 0:S], cst[:, C_AUG + 2:C_AUG + 3], cst[:, C_AUG + 3:C_AUG + 4], ALU.mult,
                            ALU.add).then_inc(drain_sem("decay"), 1)
            wait_drained(dve, "decay")
            dve.sem_inc(aug_ready, 1)
            for pair in range(4):
                last = V.tensor_scalar(augL[:, pair, :], aug_base, cst[:, C_DEL + pair:C_DEL + pair + 1], None, ALU.mult)
            last.then_inc(aug_ready, 1)

            def rotate(x1, x2, cos, sin, tmp):
                V.tensor_tensor(tmp(0), x1, cos, ALU.mult)
                V.tensor_tensor(tmp(1), x2, sin, ALU.mult)
                V.tensor_tensor(tmp(2), x2, cos, ALU.mult)
                link(V.tensor_tensor(tmp(3), x1, sin, ALU.mult))
                V.tensor_tensor(x1, tmp(0), tmp(1), ALU.subtract)
                return V.tensor_tensor(x2, tmp(2), tmp(3), ALU.add)

            cos = cst[:, C_COS:C_COS + TT * HALF].rearrange("p (t r) -> p t r", t=TT)
            sin = cst[:, C_SIN:C_SIN + TT * HALF].rearrange("p (t r) -> p t r", t=TT)
            kr = lat[:, :, 8 + QL + KL:]
            link(rotate(kr[:, :, 0:HALF], kr[:, :, HALF:], cos, sin,
                        lambda k: rope_tmp[:, k, 0:TT * HALF].rearrange("p (t r) -> p t r", t=TT)))
            qh = qt.rearrange("p t (h d) -> p t h d", h=HEADS)
            kh = kt.rearrange("p t (h d) -> p t h d", h=HEADS)
            for t in range(TT):
                for n in range(2):
                    b = wait_filled(dve, "ukv", 2 * t + n)
                    bv = b[:, :].rearrange("p (h d) -> p h d", h=4)
                    V.tensor_copy(kh[:, t, 4 * n:4 * n + 4, 0:DH], bv[:, :, 0:DH])
                    V.tensor_copy(vm_v[:, t, 256 * n:256 * (n + 1)].rearrange("p (h d) -> p h d", h=4),
                                  bv[:, :, DH:]).then_inc(drain_sem("ukv", 2 * t + n), 1)
            for i in range(4):
                wait_drained(dve, "uq", i)
            for t in range(TT):
                last = rotate(qh[:, t, :, DH:DH + HALF], qh[:, t, :, DH + HALF:],
                              cos[:, t, :].unsqueeze(1).to_broadcast([P, HEADS, HALF]),
                              sin[:, t, :].unsqueeze(1).to_broadcast([P, HEADS, HALF]),
                              lambda k: rope_tmp[:, k, 128 * t:128 * (t + 1)].rearrange("p (h r) -> p h r", h=HEADS))
            last.then_inc(rope_ready, 1)
            for t in range(TT):
                last = V.tensor_copy(kh[:, t, :, DH:], kr[:, t, :].unsqueeze(1).to_broadcast([P, HEADS, ROPE]))
            for i in range(4):
                wait_drained(dve, "ukv", i)
            last.then_inc(rope_ready, 1)
            for i in range(4):
                b = wait_filled(dve, "mkT", i)
                V.tensor_copy(kmT[:, 2 * i:2 * i + 2, :], b[0:DQ, :].rearrange("p (h s) -> p h s", h=2)).then_inc(drain_sem("mkT", i), 1)
            wait_filled(dve, "qk", 3)
            for i in (0, 2):
                scaled_T("memT", G_AT["g_mem_kv"], i)

            def head_max(i):
                b = wait_filled(dve, "S", i)
                if i >= 3:
                    wait_filled(dve, "T", i - 3)
                l = logit[:, i % 3, :]
                mask = C_FOX if i < HEADS else C_MLA
                V.scalar_tensor_tensor(out=l[:, 0:384], in0=b[:, 0:384], scalar=(DH if i < HEADS else DQ) ** -0.5,
                                       in1=cst[:, mask:mask + 384], op0=ALU.mult, op1=ALU.add).then_inc(drain_sem("S", i), 1)
                wait_drained(dve, "S", i)
                V.reduce_max(mx[:, i % 3, 0:1], l[:, 0:P], AX)
                link(V.reduce_max(mx[:, i % 3, 1:2], l[:, P:384], AX))
                V.tensor_scalar(nmx[:, i % 3, :], mx[:, i % 3, :], -1.0, None, ALU.mult).then_inc(max_ready, 1)

            def head_probs(i):
                dve.wait_ge(exp_ready, i + 1)
                l = logit[:, i % 3, :]
                link(V.reciprocal(rden[:, i % 3, :], den[:, i % 3, :]))
                V.tensor_scalar(l[:, 0:P], l[:, 0:P], rden[:, i % 3, 0:1], None, ALU.mult)
                V.tensor_scalar(l[:, P:384], l[:, P:384], rden[:, i % 3, 1:2], None, ALU.mult).then_inc(prob_ready, 1)

            for i in range(4):
                wait_filled(dve, "mqT", i)
            for i in range(2 * HEADS + 1):
                if i < 2 * HEADS:
                    head_max(i)
                if i >= 1:
                    head_probs(i - 1)
                if i in (3, 6, 9, 12):
                    n = (i - 3) // 3
                    b = wait_filled(dve, "memkv", n)
                    V.tensor_copy(qkt[:, n * 512:(n + 1) * 512], b[:, :]).then_inc(drain_sem("memkv", n), 1)
            b = wait_filled(dve, "oss")
            V.tensor_scalar(o_ssq, b[:, 0:4], 1.0 / 512, EPS, ALU.mult, ALU.add).then_inc(drain_sem("oss"), 1)
            wait_drained(dve, "oss")
            dve.sem_inc(meansq["o"], 1)
            dve.wait_ge(rooted["o"], 1)
            link(V.reciprocal(o_rstd, o_ssq))
            for t in range(TT):
                for grp in range(2):
                    for n in range(2):
                        i = 4 * t + 2 * grp + n
                        b = wait_filled(dve, "wo", i)
                        if grp == 1:
                            wait_drained(dve, "wo", i - 2)
                        hs = h_v[:, t, n * 512:(n + 1) * 512]
                        V.scalar_tensor_tensor(out=hs, in0=b[:, :], scalar=o_rstd[:, 2 * grp + t:2 * grp + t + 1], in1=hs,
                                               op0=ALU.mult, op1=ALU.add).then_inc(drain_sem("wo", i), 1)
            for i in (0, 2):
                scaled_T("h1T", G_AT["g_mem_q"], i)
            dve.wait_ge(sumsq["h1"], TT)
            inverse_rms("h1", ssq, D, rms, rstd)
            V.tensor_scalar(q_scale, rstd, MD ** -0.5, None, ALU.mult).then_inc(inv_root["h1"], 1)
            link(V.tensor_scalar(q_neg, rstd, -(MD ** -0.5), None, ALU.mult))
            b = wait_filled(dve, "mq", 0)
            V.tensor_copy(latr[:, 0:512], b[:, :]).then_inc(drain_sem("mq", 0), 1)
            for i in range(MEM_HEADS + 1):
                if i < MEM_HEADS:
                    b = wait_filled(dve, "cS", i)
                    link(V.tensor_reduce(mx[:, i % 3, :], b[:, :].rearrange("p (t s) -> p t s", t=TT), AX, ALU.max))
                    V.tensor_tensor(nmx[:, i % 3, :], mx[:, i % 3, :], q_neg, ALU.mult).then_inc(cmax_ready, 1)
                if i >= 1:
                    j = i - 1
                    dve.wait_ge(cexp_ready, j + 1)
                    wait_drained(dve, "cS", j)
                    l = logit[:, j % 3, :]
                    link(V.reciprocal(rden[:, j % 3, :], den[:, j % 3, :]))
                    V.tensor_scalar(l[:, 0:S], l[:, 0:S], rden[:, j % 3, 0:1], None, ALU.mult)
                    V.tensor_scalar(l[:, S:2 * S], l[:, S:2 * S], rden[:, j % 3, 1:2], None, ALU.mult).then_inc(cprob_ready, 1)
            for i in range(4):
                t, n = i // 2, i % 2
                b = wait_filled(dve, "mo", i)
                hs = h_v[:, t, n * 512:(n + 1) * 512]
                V.tensor_tensor(hs, b[:, :], hs, ALU.add).then_inc(drain_sem("mo", i), 1)
            for i in (0, 2):
                scaled_T("h2T", G_AT["g_ffn"], i)
            normalise("h2", h_v, xn_v)
            b = wait_filled(dve, "router")
            dve.wait_ge(loaded["b_r"], 16)
            for t in range(TT):
                last = V.scalar_tensor_tensor(out=lg[:, t, :], in0=b[:, t * E:(t + 1) * E], scalar=rstd[:, t:t + 1],
                                              in1=brt[:, :], op0=ALU.mult, op1=ALU.add)
            last.then_inc(drain_sem("router"), 1)
            wait_drained(dve, "router")
            for t in range(TT):
                last = V.max(topv[:, t, :], lg[:, t, :])
            link(last)
            for t in range(TT):
                V.tensor_scalar(ex[:, t, :], lg[:, t, :], topv[:, t, 0:1], None, ALU.subtract).then_inc(r_shift, 1)
                V.tensor_scalar(gt[:, t, :], lg[:, t, :], topv[:, t, TOPK - 1:TOPK], None, ALU.is_gt)
                last = V.tensor_scalar(eq[:, t, :], lg[:, t, :], topv[:, t, TOPK - 1:TOPK], None, ALU.is_equal)
            link(last)
            for t in range(TT):
                V.tensor_tensor_scan(cs[:, t, :], cst[:, C_ONE:C_ONE + 1].to_broadcast([P, E]), eq[:, t, :], 0.0, ALU.mult, ALU.add)
            link(V.reduce_sum(r_tmp[:, 0:2], gt, AX))
            link(V.tensor_scalar(r_tmp[:, 2:4], r_tmp[:, 0:2], -1.0, float(TOPK), ALU.mult, ALU.add))
            for t in range(TT):
                last = V.tensor_scalar(keep[:, t, :], cs[:, t, :], r_tmp[:, 2 + t:3 + t], None, ALU.is_le)
            link(last)
            link(V.tensor_tensor(keep, keep, eq, ALU.mult))
            V.tensor_tensor(sel, keep, gt, ALU.add).then_inc(sel_ready, 1)
            dve.wait_ge(sel_ready, 1)
            dve.wait_ge(r_exp, 1)
            link(V.tensor_tensor(ex, ex, sel, ALU.mult))
            link(V.reduce_sum(r_tmp[:, 0:2], ex, AX))
            link(V.reciprocal(r_tmp[:, 0:2], r_tmp[:, 0:2]))
            for t in range(TT):
                last = V.tensor_scalar(gates[:, t, :], ex[:, t, :], r_tmp[:, t:t + 1], None, ALU.mult)
            last.then_inc(gates_ready, 1)
            b = wait_filled(dve, "rank")
            link(V.tensor_tensor(pos, b[:, 0:TT * E].rearrange("p (t e) -> p t e", t=TT), sel, ALU.mult))
            link(V.tensor_scalar(pos, pos, -1.0, None, ALU.add))
            dve.wait_ge(gates_ready, 1)

            def select(e, p):
                for t in range(TT):
                    at = pos[:, t, bass.ds(e, 1)]
                    V.tensor_scalar(oh[:, p, t, :], cst[:, C_SEAT:C_SEAT + SEATS], at, None, ALU.is_equal)
                    last = V.tensor_scalar(ohg[:, p, t, :], cst[:, C_SEAT:C_SEAT + P], at, gates[:, t, bass.ds(e, 1)],
                                           ALU.is_equal, ALU.mult)
                last = V.tensor_copy(chosen[:, p], cst[:, bass.ds(4 * e, 4)].unsqueeze(2).to_broadcast([P, 4, SEATS]))
                last.then_inc(onehot_ready, 1)

            def advance(e):
                return V.tensor_scalar(pos[:, :, bass.ds(e, 1)], pos[:, :, bass.ds(e, 1)], -float(SEATS), None, ALU.add)

            def take_rows(p):
                g0 = G_AT["g_ffn"]
                V.tensor_tensor(xg[:, p, :, :], bank[X_BANK][:, :].rearrange("p (c s) -> p c s", c=DC),
                                gT[:, g0:g0 + DC].unsqueeze(2).to_broadcast([P, DC, SEATS]), ALU.mult).then_inc(xg_ready, 1)

            select(0, 0)
            V.reduce_max(cntmax, b[0:1, 2 * E:3 * E], AX).then_inc(drain_sem("rank"), 1)
            wait_drained(dve, "rank")
            link(V.tensor_scalar(over, cst[0:1, C_LIM:C_LIM + 3], cntmax, None, ALU.is_lt))
            link(V.reduce_sum(novr, over, AX))
            V.tensor_scalar(nit[0:1, 0:1], novr, float(E // 2), float(E // 2 - 1), ALU.mult, ALU.add).then_inc(rounds_ready, 1)
            dve.wait_ge(gatesT_full, 1)
            V.tensor_copy(gatesT, bank[D_BANK][0:E, 0:S]).then_inc(gatesT_ready, 1)
            dve.wait_ge(onehot_ready, 1)
            link(advance(0))
            dve.wait_ge(gathered, 1)
            take_rows(0)
            dve.wait_ge(rounds_ready, 1)
            n_pairs = dve.value_load(nit[0:1, 0:1], min_val=E // 2 - 1, max_val=S // SEATS * E // 2 - 1) + 1
            LINKS = 3
            with dve.Fori(0, n_pairs) as pair:
                for p in range(2):
                    g = 2 * pair + p
                    e_next = (g + 1) & (E - 1)
                    at = [LINKS * p]

                    def chain(ins):
                        at[0] += 1
                        ins.then_inc(moe_chain, 1)
                        dve.wait_ge(moe_chain, pair * (2 * LINKS) + at[0])

                    dve.wait_ge(gate_full, g + 1)
                    V.tensor_scalar(zg, bank[A_BANK][:, :], LIMIT, None, ALU.min).then_inc(gate_ready, 1)
                    select(e_next, 1 - p)
                    dve.wait_ge(onehot_ready, g + 2)
                    chain(advance(e_next))
                    dve.wait_ge(up_full, g + 1)
                    chain(V.tensor_scalar(zu, bank[B_BANK][:, :], LIMIT, -LIMIT, ALU.min, ALU.max))
                    chain(V.scalar_tensor_tensor(out=prod, in0=zu, scalar=1.0, in1=zg, op0=ALU.add, op1=ALU.mult))
                    dve.wait_ge(sig_ready, g + 1)
                    V.tensor_tensor(act_rows, prod, sig, ALU.mult).then_inc(act_ready, 1)
                    dve.wait_ge(gathered, g + 2)
                    take_rows(1 - p)
            for t in range(TT):
                dve.wait_ge(y_done, t + 1)
                for n in range(2):
                    hs = h_v[:, t, n * 512:(n + 1) * 512]
                    last = V.tensor_tensor(hs, bank[Y_BANK[2 * t + n]][:, :], hs, ALU.add)
                last.then_inc(residual3, 1)
            dve.wait_ge(loaded["g_final"], 16)
            for t in range(TT):
                dve.wait_ge(sumsq["h3"], t + 1)
                one_t = slice(t, t + 1)
                V.tensor_scalar(rms[:, one_t], ssq[:, one_t], 1.0 / D, EPS, ALU.mult, ALU.add).then_inc(meansq["h3"], 1)
                dve.wait_ge(rooted["h3"], t + 1)
                link(V.reciprocal(rstd[:, one_t], rms[:, one_t]))
                V.scalar_tensor_tensor(out=xn_v[:, t, :], in0=h_v[:, t, :], scalar=rstd[:, one_t], in1=gfin,
                                       op0=ALU.mult, op1=ALU.mult).then_inc(out_ready, 1)

        @block.gpsimd
        def _(pool):
            wait_filled(pool, "cPV", MEM_HEADS - 1)
            nc.gpsimd.memset(back[:, 1, :], 0.0)
            nc.gpsimd.memset(res[:, 1, :], 0.0).then_inc(res_ready, 1)

        @block.scalar
        def _(act):
            A_ = nc.scalar.activation
            steps = [0]

            def link(ins):
                steps[0] += 1
                ins.then_inc(act_chain, 1)
                act.wait_ge(act_chain, steps[0])

            def squares(name, src, dst):
                for t in range(TT):
                    A_(dst[:, t, :], src[:, t, :], ACT.Square, accum_out=ssq[:, t:t + 1]).then_inc(sumsq[name], 1)

            def root(name, ap):
                act.wait_ge(meansq[name], 1)
                A_(ap, ap, ACT.Sqrt).then_inc(rooted[name], 1)

            def second_tile(name, src, dst):
                act.wait_ge(inv_root[name], 1)
                A_(dst[:, 1, :], src[:, 1, :], ACT.Copy, scale=rstd[:, 1:2]).then_inc(normed[name], 1)

            def scaled_T(name, gain, i):
                b = wait_filled(act, name, i)
                for j in range(2):
                    c = 2 * i + j
                    last = A_(aT_v[:, c, :], b[:, j * S:(j + 1) * S], ACT.Copy, scale=gT[:, gain + c:gain + c + 1])
                last.then_inc(drain_sem(name, i), 1)

            act.wait_ge(loaded["x"], 16)
            squares("x", h_v, xn_v)
            act.wait_ge(sumsq["x"], TT)
            root("x", rms)
            second_tile("x", h_v, xn_v)
            wait_drained(act, "gT")
            for i in (1, 3):
                scaled_T("xT", G_AT["g_mix"], i)
            for t in range(TT):
                b = wait_filled(act, "rest", 2 * t + 1)
                A_(lat[:, t, 340:680], b[:, 0:340], ACT.Copy).then_inc(drain_sem("rest", 2 * t + 1), 1)
            for i in range(4):
                wait_drained(act, "rest", i)
            for t in range(TT):
                for k, (at, n) in enumerate(((8, QL), (8 + QL, KL))):
                    A_(scratch[:, 1024 * k + 512 * t:1024 * k + 512 * t + n], lat[:, t, at:at + n], ACT.Square,
                       accum_out=lat_ssq[:, k, t:t + 1]).then_inc(sumsq["lat"], 1)
            act.wait_ge(f_in, 1)
            link(A_(fz[:, 2], fz[:, 1], ACT.Exp))
            A_(fz[:, 2], fz[:, 2], ACT.Ln, bias=1.0).then_inc(f_exp, 1)
            root("lat", lat_rms)
            act.wait_ge(loaded["mem"], 16)
            act.wait_ge(normed["x"], TT)
            act.wait_ge(sumsq["lat"], 2 * TT)
            squares("mem", mem_v, v3(work, TT, 0, TT * D))
            for i in (2, 3):
                b = wait_filled(act, "qk", i)
                A_(qkf[:, i * 512:(i + 1) * 512], b[:, :], ACT.Copy).then_inc(drain_sem("qk", i), 1)
            act.wait_ge(sumsq["mem"], TT)
            root("mem", rms)
            second_tile("mem", mem_v, mem_v)
            for i in range(4):
                t, n = i // 2, i % 2
                b = wait_filled(act, "uq", i)
                A_(qt[:, t, n * 384:(n + 1) * 384], b[:, 0:384], ACT.Copy).then_inc(drain_sem("uq", i), 1)
            for i in range(4):
                b = wait_filled(act, "mqT", i)
                A_(qmT[:, 2 * i:2 * i + 2, :], b[0:DQ, :].rearrange("p (h s) -> p h s", h=2), ACT.Copy).then_inc(drain_sem("mqT", i), 1)
            for i in (1, 3):
                scaled_T("memT", G_AT["g_mem_kv"], i)

            for i in range(2 * HEADS + 3):
                if i < 2 * HEADS:
                    act.wait_ge(max_ready, i + 1)
                    l = logit[:, i % 3, :]
                    for k, (a, n) in enumerate(((0, P), (P, S))):
                        last = A_(l[:, a:a + n], l[:, a:a + n], ACT.Exp, bias=nmx[:, i % 3, k:k + 1],
                                  accum_out=den[:, i % 3, k:k + 1])
                    last.then_inc(exp_ready, 1)
                if 2 <= i < 2 * HEADS + 2:
                    j = i - 2
                    b = wait_filled(act, "T", j)
                    if j >= 2:
                        wait_filled(act, "PV", j - 2)
                    A_(probT[:, j % 2, 0:384], b[:, 0:384], ACT.Copy).then_inc(drain_sem("T", j), 1)
                if i >= 3:
                    j = i - 3
                    b = wait_filled(act, "PV", j)
                    if j == 0:
                        wait_filled(act, "memT", 3)
                        act.wait_ge(normed["x"], TT)
                    r = slice(64 * (j % 2), 64 * (j % 2) + 64)
                    g = G_AT["g_fox_out"] + j // 2
                    A_(oT_v[r, j // 2, :], b[r, 0:S], ACT.Copy, scale=gT[r, g:g + 1])
                    A_(sq_v[r, j // 2, :], b[r, 0:S], ACT.Square).then_inc(drain_sem("PV", j), 1)
            root("o", o_ssq)
            wait_filled(act, "oss")
            for i in (2, 3, 6, 7):
                wait_drained(act, "wo", i)
            squares("h1", h_v, xn_v)
            for i in (1, 3):
                scaled_T("h1T", G_AT["g_mem_q"], i)
            root("h1", rms)
            b = wait_filled(act, "mq", 1)
            A_(latr[:, 512:1024], b[:, :], ACT.Copy).then_inc(drain_sem("mq", 1), 1)
            act.wait_ge(inv_root["h1"], 1)
            for i in range(MEM_HEADS + 3):
                if i < MEM_HEADS:
                    act.wait_ge(cmax_ready, i + 1)
                    if i >= 3:
                        wait_filled(act, "cT", i - 3)
                    b = wait_filled(act, "cS", i)
                    for t in range(TT):
                        last = A_(logit[:, i % 3, t * S:(t + 1) * S], b[:, t * S:(t + 1) * S], ACT.Exp,
                                  bias=nmx[:, i % 3, t:t + 1], scale=q_scale[:, t:t + 1], accum_out=den[:, i % 3, t:t + 1])
                    last.then_inc(drain_sem("cS", i), 1)
                    wait_drained(act, "cS", i)
                    act.sem_inc(cexp_ready, 1)
                if 2 <= i < MEM_HEADS + 2:
                    j = i - 2
                    b = wait_filled(act, "cT", j)
                    if j >= 2:
                        wait_filled(act, "cPV", j - 2)
                    A_(probT[:, j % 2, :], b[:, :], ACT.Copy).then_inc(drain_sem("cT", j), 1)
                if i >= 3:
                    j = i - 3
                    b = wait_filled(act, "cPV", j)
                    A_(moT[:, j, :], b[:, 0:S], ACT.Copy).then_inc(drain_sem("cPV", j), 1)
            for i in range(4):
                wait_drained(act, "mo", i)
            squares("h2", h_v, xn_v)
            for i in (1, 3):
                scaled_T("h2T", G_AT["g_ffn"], i)
            root("h2", rms)
            second_tile("h2", h_v, xn_v)
            act.wait_ge(r_shift, TT)
            A_(ex, ex, ACT.Exp).then_inc(r_exp, 1)
            act.wait_ge(rounds_ready, 1)
            n_pairs = act.value_load(nit[0:1, 0:1], min_val=E // 2 - 1, max_val=S // SEATS * E // 2 - 1) + 1
            with act.Fori(0, n_pairs) as pair:
                for p in range(2):
                    g = 2 * pair + p
                    act.wait_ge(gate_ready, g + 1)
                    A_(sig, zg, ACT.Sigmoid, scale=ALPHA).then_inc(sig_ready, 1)
                    act.wait_ge(back_full, g + 1)
                    A_(back[:, p, :], bank[D_BANK][:, 0:S], ACT.Copy).then_inc(back_ready, 1)
                    act.wait_ge(actT_full, g + 1)
                    A_(actT.rearrange("p j h s -> p (j h s)"), bank[A_BANK][:, :], ACT.Copy).then_inc(actT_ready, 1)
                    act.wait_ge(down_full, g + 1)
                    A_(res[:, p, :], bank[D_BANK][:, :], ACT.Copy).then_inc(res_ready, 1)
            for t in range(TT):
                act.wait_ge(residual3, t + 1)
                A_(xn_v[:, t, :], h_v[:, t, :], ACT.Square, accum_out=ssq[:, t:t + 1]).then_inc(sumsq["h3"], 1)
            for t in range(TT):
                act.wait_ge(meansq["h3"], t + 1)
                A_(rms[:, t:t + 1], rms[:, t:t + 1], ACT.Sqrt).then_inc(rooted["h3"], 1)


def kernel(**inputs):
    import concourse.bacc as bacc
    from concourse.bass_utils import run_bass_kernel_spmd

    nc = bacc.Bacc("TRN2", target_bir_lowering=False, num_devices=1)
    arrays, access = {}, {}
    for name, a in dict(inputs, constants=constants()).items():
        a = np.ascontiguousarray(a)
        arrays[f"in_{name}"] = a
        access[name] = nc.dram_tensor(f"in_{name}", a.shape, mybir.dt.from_np(a.dtype), kind="ExternalInput").ap()
    out = nc.dram_tensor("out", (1, S, D), F32, kind="ExternalOutput").ap()
    layer_kernel(nc, access, out)
    r = run_bass_kernel_spmd(nc, [arrays], core_ids=[0])
    return r.results[0]["out"]
```

```python
from contextlib import ExitStack

import numpy as np

import concourse.bass as bass
from concourse import mybir

F32 = mybir.dt.float32
I32 = mybir.dt.int32
ALU = mybir.AluOpType
ACT = mybir.ActivationFunctionType
AX = mybir.AxisListType.X

P = 128
D = 1024
S = 256
TT = S // P
DC = D // P
EPS = 1e-6
HEADS = 8
DH = 64
ROPE = 32
HALF = ROPE // 2
DQ = DH + ROPE
QL, KL = 384, 256
REST = HEADS + QL + KL + ROPE
MEM_HEADS = 4
MD = 128
E = 32
TOPK = 4
SEATS = 64
AHEAD = 4
LIMIT, ALPHA = 7.0, 1.702
MASKED = -1e30

C_ID, C_TRI, C_FOX, C_MLA, C_SEAT, C_COS, C_SIN = 0, 128, 640, 1024, 1408, 1536, 1568
C_AUG, C_DEL, C_ONE, C_LIM, C_END = 1600, 1604, 1608, 1609, 1612

GAINS = (("g_mix", 8), ("g_q_lat", 3), ("g_kv_lat", 2), ("g_fox_out", 4), ("g_mla_out", 4),
         ("g_mem_q", 8), ("g_mem_kv", 8), ("g_ffn", 8))
G_AT = {}
for _n, _c in GAINS:
    G_AT[_n] = sum(c for _, c in GAINS[:len(G_AT)])
G_ALL = sum(c for _, c in GAINS)


def constants():
    c = np.zeros((P, C_END), np.float32)
    tok = np.arange(S)
    c[:, C_ID:C_ID + P] = np.eye(P)
    tri = (tok[:, None] <= tok[None, :]).astype(np.float32)
    c[:, C_TRI:C_TRI + 2 * S] = tri.reshape(TT, P, S).transpose(1, 0, 2).reshape(P, TT * S)
    for at, ok in ((C_FOX, tok[None, :] <= tok[:, None]), (C_MLA, tok[None, :] // 64 <= tok[:, None] // 64)):
        m = np.where(ok, 0.0, MASKED).astype(np.float32)
        c[:, at:at + P] = m[:P, :P]
        c[:, at + P:at + P + S] = m[P:, :]
    c[:, C_SEAT:C_SEAT + P] = np.tile(np.arange(1, SEATS + 1), P // SEATS)
    inv = (1.0 / (np.float32(10000.0) ** (np.arange(0, ROPE, 2, dtype=np.float32) / ROPE))).astype(np.float32)
    ang = tok.astype(np.float32)[:, None] * inv[None, :]
    for at, f in ((C_COS, np.cos), (C_SIN, np.sin)):
        c[:, at:at + TT * HALF] = f(ang).astype(np.float32).reshape(TT, P, HALF).transpose(1, 0, 2).reshape(P, -1)
    for base in (0, 64):
        lo, hi = slice(base, base + 8), slice(base + 32, base + 40)
        c[hi, C_AUG] = 8.0
        c[lo, C_AUG + 1] = -8.0
        c[lo, C_AUG + 2] = 1.0
        c[hi, C_AUG + 3] = 1.0
        for pair in range(HEADS // 2):
            h = 2 * pair + base // 64
            c[base + h, C_DEL + pair] = c[base + 32 + h, C_DEL + pair] = 1.0
    c[:, C_ONE] = 1.0
    c[:, C_LIM:C_LIM + 3] = (SEATS, 2 * SEATS, 3 * SEATS)
    return c


MEMKV_AT = tuple(range(2, 2 * HEADS + 1, 2))


CROSS = [("mq", 0), ("mq", 1), ("cS", 0), ("mq", 2), ("cS", 1), ("mq", 3), ("cS", 2), ("cT", 0), ("cS", 3), ("cT", 1),
         ("cPV", 0), ("cT", 2), ("out", 0), ("cPV", 1), ("cT", 3), ("out", 1), ("cPV", 2), ("cPV", 3), ("out", 2)]


def fills():
    order = [("xT", 0), ("xT", 1), ("gT", 0), ("xT", 2), ("xT", 3)]

    def stage(name, n):
        order.extend((name, i) for i in range(n))

    stage("v", 2)
    stage("rest", 4)
    order.extend([("qk", 0), ("qk", 1)])
    stage("latT", 3)
    stage("decay", 1)
    order.extend([("qk", 2), ("qk", 3)])
    stage("memT", 4)
    stage("uq", 4)
    stage("ukv", 4)
    stage("mqT", 4)
    stage("mkT", 4)
    for i in range(2 * HEADS + 3):
        if i < 2 * HEADS:
            order.append(("S", i))
        if i in MEMKV_AT:
            order.append(("memkv", MEMKV_AT.index(i)))
        if 2 <= i < 2 * HEADS + 2:
            order.append(("T", i - 2))
        if i >= 3:
            order.append(("PV", i - 3))
        if i == 2 * HEADS + 1:
            order.append(("oss", 0))
    stage("wo", 6)
    stage("h1T", 2)
    order.extend([("wo", 6), ("wo", 7), ("h1T", 2), ("h1T", 3)])
    order.extend(step for step in CROSS if step[0] != "out")
    at = order.index(("cPV", 1))
    order[at:at] = [("mo", i) for i in range(4)]
    stage("h2T", 2)
    stage("router", 1)
    order.extend([("h2T", 2), ("h2T", 3)])
    stage("rank", 1)
    return order


ORDER = fills()
FILL = {key: n for n, key in enumerate(ORDER)}
BANKS = 8
Y0 = len(ORDER)
Y_BANK = [(Y0 + i) % BANKS for i in range(4)]
X_BANK, A_BANK, B_BANK, D_BANK = [(Y0 + 4 + i) % BANKS for i in range(4)]
GATHER_BANK = (X_BANK, B_BANK)


def layer_kernel(nc, A, out):
    with ExitStack() as ctx:
        def sb(name, width, dt=F32):
            return ctx.enter_context(nc.sbuf_tensor(name, [P, width], dt))

        def sem(name):
            return ctx.enter_context(nc.semaphore(name))

        bank = [ctx.enter_context(nc.psum_tensor(f"bank{i}", [P, 512], F32)) for i in range(BANKS)]

        SLOT = 4096
        slots = sb("slots", 6 * SLOT)
        cst = sb("cst", C_END)
        gT = sb("gT", G_ALL)
        hres = sb("hres", TT * D)
        xn = sb("xn", TT * D)
        late = sb("late", SLOT)
        aT = late[:, 0:DC * S]
        qkf = late[:, DC * S:2 * DC * S]
        memo = sb("memo", TT * D)
        mid = sb("mid", 2 * SLOT)
        vf = mid[:, 0:1024]
        vm = mid[:, 1024:2048]
        latr = mid[:, 2048:2048 + TT * REST + 5 * S]
        qkt = mid[:, 4736:4736 + 2 * TT * HEADS * DQ]
        work = sb("work", 2 * HEADS * S + 3 * 512 + 2 * 512)
        aug = sb("aug", 2 * S)
        wr = sb("wr", DC * E)
        brt = sb("brt", E)
        bf = sb("bf", HEADS)
        small = sb("small", 96)
        route = sb("route", 12 * TT * E)
        nit = sb("nit", 1, I32)

        def v3(t, a, at=0, n=None, rows=slice(None)):
            n = n or t.shape[1] - at
            return t[rows, at:at + n].rearrange("p (a b) -> p a b", a=a)

        h_v, xn_v = v3(hres, TT), v3(xn, TT)
        aT_v = v3(aT, DC)
        mem_v, oT_v = v3(memo, TT), v3(memo, 8)
        sq_v = v3(xn, 8)
        qfT, kfT = v3(qkf, 4, 0, 1024), v3(qkf, 4, 1024, 1024)
        gfin = slots[:, 0:D]
        vf_v, vm_v = v3(vf, TT), v3(vm, TT)
        lat = v3(latr, TT, 0, TT * REST)
        latT = v3(latr, 5, TT * REST, 5 * S)
        mq, moT = v3(mid, 4, SLOT, 1024), v3(mid, 4, SLOT + 3072, 1024)
        qt, kt = v3(qkt, TT, 0, TT * 768), v3(qkt, TT, TT * 768, TT * 768)
        mkv = mid[:, SLOT + 1024:SLOT + 3072]
        mk, mv = v3(mkv, 4, 0, 1024), v3(mkv, TT, 1024, 1024)
        qmT = work[0:DQ, 0:2048].rearrange("p (h s) -> p h s", h=HEADS)
        kmT = work[0:DQ, 2048:4096].rearrange("p (h s) -> p h s", h=HEADS)
        logit = v3(work, 3, 4096, 3 * 512)
        probT = v3(work, 2, 4096 + 3 * 512, 2 * 512)
        scratch = work
        rope_tmp = v3(work, 4, 0, 1024)
        ident = cst[:, C_ID:C_ID + P]
        tri = v3(cst, TT, C_TRI, TT * S)
        one = cst[:, C_ONE:C_ONE + 1]
        graw = logit[:, 0, 0:P]
        augL = slots[:, 5 * SLOT + 2048:5 * SLOT + 3072].rearrange("p (a s) -> p a s", a=4)
        aug_base, aug_right = aug[:, 0:S], aug[:, S:2 * S]
        logfpad = v3(slots, TT, 5 * SLOT + 3072, TT * P)
        fz = slots[:, 5 * SLOT + 3328:5 * SLOT + 3328 + 64].rearrange("p (k t h) -> p k t h", k=4, t=TT)

        def slot(c, a, n, at=0):
            return slots[:, c * SLOT + at:c * SLOT + at + n].rearrange("p (a b) -> p a b", a=a)

        w_qk = slot(0, DC, DC * 1024)
        w_v = slot(2, DC, DC * 512)
        w_rest = slot(3, DC, DC * REST)
        w_uq = slot(3, 3, 3 * 768, DC * REST)
        w_ukv = slot(5, 2, 2 * 1024)
        w_mkv = slot(0, DC, DC * 1024)
        w_mq = slot(2, DC, DC * 512)
        w_o = slot(3, 8, 8 * D)
        w_mo = slot(5, 4, 4 * D)
        w_gate = [[slot(0, 4, 4 * D), slot(1, 4, 4 * D)],
                  [v3(mid, 4, 0, 4 * D), v3(mid, 4, SLOT, 4 * D)]]
        w_up = [[slot(2, 4, 4 * D), slot(3, 4, 4 * D)], [v3(late, 4), slot(3, 4, 4 * D)]]
        w_down = [slot(4, 4, 4 * D), slot(5, 4, 4 * D)]

        def st(i, n=2):
            return small[:, i:i + n]

        ssq, rms, rstd = st(0), st(2), st(4)
        o_ssq, o_rstd = st(8, 4), st(12, 4)
        mx, nmx, den, rden = [v3(small, 3, 16 + 6 * k, 6) for k in range(4)]
        topv = v3(small, TT, 40, 16)
        r_tmp = st(56, 4)
        cntmax, over, novr = small[0:1, 60:61], small[0:1, 62:65], small[0:1, 66:67]
        lat_ssq, lat_rstd = v3(small, 2, 68, 4), v3(small, 2, 72, 4)
        lat_rms = v3(small, 2, 76, 4)

        q_scale, q_neg = st(80), st(82)
        warm = st(84, 1)

        def rt(i):
            return v3(route, TT, i * TT * E, TT * E)

        lg, gt, eq, cs, sel, ex, gates, pos, keep = [rt(i) for i in range(9)]
        gatesT = memo[0:E, 512:512 + S]

        oh = v3(work, TT, 0, TT * P)
        ohg = work[:, 256:768].rearrange("p (b t c) -> p b t c", b=2, t=TT)
        back = v3(work, 2, 768, 512)
        xg = v3(work, DC, 1280, DC * P)
        zg, zu, sig, prod, act_rows = [work[:, 2304 + 512 * k:2816 + 512 * k] for k in range(5)]
        actT = work[:, 4864:5376].rearrange("p (j h s) -> p j h s", j=4, h=2)
        res = v3(work, 2, 5376, 1024)
        chosen = aug[:, :].rearrange("p (b q s) -> p b q s", b=2, q=4)
        bgu = memo[:, 0:512]
        bdown = work[0:E, 2304:2304 + D]

        filled = [sem(f"filled{i}") for i in range(BANKS)]
        drained = [sem(f"drained{i}") for i in range(BANKS)]
        names = ("x0 x1 ident w_v0 w_v1 cst gains bias b_f b_r w_r w_rest w_uq w_ukv w_v w_qk mem w_mkv w_o w_mq w_mo "
                 "b_down b_gu g_final").split()
        loaded = {n: sem("loaded_" + n) for n in names}
        vec_chain = sem("vec_chain")
        act_chain = sem("act_chain")
        sumsq = {n: sem("sumsq_" + n) for n in "x mem lat h1 h2 h3".split()}
        meansq = {n: sem("meansq_" + n) for n in "x mem lat o h1 h2 h3".split()}
        rooted = {n: sem("rooted_" + n) for n in "x mem lat o h1 h2 h3".split()}
        inv_root = {n: sem("inv_root_" + n) for n in "x mem h1 h2".split()}
        normed = {n: sem("normed_" + n) for n in "x mem lat h1 h2".split()}
        residual3 = sem("residual3")
        warm_ready = sem("warm_ready")
        f_in, f_exp = sem("f_in"), sem("f_exp")
        logf_ready, aug_ready = sem("logf_ready"), sem("aug_ready")
        rope_ready = sem("rope_ready")
        max_ready, exp_ready, prob_ready = sem("max_ready"), sem("exp_ready"), sem("prob_ready")
        cmax_ready, cexp_ready, cprob_ready = sem("cmax_ready"), sem("cexp_ready"), sem("cprob_ready")
        r_shift, r_exp, sel_ready, gates_ready = sem("r_shift"), sem("r_exp"), sem("sel_ready"), sem("gates_ready")
        rounds_ready = sem("rounds_ready")
        gatesT_full, gatesT_ready = sem("gatesT_full"), sem("gatesT_ready")
        gate_loaded = [[sem(f"gate_loaded{p}_{k}") for k in range(2)] for p in range(2)]
        up_loaded = [sem("up_loaded_even0"), sem("up_loaded_odd0")]
        up1_loaded = sem("up_loaded1")
        down_loaded = [sem(f"down_loaded{k}") for k in range(2)]
        first_chosen = sem("first_chosen")
        seats_ready = sem("seats_ready")
        onehot_ready = sem("onehot_ready")
        gathered, xg_ready = sem("gathered"), sem("xg_ready")
        gate_used, gate_full = sem("gate_used"), sem("gate_full")
        up_used, up_full = sem("up_used"), sem("up_full")
        down_used = sem("down_used")
        gate_ready, sig_ready, act_ready = sem("gate_ready"), sem("sig_ready"), sem("act_ready")
        actT_full, actT_ready = sem("actT_full"), sem("actT_ready")
        back_full, back_ready = sem("back_full"), sem("back_ready")
        down_full, res_ready = sem("down_full"), sem("res_ready")
        moe_chain = sem("moe_chain")
        y_done = sem("y_done")
        out_ready, stored = sem("out_ready"), sem("stored")

        def wait_bank(pe, name, i=0):
            n = FILL[(name, i)]
            if n >= BANKS:
                pe.wait_ge(drained[n % BANKS], n // BANKS)
            return bank[n % BANKS]

        def wait_filled(eng, name, i=0):
            n = FILL[(name, i)]
            eng.wait_ge(filled[n % BANKS], n // BANKS + 1)
            return bank[n % BANKS]

        def wait_drained(eng, name, i=0):
            n = FILL[(name, i)]
            eng.wait_ge(drained[n % BANKS], n // BANKS + 1)

        def fill_sem(name, i=0):
            return filled[FILL[(name, i)] % BANKS]

        def drain_sem(name, i=0):
            return drained[FILL[(name, i)] % BANKS]

        def dram(name, pat, **kw):
            return A[name].rearrange(pat, **kw)

        block = ctx.enter_context(nc.Block())

        @block.sync
        def _(sp):
            def load(name, dst, src):
                sp.dma_start(dst, src).then_inc(loaded[name], 16)

            w_in = dram("w_in", "o (c p) n -> p (o c) n", p=P)
            for t in range(TT):
                load(f"x{t}", h_v[:, t, :], dram("x", "b (t p) d -> p (b t) d", p=P)[:, t, :])
            load("ident", ident, A["constants"][:, 0:P])
            load("w_v0", w_v[:, 0:4, :], w_in[:, 0:4, 1024:1536])
            at = 0
            for name, n in GAINS:
                load("gains", graw[at:at + n, :], dram(name, "o (c q) -> (o c) q", q=P))
                at += n
            load("w_v1", w_v[:, 4:8, :], w_in[:, 4:8, 1024:1536])
            load("w_rest", w_rest, w_in[:, :, 1536:1536 + REST])
            load("b_f", bf[:, :], A["b_f"].partition_broadcast(P).rearrange("p o n -> p (o n)"))
            load("b_r", brt[:, :], A["b_router"].partition_broadcast(P).rearrange("p o n -> p (o n)"))
            load("w_qk", w_qk, w_in[:, :, 0:1024])
            load("cst", cst[:, P:], A["constants"][:, P:])
            load("w_uq", w_uq, dram("w_uq", "o (c p) n -> p (o c) n", p=P))
            load("w_ukv", w_ukv, dram("w_ukv", "o (c p) n -> p (o c) n", p=P))
            load("mem", mem_v, dram("mem", "b (t p) d -> p (b t) d", p=P))
            load("w_r", v3(wr, DC), dram("w_router", "o (c p) n -> p (o c) n", p=P))
            wait_filled(sp, "qk", 3)
            load("w_mkv", w_mkv, dram("w_mem_kv", "o (c p) n -> p (o c) n", p=P))
            load("w_mq", w_mq, dram("w_mem_q", "o (c p) n -> p (o c) n", p=P))
            wait_filled(sp, "uq", 3)
            load("w_o", w_o, dram("w_o", "o (c p) n -> p (o c) n", p=P))
            wait_filled(sp, "S", HEADS - 1)
            load("w_mo", w_mo, dram("w_mem_o", "o (c p) n -> p (o c) n", p=P))

            w_gu = dram("w_gate_up", "o e (c p) n -> p (o e) c n", p=P)
            w_dn = dram("w_down", "o e (c p) n -> p (o e) c n", p=P)

            def load_rows(dst, src, arrived):
                sp.dma_start(dst, src.rearrange("p o c n -> p (o c) n")).then_inc(arrived, 16)

            def rows(k):
                return slice(4 * k, 4 * k + 4)

            def load_gate(k, p, e):
                load_rows(w_gate[p][k], w_gu[:, bass.ds(e, 1), rows(k), 0:D], gate_loaded[p][k])

            def load_up(k, p, e):
                load_rows(w_up[p][k], w_gu[:, bass.ds(e, 1), rows(k), D:2 * D], (up_loaded[p], up1_loaded)[k])

            def load_down(k, e):
                load_rows(w_down[k], w_dn[:, bass.ds(e, 1), rows(k), :], down_loaded[k])

            wait_filled(sp, "memkv", len(MEMKV_AT) - 1)
            load_gate(0, 0, 0)
            load_gate(1, 0, 0)
            wait_filled(sp, "PV", 2 * HEADS - 1)
            load_gate(0, 1, 1)
            wait_filled(sp, "wo", 7)
            load("b_gu", bgu, dram("b_gate_up", "o e (q n) -> (o e q) n", q=4))
            load_up(1, 0, 0)
            load_down(0, 0)
            wait_filled(sp, "mq", 3)
            load_up(0, 0, 0)
            wait_filled(sp, "cPV", MEM_HEADS - 1)
            load("b_down", bdown, dram("b_down", "o e n -> (o e) n"))
            wait_filled(sp, "mo", 3)
            load_down(1, 0)
            load_gate(1, 1, 1)
            wait_filled(sp, "router", 0)
            load_up(0, 1, 1)
            sp.wait_ge(rounds_ready, 1)
            more_pairs = sp.value_load(nit[0:1, 0:1], min_val=E // 2 - 1, max_val=S // SEATS * E // 2 - 1)

            def refill(used, count, load_piece, *where):
                sp.wait_ge(used, count)
                sp.nop(nofuse=True)
                load_piece(*where)

            def single_pieces(g, p, e):
                refill(up_full, g, load_up, 1, p, e)
                refill(down_used, g, load_down, 0, e)
                refill(down_full, g, load_down, 1, e)

            def double_pieces(g, p, e):
                refill(gate_used, g + 1, load_gate, 0, p, e)
                refill(gate_full, g + 1, load_gate, 1, p, e)
                refill(up_used, g + 1, load_up, 0, p, e)

            with sp.Fori(0, AHEAD) as pair:
                for p in range(2):
                    g = 2 * pair + p
                    double_pieces(g, p, (g + 2) & (E - 1))
                    single_pieces(g + 1, 1 - p, (g + 1) & (E - 1))
            with sp.Fori(AHEAD, more_pairs) as pair:
                for p in range(2):
                    g = 2 * pair + p
                    single_pieces(g + 1, 1 - p, (g + 1) & (E - 1))
                    double_pieces(g, p, (g + 2) & (E - 1))
            single_pieces(2 * more_pairs + 1, 1, E - 1)
            load("g_final", gfin, A["g_final"].partition_broadcast(P))
            for t in range(TT):
                sp.wait_ge(out_ready, t + 1)
                sp.dma_start(out.rearrange("b (t p) d -> p (b t) d", p=P)[:, t, :], xn_v[:, t, :]).then_inc(stored, 16)
            sp.wait_ge(stored, 16 * TT)

        @block.tensor
        def _(pe):
            def transposes(name, i, blocks):
                b = wait_bank(pe, name, i)
                for col, rows, src in blocks:
                    last = nc.tensor.transpose(b[0:rows, col:col + src.shape[0]], src, ident[0:src.shape[0], 0:src.shape[0]])
                last.then_inc(fill_sem(name, i), 1)

            def rows_to_T(name, src, i):
                transposes(name, i, [(256 * c + 128 * t, P, src[:, t, (2 * i + c) * P:(2 * i + c + 1) * P])
                                     for c in range(2) for t in range(TT)])

            def tile_to_T(name, src, t):
                for k in range(2):
                    transposes(name, 2 * t + k, [(P * c, P, src[:, t, (4 * k + c) * P:(4 * k + c + 1) * P]) for c in range(4)])

            def product(name, i, parts, b=None):
                for o, l, r, first, stop in parts:
                    mm = nc.tensor.matmul(o, l, r, start=first, stop=stop)
                mm.then_inc(fill_sem(name, i), 1)

            def contract(o, ls, rs):
                n = len(ls)
                return [(o, ls[k], rs[k], k == 0, k == n - 1) for k in range(n)]

            pe.wait_ge(loaded["ident"], 16)
            pe.wait_ge(normed["x"], TT)
            for i in range(4):
                if i == 2:
                    pe.wait_ge(loaded["gains"], 16 * len(GAINS))
                    transposes("gT", 0, [(0, P, graw[0:G_ALL, :])])
                rows_to_T("xT", xn_v, i)
            for t in range(TT):
                b = wait_bank(pe, "v", t)
                for c in range(DC):
                    if t == 0 and c % 4 == 0:
                        pe.wait_ge(loaded[f"w_v{c // 4}"], 16)
                    if t == 0 and c % 2 == 0:
                        wait_drained(pe, "xT", c // 2)
                    mm = nc.tensor.matmul(b[:, :], aT_v[:, c, t * P:(t + 1) * P], w_v[:, c, :], start=(c == 0), stop=(c == DC - 1))
                mm.then_inc(fill_sem("v", t), 1)
            pe.wait_ge(loaded["w_rest"], 16)
            for t in range(TT):
                for n in range(2):
                    b = wait_bank(pe, "rest", 2 * t + n)
                    product("rest", 2 * t + n, contract(b[:, 0:340], [aT_v[:, c, t * P:(t + 1) * P] for c in range(DC)],
                                                        [w_rest[:, c, n * 340:(n + 1) * 340] for c in range(DC)]))
            def qk_rows(i):
                b = wait_bank(pe, "qk", i)
                parts = []
                for j in range(2):
                    f = 2 * i + j
                    parts += contract(b[:, j * S:(j + 1) * S], [w_qk[:, c, f * P:(f + 1) * P] for c in range(DC)],
                                      [aT_v[:, c, :] for c in range(DC)])
                product("qk", i, parts)

            pe.wait_ge(loaded["w_qk"], 16)
            for i in range(2):
                qk_rows(i)
            pe.wait_ge(normed["lat"], 2 * TT)
            for i in range(3):
                transposes("latT", i, [(256 * j + 128 * t, P, lat[:, t, 8 + (2 * i + j) * P:8 + (2 * i + j + 1) * P])
                                       for j in range(2 if i < 2 else 1) for t in range(TT)])
            pe.wait_ge(logf_ready, 1)
            pe.wait_ge(loaded["cst"], 16)
            b = wait_bank(pe, "decay")
            product("decay", 0, contract(b[:, 0:S], [logfpad[:, t, :] for t in range(TT)], [tri[:, t, :] for t in range(TT)]))
            for i in range(2, 4):
                qk_rows(i)
            pe.wait_ge(normed["mem"], TT)
            for i in range(4):
                rows_to_T("memT", mem_v, i)
            for i in range(3):
                wait_drained(pe, "latT", i)
            pe.wait_ge(loaded["w_uq"], 16)
            for t in range(TT):
                for n in range(2):
                    b = wait_bank(pe, "uq", 2 * t + n)
                    product("uq", 2 * t + n, contract(b[:, 0:384], [latT[:, c, t * P:(t + 1) * P] for c in range(3)],
                                                      [w_uq[:, c, n * 384:(n + 1) * 384] for c in range(3)]))
            pe.wait_ge(loaded["w_ukv"], 16)
            for t in range(TT):
                for n in range(2):
                    b = wait_bank(pe, "ukv", 2 * t + n)
                    product("ukv", 2 * t + n, contract(b[:, :], [latT[:, 3 + c, t * P:(t + 1) * P] for c in range(2)],
                                                       [w_ukv[:, c, n * 512:(n + 1) * 512] for c in range(2)]))
            pe.wait_ge(rope_ready, 2)
            for i in range(4):
                transposes("mqT", i, [(256 * j + 128 * t, DQ, qt[:, t, (2 * i + j) * DQ:(2 * i + j + 1) * DQ])
                                      for j in range(2) for t in range(TT)])
            for i in range(4):
                wait_drained(pe, "ukv", i)
            for i in range(4):
                transposes("mkT", i, [(256 * j + 128 * t, DQ, kt[:, t, (2 * i + j) * DQ:(2 * i + j + 1) * DQ])
                                      for j in range(2) for t in range(TT)])

            def scores(i):
                b = wait_bank(pe, "S", i)
                parts = []
                for o, q0, n in ((0, 0, P), (P, P, S)):
                    if i < HEADS:
                        r = slice(64 * (i % 2), 64 * (i % 2) + 64)
                        a = slice(64 * (i % 2), 64 * (i % 2) + 40)
                        ls = [qfT[r, i // 2, q0:q0 + P], augL[a, i // 2, q0:q0 + P]]
                        rs = [kfT[r, i // 2, 0:n], aug_right[a, 0:n]]
                    else:
                        ls, rs = [qmT[:, i - HEADS, q0:q0 + P]], [kmT[:, i - HEADS, 0:n]]
                    parts += contract(b[:, o:o + n], ls, rs)
                product("S", i, parts)

            def head_out(i):
                wait_drained(pe, "T", i)
                b = wait_bank(pe, "PV", i)
                v = vf_v if i < HEADS else vm_v
                h, r = i % HEADS, slice(64 * (i % 2), 64 * (i % 2) + 64)
                product("PV", i, [(b[r, 0:S], v[:, 0, h * DH:(h + 1) * DH], probT[:, i % 2, 0:S], True, False),
                                  (b[r, P:S], v[:, 1, h * DH:(h + 1) * DH], probT[:, i % 2, S:S + P], False, True)])

            def square_sums(b, pairs, at):
                return [part for t in range(TT)
                        for part in contract(b[:, at + t:at + t + 1], [sq_v[:, c, t * P:(t + 1) * P] for c in pairs],
                                             [one] * len(pairs))]

            for i in range(4):
                wait_drained(pe, "qk", i)
            for t in range(TT):
                wait_drained(pe, "v", t)
            pe.wait_ge(aug_ready, 2)
            for i in range(2 * HEADS + 3):
                if i < 2 * HEADS:
                    if i == HEADS:
                        for j in range(4):
                            wait_drained(pe, "mqT", j)
                            wait_drained(pe, "mkT", j)
                    scores(i)
                if i in MEMKV_AT:
                    n = MEMKV_AT.index(i)
                    if n == 0:
                        pe.wait_ge(loaded["w_mkv"], 16)
                        for j in range(4):
                            wait_drained(pe, "memT", j)
                    b = wait_bank(pe, "memkv", n)
                    if n < MEM_HEADS:
                        parts = contract(b[:, 0:S], [w_mkv[:, c, n * P:(n + 1) * P] for c in range(DC)],
                                         [aT_v[:, c, :] for c in range(DC)])
                    else:
                        t, at = (n - MEM_HEADS) // 2, 512 + (n % 2) * 256
                        parts = contract(b[:, 0:256], [aT_v[:, c, t * P:(t + 1) * P] for c in range(DC)],
                                         [w_mkv[:, c, at:at + 256] for c in range(DC)])
                    product("memkv", n, parts)
                if 2 <= i < 2 * HEADS + 2:
                    j = i - 2
                    pe.wait_ge(prob_ready, j + 1)
                    transposes("T", j, [(P * k, P, logit[:, j % 3, P * k:P * (k + 1)]) for k in range(3)])
                if i >= 3:
                    head_out(i - 3)
                if i == 2 * HEADS + 1:
                    for j in range(2 * HEADS - 2):
                        wait_drained(pe, "PV", j)
                    ss = wait_bank(pe, "oss")
                    for o, l, r, first, stop in square_sums(ss, range(0, 4), 0) + square_sums(ss, range(4, 7), 2):
                        nc.tensor.matmul(o, l, r, start=first, stop=stop)
            for i in (2 * HEADS - 2, 2 * HEADS - 1):
                wait_drained(pe, "PV", i)
            product("oss", 0, square_sums(ss, range(7, 8), 4))
            pe.wait_ge(loaded["w_o"], 16)
            for i in range(8):
                t, grp, n = i // 4, i // 2 % 2, i % 2
                b = wait_bank(pe, "wo", i)
                product("wo", i, contract(b[:, :], [oT_v[:, 4 * grp + c, t * P:(t + 1) * P] for c in range(4)],
                                          [w_o[:, 4 * grp + c, n * 512:(n + 1) * 512] for c in range(4)]))
                if i in (5, 7):
                    t = (i - 5) // 2
                    for j in (4 * t + 2, 4 * t + 3):
                        wait_drained(pe, "wo", j)
                    tile_to_T("h1T", h_v, t)

            def out_part(j, i):
                t, n = i // 2, i % 2
                b = wait_bank(pe, "mo", i) if j == 0 else bank[FILL[("mo", i)] % BANKS]
                return nc.tensor.matmul(b[:, :], moT[:, j, t * P:(t + 1) * P], w_mo[:, j, n * 512:(n + 1) * 512],
                                        start=(j == 0), stop=(j == MEM_HEADS - 1))

            pe.wait_ge(loaded["w_mq"], 16)
            for name, j in CROSS:
                if name == "mq":
                    b = wait_bank(pe, "mq", j)
                    for c in range(DC):
                        if j == 0 and c % 4 == 0:
                            for t in range(TT):
                                wait_drained(pe, "h1T", 2 * t + c // 4)
                        mm = nc.tensor.matmul(b[:, 0:S], w_mq[:, c, j * P:(j + 1) * P], aT_v[:, c, :],
                                              start=(c == 0), stop=(c == DC - 1))
                    mm.then_inc(fill_sem("mq", j), 1)
                elif name == "cS":
                    wait_drained(pe, "mq", j)
                    wait_drained(pe, "memkv", j)
                    b = wait_bank(pe, "cS", j)
                    product("cS", j, [(b[:, t * S:(t + 1) * S], mq[:, j, t * P:(t + 1) * P], mk[:, j, :], True, True)
                                      for t in range(TT)])
                elif name == "cT":
                    pe.wait_ge(cprob_ready, j + 1)
                    transposes("cT", j, [(k * S + t * P, P, logit[:, j % 3, t * S + k * P:t * S + (k + 1) * P])
                                         for k in range(TT) for t in range(TT)])
                elif name == "cPV":
                    for n in range(MEM_HEADS, 2 * MEM_HEADS):
                        wait_drained(pe, "memkv", n)
                    wait_drained(pe, "cT", j)
                    b = wait_bank(pe, "cPV", j)
                    product("cPV", j, contract(b[:, 0:S], [mv[:, k, j * MD:(j + 1) * MD] for k in range(TT)],
                                               [probT[:, j % 2, k * S:(k + 1) * S] for k in range(TT)]))
                else:
                    if j == 0:
                        pe.wait_ge(loaded["w_mo"], 16)
                    wait_drained(pe, "cPV", j)
                    for n in range(4):
                        out_part(j, n)
            wait_drained(pe, "cPV", MEM_HEADS - 1)
            for n in range(3):
                out_part(MEM_HEADS - 1, n).then_inc(fill_sem("mo", n), 1)
            for i in (0, 1):
                wait_drained(pe, "mo", i)
            tile_to_T("h2T", h_v, 0)
            out_part(MEM_HEADS - 1, 3).then_inc(fill_sem("mo", 3), 1)
            pe.wait_ge(loaded["w_r"], 16)
            router = wait_bank(pe, "router")
            for t in range(TT):
                if t == 1:
                    for i in (2, 3):
                        wait_drained(pe, "mo", i)
                    tile_to_T("h2T", h_v, 1)
                for c in range(DC):
                    if c % 4 == 0:
                        wait_drained(pe, "h2T", 2 * t + c // 4)
                    mm = nc.tensor.matmul(router[:, t * E:(t + 1) * E], aT_v[:, c, t * P:(t + 1) * P],
                                          wr[:, c * E:(c + 1) * E], start=(c == 0), stop=(c == DC - 1))
            mm.then_inc(fill_sem("router"), 1)

            def bias(u, p, b):
                for n in range(2):
                    nc.tensor.matmul(b[64 * n:64 * n + 64, :], chosen[:, p, 2 * u + n, :], bgu,
                                     start=True, stop=False, skip_group_check=True)

            pe.wait_ge(drained[A_BANK], (Y0 + 5) // BANKS)
            pe.wait_ge(loaded["b_gu"], 16)
            pe.wait_ge(first_chosen, 1)
            bias(0, 0, bank[A_BANK])
            pe.wait_ge(sel_ready, 1)
            b = wait_bank(pe, "rank")
            product("rank", 0, contract(b[:, 0:E], [tri[:, 0, 0:P]], [sel[:, 0, :]])
                    + contract(b[:, E:2 * E], [tri[:, t, P:S] for t in range(TT)], [sel[:, t, :] for t in range(TT)])
                    + contract(b[0:1, 2 * E:3 * E], [one] * TT, [sel[:, t, :] for t in range(TT)]))
            for i in range(BANKS - 1):
                n = Y0 + i
                pe.wait_ge(drained[n % BANKS], n // BANKS)

            def gather(k):
                for c in range(4):
                    for t in range(TT):
                        mm = nc.tensor.matmul(bank[GATHER_BANK[k]][:, c * P:(c + 1) * P],
                                              xn_v[:, t, (4 * k + c) * P:(4 * k + c + 1) * P],
                                              oh[:, t, :], start=(t == 0), stop=(t == TT - 1))
                mm.then_inc(gathered, 1)

            pe.wait_ge(gates_ready, 1)
            for t in range(TT):
                mm = nc.tensor.transpose(bank[B_BANK][0:E, t * P:(t + 1) * P], gates[:, t, :], ident)
            mm.then_inc(gatesT_full, 1)
            pe.wait_ge(seats_ready, 1)
            pe.wait_ge(normed["h2"], TT)
            for k in range(2):
                gather(k)
                if k == 0:
                    pe.wait_ge(gatesT_ready, 1)
                    pe.wait_ge(loaded["b_down"], 16)
                for n in range(2):
                    nc.tensor.matmul(bank[Y_BANK[2 * k + n]][:, :], gatesT[:, k * P:(k + 1) * P],
                                     bdown[0:E, n * 512:(n + 1) * 512], start=True, stop=False, skip_group_check=True)
            wait_drained(pe, "rank")

            def half_rows(b, lhsT, w, arrived, count, used, full, first=True):
                for c in range(DC):
                    if c % (DC // 2) == 0:
                        pe.wait_ge(arrived[c // (DC // 2)], count[c // (DC // 2)])
                    for n in range(2):
                        mm = nc.tensor.matmul(b[64 * n:64 * n + 64, :], lhsT(c), w[c // 4][:, c % 4, n * 512:(n + 1) * 512],
                                              start=(first and c == 0), stop=(c == DC - 1), skip_group_check=True)
                    if c == DC // 2 - 1:
                        mm.then_inc(used, 1)
                mm.then_inc(full, 1)

            def projection(p, b, w, arrived, count, used, full):
                half_rows(b, lambda c: xg[:, c, p * SEATS:(p + 1) * SEATS], w, arrived, count, used, full, first=False)

            def scatter(p, t):
                for n in range(2):
                    r = slice(64 * n, 64 * n + 64)
                    mm = nc.tensor.matmul(bank[Y_BANK[2 * t + n]][:, :], back[r, p, t * P:(t + 1) * P], res[r, p, :],
                                          start=False, stop=False, skip_group_check=True)
                return mm

            pe.wait_ge(rounds_ready, 1)
            more_pairs = pe.value_load(nit[0:1, 0:1], min_val=E // 2 - 1, max_val=S // SEATS * E // 2 - 1)
            bank_a, bank_b, bank_d = bank[A_BANK], bank[B_BANK], bank[D_BANK]

            def expert(pair, p, last=False):
                g = 2 * pair + p
                if p == 0:
                    pe.wait_ge(xg_ready, 2 * pair + 2)
                by_pair, by_expert = 16 * pair + 16, 16 * g + 16
                projection(p, bank_a, w_gate[p], gate_loaded[p], (by_pair, by_pair), gate_used, gate_full)
                pe.wait_ge(res_ready, g + 1)
                if p == 1 and not last:
                    for t in range(TT):
                        scatter(0, t)
                bias(1, p, bank_b)
                projection(p, bank_b, w_up[p], (up_loaded[p], up1_loaded), (by_pair, by_expert), up_used, up_full)
                for t in range(TT):
                    mm = nc.tensor.transpose(bank_d[:, t * P:(t + 1) * P], ohg[:, p, t, :], ident)
                mm.then_inc(back_full, 1)
                if p == 0 or last:
                    scatter(1 - p, 0)
                else:
                    pe.wait_ge(seats_ready, pair + 2)
                    gather(0)
                pe.wait_ge(act_ready, g + 1)
                for j in range(4):
                    mm = nc.tensor.transpose(bank_a[:, j * P:(j + 1) * P], act_rows[:, j * P:(j + 1) * P], ident)
                mm.then_inc(actT_full, 1)
                if p == 0 or last:
                    scatter(1 - p, 1)
                else:
                    gather(1)
                pe.wait_ge(back_ready, g + 1)
                pe.wait_ge(actT_ready, g + 1)
                half_rows(bank_d, lambda c: actT[:, c % 4, c // 4, :], w_down, down_loaded, (by_expert, by_expert),
                          down_used, down_full)
                if not last:
                    pe.wait_ge(onehot_ready, g + 2)
                    bias(0, 1 - p, bank_a)

            with pe.Fori(0, more_pairs) as pair:
                for p in range(2):
                    expert(pair, p)
            expert(more_pairs, 0)
            expert(more_pairs, 1, last=True)
            pe.wait_ge(res_ready, 2 * more_pairs + 3)
            for t in range(TT):
                scatter(1, t).then_inc(y_done, 1)

        @block.vector
        def _(dve):
            V = nc.vector
            steps = [0]

            def link(ins):
                steps[0] += 1
                ins.then_inc(vec_chain, 1)
                dve.wait_ge(vec_chain, steps[0])

            def inverse_rms(name):
                V.tensor_scalar(rms, ssq, 1.0 / D, EPS, ALU.mult, ALU.add).then_inc(meansq[name], 1)
                dve.wait_ge(rooted[name], 1)
                link(V.reciprocal(rstd, rms))

            def normalise(name, src, dst):
                dve.wait_ge(sumsq[name], TT)
                inverse_rms(name)
                dve.sem_inc(inv_root[name], 1)
                V.tensor_scalar(dst[:, 0, :], src[:, 0, :], rstd[:, 0:1], None, ALU.mult).then_inc(normed[name], 1)

            def scaled_T(name, gain, i):
                b = wait_filled(dve, name, i)
                for j in range(2):
                    c = 2 * i + j
                    last = V.tensor_scalar(aT_v[:, c, :], b[:, j * S:(j + 1) * S], gT[:, gain + c:gain + c + 1], None, ALU.mult)
                last.then_inc(drain_sem(name, i), 1)

            def scaled_tile_T(name, gain, i):
                t, k = i // 2, i % 2
                b = wait_filled(dve, name, i)
                V.tensor_tensor(aT_v[:, 4 * k:4 * k + 4, t * P:(t + 1) * P], b[:, :].rearrange("p (c s) -> p c s", c=4),
                                gT[:, gain + 4 * k:gain + 4 * k + 4].unsqueeze(2).to_broadcast([P, 4, P]),
                                ALU.mult).then_inc(drain_sem(name, i), 1)

            normalise("x", h_v, xn_v)
            b = wait_filled(dve, "gT")
            V.tensor_copy(gT[:, :], b[:, 0:G_ALL]).then_inc(drain_sem("gT"), 1)
            wait_drained(dve, "gT")
            scaled_T("xT", G_AT["g_mix"], 0)
            scaled_T("xT", G_AT["g_mix"], 2)
            for t in range(TT):
                b = wait_filled(dve, "v", t)
                V.tensor_copy(vf_v[:, t, :], b[:, :]).then_inc(drain_sem("v", t), 1)
            for t in range(TT):
                b = wait_filled(dve, "rest", 2 * t)
                V.tensor_copy(lat[:, t, 0:340], b[:, 0:340]).then_inc(drain_sem("rest", 2 * t), 1)
            dve.wait_ge(loaded["b_f"], 16)
            for t in range(TT):
                wait_drained(dve, "rest", 2 * t)
            link(V.memset(logfpad, 0.0))
            link(V.tensor_tensor(fz[:, 0], lat[:, :, 0:HEADS], bf[:, :].unsqueeze(1).to_broadcast([P, TT, HEADS]), ALU.add))
            link(V.tensor_scalar(fz[:, 1], fz[:, 0], -1.0, None, ALU.mult))
            V.tensor_tensor(fz[:, 1], fz[:, 1], fz[:, 0], ALU.min).then_inc(f_in, 1)
            link(V.tensor_scalar(fz[:, 3], fz[:, 0], 0.0, None, ALU.min))
            dve.wait_ge(f_exp, 1)
            link(V.tensor_tensor(fz[:, 0], fz[:, 3], fz[:, 2], ALU.subtract))
            for t in range(TT):
                last = V.tensor_copy(logfpad[:, t, :].rearrange("p (a b) -> p a b", a=4)[:, :, 0:HEADS],
                                     fz[:, 0, t, :].unsqueeze(1).to_broadcast([P, 4, HEADS]))
            last.then_inc(logf_ready, 1)
            for t in range(TT):
                wait_drained(dve, "rest", 2 * t + 1)
            dve.wait_ge(sumsq["lat"], 2 * TT)
            link(V.tensor_scalar(lat_rms[:, 0, :], lat_ssq[:, 0, :], 1.0 / QL, EPS, ALU.mult, ALU.add))
            V.tensor_scalar(lat_rms[:, 1, :], lat_ssq[:, 1, :], 1.0 / KL, EPS, ALU.mult, ALU.add).then_inc(meansq["lat"], 1)
            dve.wait_ge(rooted["lat"], 1)
            link(V.reciprocal(lat_rstd, lat_rms))
            for t in range(TT):
                for k, (at, n) in enumerate(((8, QL), (8 + QL, KL))):
                    V.tensor_scalar(lat[:, t, at:at + n], lat[:, t, at:at + n], lat_rstd[:, k, t:t + 1], None,
                                    ALU.mult).then_inc(normed["lat"], 1)
            normalise("mem", mem_v, mem_v)
            for i in range(2):
                b = wait_filled(dve, "qk", i)
                V.tensor_copy(qkf[:, i * 512:(i + 1) * 512], b[:, :]).then_inc(drain_sem("qk", i), 1)
            for i in (0, 2):
                b = wait_filled(dve, "latT", i)
                for j in range(2 if i == 0 else 1):
                    c = 2 * i + j
                    g = G_AT["g_q_lat"] + c
                    last = V.tensor_scalar(latT[:, c, :], b[:, j * S:(j + 1) * S], gT[:, g:g + 1], None, ALU.mult)
                last.then_inc(drain_sem("latT", i), 1)
            b = wait_filled(dve, "decay")
            link(V.tensor_scalar(aug_base, b[:, 0:S], cst[:, C_AUG:C_AUG + 1], cst[:, C_AUG + 1:C_AUG + 2], ALU.mult, ALU.add))
            V.tensor_scalar(aug_right, b[:, 0:S], cst[:, C_AUG + 2:C_AUG + 3], cst[:, C_AUG + 3:C_AUG + 4], ALU.mult,
                            ALU.add).then_inc(drain_sem("decay"), 1)
            wait_drained(dve, "decay")
            dve.sem_inc(aug_ready, 1)
            for pair in range(4):
                last = V.tensor_scalar(augL[:, pair, :], aug_base, cst[:, C_DEL + pair:C_DEL + pair + 1], None, ALU.mult)
            last.then_inc(aug_ready, 1)

            def rotate(x1, x2, cos, sin, tmp):
                V.tensor_tensor(tmp(0), x1, cos, ALU.mult)
                V.tensor_tensor(tmp(1), x2, sin, ALU.mult)
                V.tensor_tensor(tmp(2), x2, cos, ALU.mult)
                link(V.tensor_tensor(tmp(3), x1, sin, ALU.mult))
                V.tensor_tensor(x1, tmp(0), tmp(1), ALU.subtract)
                return V.tensor_tensor(x2, tmp(2), tmp(3), ALU.add)

            cos = cst[:, C_COS:C_COS + TT * HALF].rearrange("p (t r) -> p t r", t=TT)
            sin = cst[:, C_SIN:C_SIN + TT * HALF].rearrange("p (t r) -> p t r", t=TT)
            kr = lat[:, :, 8 + QL + KL:]
            link(rotate(kr[:, :, 0:HALF], kr[:, :, HALF:], cos, sin,
                        lambda k: rope_tmp[:, k, 0:TT * HALF].rearrange("p (t r) -> p t r", t=TT)))
            qh = qt.rearrange("p t (h d) -> p t h d", h=HEADS)
            kh = kt.rearrange("p t (h d) -> p t h d", h=HEADS)
            for t in range(TT):
                last = V.tensor_copy(kh[:, t, :, DH:], kr[:, t, :].unsqueeze(1).to_broadcast([P, HEADS, ROPE]))
            last.then_inc(rope_ready, 1)
            wait_filled(dve, "qk", 3)
            for i in (0, 2):
                scaled_T("memT", G_AT["g_mem_kv"], i)
            for t in range(TT):
                for n in range(2):
                    wait_drained(dve, "uq", 2 * t + n)
                last = rotate(qh[:, t, :, DH:DH + HALF], qh[:, t, :, DH + HALF:],
                              cos[:, t, :].unsqueeze(1).to_broadcast([P, HEADS, HALF]),
                              sin[:, t, :].unsqueeze(1).to_broadcast([P, HEADS, HALF]),
                              lambda k: rope_tmp[:, k, 128 * t:128 * (t + 1)].rearrange("p (h r) -> p h r", h=HEADS))
            last.then_inc(rope_ready, 1)
            for t in range(TT):
                for n in range(2):
                    b = wait_filled(dve, "ukv", 2 * t + n)
                    bv = b[:, :].rearrange("p (h d) -> p h d", h=4)
                    V.tensor_copy(kh[:, t, 4 * n:4 * n + 4, 0:DH], bv[:, :, 0:DH])
                    V.tensor_copy(vm_v[:, t, 256 * n:256 * (n + 1)].rearrange("p (h d) -> p h d", h=4),
                                  bv[:, :, DH:]).then_inc(drain_sem("ukv", 2 * t + n), 1)
            for i in (0, 1):
                b = wait_filled(dve, "mkT", i)
                V.tensor_copy(kmT[:, 2 * i:2 * i + 2, :], b[0:DQ, :].rearrange("p (h s) -> p h s", h=2)).then_inc(drain_sem("mkT", i), 1)

            def head_max(i):
                b = wait_filled(dve, "S", i)
                if i >= 3:
                    wait_filled(dve, "T", i - 3)
                l = logit[:, i % 3, :]
                mask = C_FOX if i < HEADS else C_MLA
                V.scalar_tensor_tensor(out=l[:, 0:384], in0=b[:, 0:384], scalar=(DH if i < HEADS else DQ) ** -0.5,
                                       in1=cst[:, mask:mask + 384], op0=ALU.mult, op1=ALU.add).then_inc(drain_sem("S", i), 1)
                wait_drained(dve, "S", i)
                V.reduce_max(mx[:, i % 3, 0:1], l[:, 0:P], AX)
                link(V.reduce_max(mx[:, i % 3, 1:2], l[:, P:384], AX))
                V.tensor_scalar(nmx[:, i % 3, :], mx[:, i % 3, :], -1.0, None, ALU.mult).then_inc(max_ready, 1)

            def head_probs(i):
                dve.wait_ge(exp_ready, i + 1)
                l = logit[:, i % 3, :]
                link(V.reciprocal(rden[:, i % 3, :], den[:, i % 3, :]))
                V.tensor_scalar(l[:, 0:P], l[:, 0:P], rden[:, i % 3, 0:1], None, ALU.mult)
                V.tensor_scalar(l[:, P:384], l[:, P:384], rden[:, i % 3, 1:2], None, ALU.mult).then_inc(prob_ready, 1)

            for i in range(4):
                wait_filled(dve, "mqT", i)
                wait_filled(dve, "mkT", i)
            for i in range(2 * HEADS + 2):
                if i < 2 * HEADS:
                    head_max(i)
                if 1 <= i <= 2 * HEADS:
                    head_probs(i - 1)
                if i - 1 in MEMKV_AT:
                    n = MEMKV_AT.index(i - 1)
                    b = wait_filled(dve, "memkv", n)
                    V.tensor_copy(mkv[:, n * 256:(n + 1) * 256], b[:, 0:256]).then_inc(drain_sem("memkv", n), 1)
            b = wait_filled(dve, "oss")
            link(V.tensor_scalar(o_ssq, b[:, 0:4], 1.0 / 512, EPS, ALU.mult, ALU.add))
            V.scalar_tensor_tensor(out=o_ssq[:, 2:4], in0=b[:, 4:6], scalar=1.0 / 512, in1=o_ssq[:, 2:4], op0=ALU.mult,
                                   op1=ALU.add).then_inc(drain_sem("oss"), 1)
            wait_drained(dve, "oss")
            dve.sem_inc(meansq["o"], 1)
            dve.wait_ge(rooted["o"], 1)
            link(V.reciprocal(o_rstd, o_ssq))
            for i in range(8):
                t, grp, n = i // 4, i // 2 % 2, i % 2
                b = wait_filled(dve, "wo", i)
                if grp == 1:
                    wait_drained(dve, "wo", i - 2)
                hs = h_v[:, t, n * 512:(n + 1) * 512]
                V.scalar_tensor_tensor(out=hs, in0=b[:, :], scalar=o_rstd[:, 2 * grp + t:2 * grp + t + 1], in1=hs,
                                       op0=ALU.mult, op1=ALU.add).then_inc(drain_sem("wo", i), 1)
                if i in (5, 7):
                    for k in range(2):
                        scaled_tile_T("h1T", G_AT["g_mem_q"], i - 5 + k)
            dve.wait_ge(sumsq["h1"], TT)
            inverse_rms("h1")
            V.tensor_scalar(q_scale, rstd, MD ** -0.5, None, ALU.mult).then_inc(inv_root["h1"], 1)
            link(V.tensor_scalar(q_neg, rstd, -(MD ** -0.5), None, ALU.mult))
            b = wait_filled(dve, "mq", 0)
            V.tensor_copy(mq[:, 0, :], b[:, 0:S]).then_inc(drain_sem("mq", 0), 1)
            for i in range(MEM_HEADS + 1):
                if i < MEM_HEADS:
                    b = wait_filled(dve, "cS", i)
                    link(V.tensor_reduce(mx[:, i % 3, :], b[:, :].rearrange("p (t s) -> p t s", t=TT), AX, ALU.max))
                    V.tensor_tensor(nmx[:, i % 3, :], mx[:, i % 3, :], q_neg, ALU.mult).then_inc(cmax_ready, 1)
                if i == 0:
                    b = wait_filled(dve, "mq", 2)
                    V.tensor_copy(mq[:, 2, :], b[:, 0:S]).then_inc(drain_sem("mq", 2), 1)
                if i >= 1:
                    j = i - 1
                    dve.wait_ge(cexp_ready, j + 1)
                    wait_drained(dve, "cS", j)
                    l = logit[:, j % 3, :]
                    link(V.reciprocal(rden[:, j % 3, :], den[:, j % 3, :]))
                    V.tensor_scalar(l[:, 0:S], l[:, 0:S], rden[:, j % 3, 0:1], None, ALU.mult)
                    V.tensor_scalar(l[:, S:2 * S], l[:, S:2 * S], rden[:, j % 3, 1:2], None, ALU.mult).then_inc(cprob_ready, 1)

            def choose(e, p):
                return V.tensor_copy(chosen[:, p], cst[:, bass.ds(4 * e, 4)].unsqueeze(2).to_broadcast([P, 4, SEATS]))

            for i in range(4):
                if i == 3:
                    for k in range(2):
                        scaled_tile_T("h2T", G_AT["g_ffn"], k)
                t, n = i // 2, i % 2
                b = wait_filled(dve, "mo", i)
                hs = h_v[:, t, n * 512:(n + 1) * 512]
                V.tensor_tensor(hs, b[:, :], hs, ALU.add).then_inc(drain_sem("mo", i), 1)
            dve.wait_ge(sumsq["h2"], TT)
            V.tensor_scalar(rms, ssq, 1.0 / D, EPS, ALU.mult, ALU.add).then_inc(meansq["h2"], 1)
            for k in range(2):
                scaled_tile_T("h2T", G_AT["g_ffn"], 2 + k)
            dve.wait_ge(rooted["h2"], 1)
            link(V.reciprocal(rstd, rms))
            dve.sem_inc(inv_root["h2"], 1)
            V.tensor_scalar(xn_v[:, 0, :], h_v[:, 0, :], rstd[:, 0:1], None, ALU.mult).then_inc(normed["h2"], 1)
            choose(0, 0).then_inc(first_chosen, 1)
            b = wait_filled(dve, "router")
            dve.wait_ge(loaded["b_r"], 16)
            for t in range(TT):
                last = V.scalar_tensor_tensor(out=lg[:, t, :], in0=b[:, t * E:(t + 1) * E], scalar=rstd[:, t:t + 1],
                                              in1=brt[:, :], op0=ALU.mult, op1=ALU.add)
            last.then_inc(drain_sem("router"), 1)
            wait_drained(dve, "router")
            for t in range(TT):
                last = V.max(topv[:, t, :], lg[:, t, :])
            link(last)
            fourth = topv[:, :, TOPK - 1:TOPK].to_broadcast([P, TT, E])
            V.tensor_tensor(gt, lg, fourth, ALU.is_gt)
            link(V.tensor_tensor(eq, lg, fourth, ALU.is_equal))
            V.reduce_sum(r_tmp[:, 0:2], gt, AX)
            for t in range(TT):
                last = V.tensor_tensor_scan(cs[:, t, :], one.to_broadcast([P, E]), eq[:, t, :], 0.0, ALU.mult, ALU.add)
            link(last)
            V.tensor_scalar(r_tmp[:, 2:4], r_tmp[:, 0:2], -1.0, float(TOPK), ALU.mult, ALU.add)
            for t in range(TT):
                last = V.tensor_scalar(ex[:, t, :], lg[:, t, :], topv[:, t, 0:1], None, ALU.subtract)
                last.then_inc(r_shift, 1)
            dve.wait_ge(r_shift, TT)
            for t in range(TT):
                last = V.scalar_tensor_tensor(out=keep[:, t, :], in0=cs[:, t, :], scalar=r_tmp[:, 2 + t:3 + t],
                                              in1=eq[:, t, :], op0=ALU.is_le, op1=ALU.mult)
            link(last)
            V.tensor_tensor(sel, keep, gt, ALU.add).then_inc(sel_ready, 1)
            dve.wait_ge(sel_ready, 1)
            dve.wait_ge(r_exp, 1)
            link(V.tensor_tensor(ex, ex, sel, ALU.mult))
            link(V.reduce_sum(r_tmp[:, 0:2], ex, AX))
            link(V.reciprocal(r_tmp[:, 0:2], r_tmp[:, 0:2]))
            for t in range(TT):
                last = V.tensor_scalar(gates[:, t, :], ex[:, t, :], r_tmp[:, t:t + 1], None, ALU.mult)
            last.then_inc(gates_ready, 1)
            b = wait_filled(dve, "rank")
            link(V.tensor_tensor(pos, b[:, 0:TT * E].rearrange("p (t e) -> p t e", t=TT), sel, ALU.mult))
            dve.wait_ge(gates_ready, 1)

            def seat_pair(e):
                for t in range(TT):
                    for k in range(2):
                        last = V.tensor_scalar(oh[:, t, k * SEATS:(k + 1) * SEATS], cst[:, C_SEAT:C_SEAT + SEATS],
                                               pos[:, t, bass.ds(e + k, 1)], None, ALU.is_equal)
                last.then_inc(seats_ready, 1)

            def select(e, p):
                for t in range(TT):
                    V.tensor_scalar(ohg[:, p, t, :], cst[:, C_SEAT:C_SEAT + P], pos[:, t, bass.ds(e, 1)],
                                    gates[:, t, bass.ds(e, 1)], ALU.is_equal, ALU.mult)
                choose(e, p).then_inc(onehot_ready, 1)

            def advance(e):
                return V.tensor_scalar(pos[:, :, bass.ds(e, 1)], pos[:, :, bass.ds(e, 1)], -float(SEATS), None, ALU.add)

            def take_rows(k):
                g0 = G_AT["g_ffn"] + 4 * k
                V.tensor_tensor(xg[:, 4 * k:4 * k + 4, :], bank[GATHER_BANK[k]][:, :].rearrange("p (c s) -> p c s", c=4),
                                gT[:, g0:g0 + 4].unsqueeze(2).to_broadcast([P, 4, P]), ALU.mult).then_inc(xg_ready, 1)

            seat_pair(0)
            select(0, 0)
            V.reduce_max(cntmax, b[0:1, 2 * E:3 * E], AX).then_inc(drain_sem("rank"), 1)
            wait_drained(dve, "rank")
            link(V.tensor_scalar(over, cst[0:1, C_LIM:C_LIM + 3], cntmax, None, ALU.is_lt))
            link(V.reduce_sum(novr, over, AX))
            V.tensor_scalar(nit[0:1, 0:1], novr, float(E // 2), float(E // 2 - 1), ALU.mult, ALU.add).then_inc(rounds_ready, 1)
            dve.wait_ge(onehot_ready, 1)
            link(advance(0))
            for k in range(2):
                dve.wait_ge(gathered, k + 1)
                take_rows(k)
            dve.wait_ge(rounds_ready, 1)
            more_pairs = dve.value_load(nit[0:1, 0:1], min_val=E // 2 - 1, max_val=S // SEATS * E // 2 - 1)
            LINKS = 3

            def expert(pair, p, more=True):
                g = 2 * pair + p
                e_next = (g + 1) & (E - 1)
                at = [LINKS * p]

                def chain(ins):
                    at[0] += 1
                    ins.then_inc(moe_chain, 1)
                    dve.wait_ge(moe_chain, pair * (2 * LINKS) + at[0])

                dve.wait_ge(gate_full, g + 1)
                V.tensor_scalar(zg, bank[A_BANK][:, :], LIMIT, None, ALU.min).then_inc(gate_ready, 1)
                if p == 0 and more:
                    seat_pair((g + 2) & (E - 2))
                if p == 0 or more:
                    select(e_next, 1 - p)
                    dve.wait_ge(onehot_ready, g + 2)
                    chain(advance(e_next))
                dve.wait_ge(up_full, g + 1)
                chain(V.tensor_scalar(zu, bank[B_BANK][:, :], LIMIT, -LIMIT, ALU.min, ALU.max))
                chain(V.scalar_tensor_tensor(out=prod, in0=zu, scalar=1.0, in1=zg, op0=ALU.add, op1=ALU.mult))
                dve.wait_ge(sig_ready, g + 1)
                V.tensor_tensor(act_rows, prod, sig, ALU.mult).then_inc(act_ready, 1)
                if p == 1 and more:
                    for k in range(2):
                        dve.wait_ge(gathered, 2 * pair + 3 + k)
                        take_rows(k)

            with dve.Fori(0, more_pairs) as pair:
                for p in range(2):
                    expert(pair, p)
            for p in range(2):
                expert(more_pairs, p, more=False)
            for t in range(TT):
                dve.wait_ge(y_done, t + 1)
                for n in range(2):
                    hs = h_v[:, t, n * 512:(n + 1) * 512]
                    last = V.tensor_tensor(hs, bank[Y_BANK[2 * t + n]][:, :], hs, ALU.add)
                last.then_inc(residual3, 1)
            dve.wait_ge(loaded["g_final"], 16)
            for t in range(TT):
                dve.wait_ge(sumsq["h3"], t + 1)
                one_t = slice(t, t + 1)
                V.tensor_scalar(rms[:, one_t], ssq[:, one_t], 1.0 / D, EPS, ALU.mult, ALU.add).then_inc(meansq["h3"], 1)
                dve.wait_ge(rooted["h3"], t + 1)
                link(V.reciprocal(rstd[:, one_t], rms[:, one_t]))
                V.scalar_tensor_tensor(out=xn_v[:, t, :], in0=h_v[:, t, :], scalar=rstd[:, one_t], in1=gfin,
                                       op0=ALU.mult, op1=ALU.mult).then_inc(out_ready, 1)

        @block.gpsimd
        def _(pool):
            nc.gpsimd.memset(warm, 1.0).then_inc(warm_ready, 1)
            wait_filled(pool, "cPV", MEM_HEADS - 1)
            nc.gpsimd.memset(back[:, 1, :], 0.0)
            nc.gpsimd.memset(res[:, 1, :], 0.0).then_inc(res_ready, 1)

        @block.scalar
        def _(act):
            A_ = nc.scalar.activation
            steps = [0]

            def link(ins):
                steps[0] += 1
                ins.then_inc(act_chain, 1)
                act.wait_ge(act_chain, steps[0])

            def square(name, src, dst, t):
                A_(dst[:, t, :], src[:, t, :], ACT.Square, accum_out=ssq[:, t:t + 1]).then_inc(sumsq[name], 1)

            def root(name, ap):
                act.wait_ge(meansq[name], 1)
                A_(ap, ap, ACT.Sqrt).then_inc(rooted[name], 1)

            def second_tile(name, src, dst):
                act.wait_ge(inv_root[name], 1)
                A_(dst[:, 1, :], src[:, 1, :], ACT.Copy, scale=rstd[:, 1:2]).then_inc(normed[name], 1)

            def scaled_T(name, gain, i):
                b = wait_filled(act, name, i)
                for j in range(2):
                    c = 2 * i + j
                    last = A_(aT_v[:, c, :], b[:, j * S:(j + 1) * S], ACT.Copy, scale=gT[:, gain + c:gain + c + 1])
                last.then_inc(drain_sem(name, i), 1)

            act.wait_ge(warm_ready, 1)
            A_(warm, warm, ACT.Sqrt)
            for t in range(TT):
                act.wait_ge(loaded[f"x{t}"], 16)
                square("x", h_v, xn_v, t)
            act.wait_ge(sumsq["x"], TT)
            root("x", rms)
            second_tile("x", h_v, xn_v)
            wait_drained(act, "gT")
            for i in (1, 3):
                scaled_T("xT", G_AT["g_mix"], i)
            for t in range(TT):
                b = wait_filled(act, "rest", 2 * t + 1)
                A_(lat[:, t, 340:680], b[:, 0:340], ACT.Copy).then_inc(drain_sem("rest", 2 * t + 1), 1)
            for i in range(4):
                wait_drained(act, "rest", i)
            for t in range(TT):
                for k, (at, n) in enumerate(((8, QL), (8 + QL, KL))):
                    A_(scratch[:, 1024 * k + 512 * t:1024 * k + 512 * t + n], lat[:, t, at:at + n], ACT.Square,
                       accum_out=lat_ssq[:, k, t:t + 1]).then_inc(sumsq["lat"], 1)
            act.wait_ge(f_in, 1)
            link(A_(fz[:, 2], fz[:, 1], ACT.Exp))
            A_(fz[:, 2], fz[:, 2], ACT.Ln, bias=1.0).then_inc(f_exp, 1)
            root("lat", lat_rms)
            act.wait_ge(loaded["mem"], 16)
            act.wait_ge(normed["x"], TT)
            act.wait_ge(sumsq["lat"], 2 * TT)
            for t in range(TT):
                square("mem", mem_v, v3(work, TT, 0, TT * D), t)
            act.wait_ge(sumsq["mem"], TT)
            root("mem", rms)
            second_tile("mem", mem_v, mem_v)
            b = wait_filled(act, "latT", 1)
            for j in range(2):
                c = 2 + j
                g = G_AT["g_q_lat"] + c
                last = A_(latT[:, c, :], b[:, j * S:(j + 1) * S], ACT.Copy, scale=gT[:, g:g + 1])
            last.then_inc(drain_sem("latT", 1), 1)
            for i in (2, 3):
                b = wait_filled(act, "qk", i)
                A_(qkf[:, i * 512:(i + 1) * 512], b[:, :], ACT.Copy).then_inc(drain_sem("qk", i), 1)
            for i in (1, 3):
                scaled_T("memT", G_AT["g_mem_kv"], i)
            for i in range(4):
                t, n = i // 2, i % 2
                b = wait_filled(act, "uq", i)
                A_(qt[:, t, n * 384:(n + 1) * 384], b[:, 0:384], ACT.Copy).then_inc(drain_sem("uq", i), 1)
            for i in range(4):
                b = wait_filled(act, "mqT", i)
                A_(qmT[:, 2 * i:2 * i + 2, :], b[0:DQ, :].rearrange("p (h s) -> p h s", h=2), ACT.Copy).then_inc(drain_sem("mqT", i), 1)
            for i in (2, 3):
                b = wait_filled(act, "mkT", i)
                A_(kmT[:, 2 * i:2 * i + 2, :], b[0:DQ, :].rearrange("p (h s) -> p h s", h=2), ACT.Copy).then_inc(drain_sem("mkT", i), 1)

            for i in range(2 * HEADS + 3):
                if i < 2 * HEADS:
                    act.wait_ge(max_ready, i + 1)
                    l = logit[:, i % 3, :]
                    for k, (a, n) in enumerate(((0, P), (P, S))):
                        last = A_(l[:, a:a + n], l[:, a:a + n], ACT.Exp, bias=nmx[:, i % 3, k:k + 1],
                                  accum_out=den[:, i % 3, k:k + 1])
                    last.then_inc(exp_ready, 1)
                if 2 <= i < 2 * HEADS + 2:
                    j = i - 2
                    b = wait_filled(act, "T", j)
                    if j >= 2:
                        wait_filled(act, "PV", j - 2)
                    A_(probT[:, j % 2, 0:384], b[:, 0:384], ACT.Copy).then_inc(drain_sem("T", j), 1)
                if i >= 3:
                    j = i - 3
                    b = wait_filled(act, "PV", j)
                    if j == 0:
                        wait_filled(act, "memT", 3)
                        act.wait_ge(normed["x"], TT)
                    r = slice(64 * (j % 2), 64 * (j % 2) + 64)
                    g = G_AT["g_fox_out"] + j // 2
                    A_(oT_v[r, j // 2, :], b[r, 0:S], ACT.Copy, scale=gT[r, g:g + 1])
                    A_(sq_v[r, j // 2, :], b[r, 0:S], ACT.Square).then_inc(drain_sem("PV", j), 1)
            root("o", o_ssq)
            wait_filled(act, "oss")
            for t in range(TT):
                for i in (4 * t + 2, 4 * t + 3):
                    wait_drained(act, "wo", i)
                square("h1", h_v, xn_v, t)
            root("h1", rms)
            b = wait_filled(act, "mq", 1)
            A_(mq[:, 1, :], b[:, 0:S], ACT.Copy).then_inc(drain_sem("mq", 1), 1)
            act.wait_ge(inv_root["h1"], 1)
            for i in range(MEM_HEADS + 3):
                if i < MEM_HEADS:
                    act.wait_ge(cmax_ready, i + 1)
                    if i >= 3:
                        wait_filled(act, "cT", i - 3)
                    b = wait_filled(act, "cS", i)
                    for t in range(TT):
                        last = A_(logit[:, i % 3, t * S:(t + 1) * S], b[:, t * S:(t + 1) * S], ACT.Exp,
                                  bias=nmx[:, i % 3, t:t + 1], scale=q_scale[:, t:t + 1], accum_out=den[:, i % 3, t:t + 1])
                    last.then_inc(drain_sem("cS", i), 1)
                    wait_drained(act, "cS", i)
                    act.sem_inc(cexp_ready, 1)
                if i == 1:
                    b = wait_filled(act, "mq", 3)
                    A_(mq[:, 3, :], b[:, 0:S], ACT.Copy).then_inc(drain_sem("mq", 3), 1)
                if 2 <= i < MEM_HEADS + 2:
                    j = i - 2
                    b = wait_filled(act, "cT", j)
                    if j >= 2:
                        wait_filled(act, "cPV", j - 2)
                    A_(probT[:, j % 2, :], b[:, :], ACT.Copy).then_inc(drain_sem("cT", j), 1)
                if i >= 3:
                    j = i - 3
                    b = wait_filled(act, "cPV", j)
                    A_(moT[:, j, :], b[:, 0:S], ACT.Copy).then_inc(drain_sem("cPV", j), 1)
            for t in range(TT):
                for i in (2 * t, 2 * t + 1):
                    wait_drained(act, "mo", i)
                square("h2", h_v, xn_v, t)
            root("h2", rms)
            second_tile("h2", h_v, xn_v)
            act.wait_ge(r_shift, TT)
            A_(ex, ex, ACT.Exp).then_inc(r_exp, 1)
            act.wait_ge(gatesT_full, 1)
            A_(gatesT, bank[B_BANK][0:E, 0:S], ACT.Copy).then_inc(gatesT_ready, 1)
            act.wait_ge(rounds_ready, 1)
            n_pairs = act.value_load(nit[0:1, 0:1], min_val=E // 2 - 1, max_val=S // SEATS * E // 2 - 1) + 1
            with act.Fori(0, n_pairs) as pair:
                for p in range(2):
                    g = 2 * pair + p
                    act.wait_ge(gate_ready, g + 1)
                    A_(sig, zg, ACT.Sigmoid, scale=ALPHA).then_inc(sig_ready, 1)
                    act.wait_ge(back_full, g + 1)
                    A_(back[:, p, :], bank[D_BANK][:, 0:S], ACT.Copy).then_inc(back_ready, 1)
                    act.wait_ge(actT_full, g + 1)
                    A_(actT.rearrange("p j h s -> p (j h s)"), bank[A_BANK][:, :], ACT.Copy).then_inc(actT_ready, 1)
                    act.wait_ge(down_full, g + 1)
                    A_(res[:, p, :], bank[D_BANK][:, :], ACT.Copy).then_inc(res_ready, 1)
            A_(warm, warm, ACT.Sqrt)
            for t in range(TT):
                act.wait_ge(residual3, t + 1)
                square("h3", h_v, xn_v, t)
                act.wait_ge(meansq["h3"], t + 1)
                A_(rms[:, t:t + 1], rms[:, t:t + 1], ACT.Sqrt).then_inc(rooted["h3"], 1)


def kernel(**inputs):
    import concourse.bacc as bacc
    from concourse.bass_utils import run_bass_kernel_spmd

    nc = bacc.Bacc("TRN2", target_bir_lowering=False, num_devices=1)
    arrays, access = {}, {}
    for name, a in dict(inputs, constants=constants()).items():
        a = np.ascontiguousarray(a)
        arrays[f"in_{name}"] = a
        access[name] = nc.dram_tensor(f"in_{name}", a.shape, mybir.dt.from_np(a.dtype), kind="ExternalInput").ap()
    out = nc.dram_tensor("out", (1, S, D), F32, kind="ExternalOutput").ap()
    layer_kernel(nc, access, out)
    r = run_bass_kernel_spmd(nc, [arrays], core_ids=[0])
    return r.results[0]["out"]
```
